# Optimizing a Trainium2 kernel written in Bass

```python
import math
import jax
import jax.numpy as jnp
from jax import lax
import numpy as np

D_MODEL = 1024
BATCH = 1
SEQ = 128
DEPTH = 2
DEC_BATCH = 1
DEC_SEQ = 256
PAST_LEN = 128

F32 = jnp.float32
GRID_W = 64
BLOCK = 128
ROPE_BASE = 10000.0
NEG = -1e30
LN_EPS = 1e-5
RMS_EPS = 1e-6

HY_W = 256
HY_BANDS = 16
HY_EMB = 1 + 2 * HY_BANDS
HY_FFN = 64
HY_SIN_FREQ = 1.0
HY_FAST_DECAY = 0.3
HY_SLOW_DECAY = 1.5
HY_TARGET = 1e-2

WIN_HEADS = 4
WIN_KV_HEADS = 2
WIN_HD = 64
WINDOW = 128

RET_HEADS = 4
RET_DK = 64
RET_DV = 128

MLA_HEADS = 4
MLA_Q_LORA = 256
MLA_KV_LORA = 128
MLA_NOPE = 64
MLA_ROPE = 32
MLA_V = 64

N_EXPERTS = 16
N_GROUPS = 4
TOP_K = 2
D_EXPERT = 256
ROUTE_SCALE = 2.5

N_BRANCH = 4
ALPHA = (2.0 * DEPTH) ** 0.25
BETA = (8.0 * DEPTH) ** -0.25

COL_SIZES = (3 * HY_W,
             WIN_HEADS * WIN_HD, WIN_KV_HEADS * WIN_HD, WIN_KV_HEADS * WIN_HD,
             RET_HEADS * RET_DK, RET_HEADS * RET_DK, RET_HEADS * RET_DV, RET_HEADS * RET_DV,
             MLA_Q_LORA, MLA_KV_LORA, MLA_ROPE,
             N_BRANCH * D_MODEL)
IN_COLS = 3 * HY_W + WIN_HEADS * WIN_HD + 2 * WIN_KV_HEADS * WIN_HD + 2 * RET_HEADS * RET_DK + 2 * RET_HEADS * RET_DV + MLA_Q_LORA + MLA_KV_LORA + MLA_ROPE + N_BRANCH * D_MODEL

kernel_name = 'hybrid_diffusion_prefix_trunk_step'

def layer_norm(x, g=None, b=None):
    xf = x.astype(F32)
    mu = xf.mean(-1, keepdims=True)
    var = jnp.square(xf - mu).mean(-1, keepdims=True)
    y = (xf - mu) * lax.rsqrt(var + LN_EPS)
    if g is not None:
        y = y * g.astype(F32) + b.astype(F32)
    return y.astype(x.dtype)

def rms_norm(x, g):
    xf = x.astype(F32)
    y = xf * lax.rsqrt(jnp.mean(xf * xf, -1, keepdims=True) + RMS_EPS)
    return y.astype(x.dtype) * g

def split_columns(z):
    offs = np.cumsum(COL_SIZES)[:-1].tolist()
    return jnp.split(z, offs, axis=-1)

def axial_rope(L, rot_dim):
    rows = L // GRID_W
    n_freq = rot_dim // 4
    inv = ROPE_BASE ** (-jnp.arange(n_freq, dtype=F32) / n_freq)
    row = jnp.broadcast_to(jnp.arange(rows, dtype=F32)[:, None], (rows, GRID_W)).reshape(L)
    col = jnp.broadcast_to(jnp.arange(GRID_W, dtype=F32)[None, :], (rows, GRID_W)).reshape(L)
    ang = jnp.concatenate([row[:, None] * inv, col[:, None] * inv], -1)
    return jnp.cos(ang), jnp.sin(ang)

def apply_rope(x, cos, sin):
    half = x.shape[-1] // 2
    x1, x2 = x[..., :half], x[..., half:]
    c = cos[None, :, None, :].astype(x.dtype)
    s = sin[None, :, None, :].astype(x.dtype)
    return jnp.concatenate([x1 * c - x2 * s, x1 * s + x2 * c], -1)

def short_conv3(u, w, b):
    L = u.shape[1]
    up = jnp.pad(u, ((0, 0), (1, 1), (0, 0)))
    return up[:, :L] * w[0] + up[:, 1:L + 1] * w[1] + up[:, 2:] * w[2] + b

def hyena_filters(L, w1, b1, w2, b2, w3):
    t01 = jnp.linspace(0.0, 1.0, L, dtype=F32)[:, None]
    bands = jnp.linspace(1e-4, HY_BANDS - 1, HY_BANDS, dtype=F32)
    ang = (2.0 * math.pi / L) * jnp.arange(L, dtype=F32)[:, None] * bands[None, :]
    z = jnp.concatenate([t01, jnp.cos(ang), -jnp.sin(ang)], -1)
    a = jnp.sin(HY_SIN_FREQ * (z @ w1.astype(F32) + b1.astype(F32)))
    a = jnp.sin(HY_SIN_FREQ * (a @ w2.astype(F32) + b2.astype(F32)))
    h = (a @ w3.astype(F32)).reshape(L, 2, 2, HY_W)
    deltas = jnp.abs(jnp.linspace(math.log(HY_TARGET) / HY_SLOW_DECAY, math.log(HY_TARGET) / HY_FAST_DECAY, HY_W, dtype=F32))
    h = h * jnp.exp(-t01 * deltas[None, :])[:, None, None, :]
    fwd, bwd = h[:, :, 0], h[:, :, 1]
    k = jnp.concatenate([fwd, jnp.zeros_like(fwd[:1]), bwd[:0:-1]], 0)
    return jnp.fft.rfft(k, axis=0)

def fft_long_conv(u, kf, bias):
    L = u.shape[1]
    uf = jnp.fft.rfft(u.astype(F32), n=2 * L, axis=1)
    y = jnp.fft.irfft(uf * kf[None], n=2 * L, axis=1)[:, :L]
    return (y + u.astype(F32) * bias.astype(F32)).astype(u.dtype)

def hyena_mixer(z, p):
    L = z.shape[1]
    z = short_conv3(z, p['hy_conv_w'], p['hy_conv_b'])
    v, x1, x2 = jnp.split(z, 3, axis=-1)
    kf = hyena_filters(L, p['hy_w1'], p['hy_b1'], p['hy_w2'], p['hy_b2'], p['hy_w3'])
    u = x1 * fft_long_conv(v, kf[:, 0], p['hy_bias'][0])
    return x2 * fft_long_conv(u, kf[:, 1], p['hy_bias'][1])

def dense_attention(q, k, v, sink=None):
    B, Lq, KVH, G, dq = q.shape
    nb = Lq // BLOCK
    scale = dq ** -0.5
    qb = jnp.moveaxis(q.reshape(B, nb, BLOCK, KVH, G, dq), 1, 0)

    def one_block(qi):
        s = jnp.einsum('bqkgd,bskd->bkgqs', qi, k, preferred_element_type=F32) * scale
        if sink is not None:
            sk = jnp.broadcast_to(sink.reshape(KVH, G)[None, :, :, None, None].astype(F32), s.shape[:-1] + (1,))
            pr = jax.nn.softmax(jnp.concatenate([s, sk], -1), -1)[..., :-1]
        else:
            pr = jax.nn.softmax(s, -1)
        return jnp.einsum('bkgqs,bskd->bqkgd', pr.astype(v.dtype), v)

    o = lax.map(one_block, qb)
    return jnp.moveaxis(o, 0, 1).reshape(B, Lq, KVH * G * v.shape[-1])

def window_attention(q, k, v, ck, cv, sink):
    B, L, H, d = q.shape
    KVH = k.shape[2]
    G = H // KVH
    nb = L // BLOCK
    P = ck.shape[1]
    W = 3 * BLOCK
    qb = q.reshape(B, nb, BLOCK, KVH, G, d)
    kpos = jnp.arange(nb)[:, None] * BLOCK + jnp.arange(-BLOCK, 2 * BLOCK)[None, :]
    pad = ((0, 0), (BLOCK, BLOCK), (0, 0), (0, 0))
    kb = jnp.pad(k, pad)[:, kpos + BLOCK]
    vb = jnp.pad(v, pad)[:, kpos + BLOCK]
    qpos = jnp.arange(L).reshape(nb, BLOCK)
    valid = (jnp.abs(qpos[:, :, None] - kpos[:, None, :]) <= WINDOW) & (kpos[:, None, :] >= 0) & (kpos[:, None, :] < L)
    scale = d ** -0.5
    s_loc = jnp.einsum('bnqkgd,bnskd->bnkgqs', qb, kb, preferred_element_type=F32) * scale
    s_loc = jnp.where(valid[None, :, None, None], s_loc, NEG)
    s_ctx = jnp.einsum('bnqkgd,bpkd->bnkgqp', qb, ck, preferred_element_type=F32) * scale
    sk = jnp.broadcast_to(sink.reshape(KVH, G)[None, None, :, :, None, None].astype(F32), s_loc.shape[:-1] + (1,))
    pr = jax.nn.softmax(jnp.concatenate([s_loc, s_ctx, sk], -1), -1).astype(v.dtype)
    o = (jnp.einsum('bnkgqs,bnskd->bnqkgd', pr[..., :W], vb)
         + jnp.einsum('bnkgqp,bpkd->bnqkgd', pr[..., W:W + P], cv))
    return o.reshape(B, L, H * d)

def retention_chunked(q, k, v, gamma, s0):
    B, L, H, _ = q.shape
    dv = v.shape[-1]
    nc = L // BLOCK
    log_g = jnp.log(gamma.astype(F32))
    pos = jnp.arange(BLOCK, dtype=F32)
    diff = pos[:, None] - pos[None, :]
    decay_in = jnp.where(diff >= 0, jnp.exp(jnp.maximum(diff, 0.0)[None] * log_g[:, None, None]), 0.0)
    decay_q = jnp.exp((pos + 1.0)[:, None] * log_g[None, :])
    decay_k = jnp.exp((BLOCK - 1.0 - pos)[:, None] * log_g[None, :])
    decay_c = jnp.exp(BLOCK * log_g)

    def chunks(a):
        return jnp.moveaxis(a.astype(F32).reshape(B, nc, BLOCK, H, a.shape[-1]), 1, 0)

    def step(S, inp):
        qi, ki, vi = inp
        att = jnp.einsum('bihd,bjhd->bhij', qi, ki) * decay_in[None]
        o = (jnp.einsum('bhij,bjhe->bihe', att, vi)
             + jnp.einsum('bihd,bhde->bihe', qi, S) * decay_q[None, :, :, None])
        S = S * decay_c[None, :, None, None] + jnp.einsum('bjhd,bjhe->bhde', ki * decay_k[None, :, :, None], vi)
        return S, o

    S, o = lax.scan(step, s0.astype(F32), (chunks(q), chunks(k), chunks(v)))
    return jnp.moveaxis(o, 0, 1).reshape(B, L, H, dv), S

def retention_mixer(q, k, v, g, dec_f, dec_b, s0f, s0b):
    B, L, _ = q.shape
    qh = q.reshape(B, L, RET_HEADS, RET_DK)
    kh = k.reshape(B, L, RET_HEADS, RET_DK) * (RET_DK ** -0.5)
    vh = v.reshape(B, L, RET_HEADS, RET_DV)
    of, sf = retention_chunked(qh, kh, vh, jax.nn.sigmoid(dec_f.astype(F32)), s0f)
    ob, sb = retention_chunked(qh[:, ::-1], kh[:, ::-1], vh[:, ::-1], jax.nn.sigmoid(dec_b.astype(F32)), s0b)
    o = layer_norm(of + ob[:, ::-1]).reshape(B, L, RET_HEADS * RET_DV)
    return jax.nn.silu(g) * o.astype(g.dtype), sf, sb

def mla_queries(cq, p):
    B, L, _ = cq.shape
    cq = rms_norm(cq, p['mla_q_norm'])
    return (cq @ p['mla_w_uq']).reshape(B, L, MLA_HEADS, MLA_NOPE + MLA_ROPE)

def mla_keys_values(ckv_n, kr, p):
    B, L, _ = ckv_n.shape
    kv = (ckv_n @ p['mla_w_ukv']).reshape(B, L, MLA_HEADS, MLA_NOPE + MLA_V)
    k = jnp.concatenate([kv[..., :MLA_NOPE], jnp.broadcast_to(kr, (B, L, MLA_HEADS, MLA_ROPE)).astype(kv.dtype)], -1)
    return k, kv[..., MLA_NOPE:]

def moe(h, p):
    B, L, D = h.shape
    t = h.reshape(B * L, D)
    epg = N_EXPERTS // N_GROUPS
    scores = jax.nn.sigmoid(jnp.dot(t, p['router_w'], preferred_element_type=F32))
    biased = (scores + p['router_b'].astype(F32)).reshape(-1, N_GROUPS, epg)
    grp = jnp.argmax(lax.top_k(biased, TOP_K)[0].sum(-1), -1)
    in_grp = jnp.take_along_axis(biased, grp[:, None, None], axis=1)[:, 0]
    _, local = lax.top_k(in_grp, TOP_K)
    expert = grp[:, None] * epg + local
    w = jnp.take_along_axis(scores, expert, -1)
    w = ROUTE_SCALE * w / w.sum(-1, keepdims=True)
    combine = (jax.nn.one_hot(expert, N_EXPERTS, dtype=F32) * w[..., None]).sum(1)
    hid = jax.nn.silu(jnp.einsum('td,edf->tef', t, p['moe_w_gate'])) * jnp.einsum('td,edf->tef', t, p['moe_w_up'])
    y = jnp.einsum('tef,efd->td', hid * combine[..., None].astype(hid.dtype), p['moe_w_down'])
    return y.reshape(B, L, D)

def modulated_input(x, mod):
    s1, sc1, g1, s2, sc2, g2 = jnp.split(mod, 6, axis=-1)
    h = layer_norm(x) * (1.0 + sc1) + s1
    return h, (g1, s2, sc2, g2)

def merge_and_channel_mix(x, y_a, y_b, y_c, y_d, gate_cols, mods, p):
    g1, s2, sc2, g2 = mods
    B, L, D = x.shape
    gates = jax.nn.sigmoid(gate_cols.reshape(B, L, N_BRANCH, D))
    merged = (gates[:, :, 0] * (y_a @ p['w_br_a']) + gates[:, :, 1] * (y_b @ p['w_br_b'])
              + gates[:, :, 2] * (y_c @ p['w_br_c']) + gates[:, :, 3] * (y_d @ p['w_br_d']))
    x = layer_norm(ALPHA * x + g1 * (merged @ p['w_out']), p['ln1_g'], p['ln1_b'])
    h2 = layer_norm(x) * (1.0 + sc2) + s2
    return layer_norm(ALPHA * x + g2 * moe(h2, p), p['ln2_g'], p['ln2_b'])

def context_layer(x, mod, p):
    B, P, _ = x.shape
    h, mods = modulated_input(x, mod)
    hy, wq, wk, wv, rq, rk, rv, rg, cq, ckv, krope, gate_cols = split_columns(h @ p['w_in'])
    y_a = hyena_mixer(hy, p)
    kB = wk.reshape(B, P, WIN_KV_HEADS, WIN_HD)
    vB = wv.reshape(B, P, WIN_KV_HEADS, WIN_HD)
    y_b = dense_attention(wq.reshape(B, P, WIN_KV_HEADS, WIN_HEADS // WIN_KV_HEADS, WIN_HD), kB, vB, p['win_sink'])
    zero = jnp.zeros((B, RET_HEADS, RET_DK, RET_DV), F32)
    y_c, sf, sb = retention_mixer(rq, rk, rv, rg, p['ret_decay_fwd'], p['ret_decay_bwd'], zero, zero)
    ckv_n = rms_norm(ckv, p['mla_kv_norm'])
    k_d, v_d = mla_keys_values(ckv_n, krope[:, :, None, :], p)
    y_d = dense_attention(mla_queries(cq, p)[:, :, :, None, :], k_d, v_d)
    x = merge_and_channel_mix(x, y_a, y_b, y_c, y_d, gate_cols, mods, p)
    return x, (kB, vB, ckv_n, krope, sf, sb)

def latent_layer(x, mod, p, ck, cv, cckv, ckrope, s0f, s0b):
    B, L, _ = x.shape
    h, mods = modulated_input(x, mod)
    hy, wq, wk, wv, rq, rk, rv, rg, cq, ckv, krope, gate_cols = split_columns(h @ p['w_in'])
    y_a = hyena_mixer(hy, p)
    cos_b, sin_b = axial_rope(L, WIN_HD)
    qB = apply_rope(wq.reshape(B, L, WIN_HEADS, WIN_HD), cos_b, sin_b)
    kB = apply_rope(wk.reshape(B, L, WIN_KV_HEADS, WIN_HD), cos_b, sin_b)
    vB = wv.reshape(B, L, WIN_KV_HEADS, WIN_HD)
    y_b = window_attention(qB, kB, vB, ck, cv, p['win_sink'])
    y_c, _, _ = retention_mixer(rq, rk, rv, rg, p['ret_decay_fwd'], p['ret_decay_bwd'], s0f, s0b)
    cos_d, sin_d = axial_rope(L, MLA_ROPE)
    q = mla_queries(cq, p)
    q = jnp.concatenate([q[..., :MLA_NOPE], apply_rope(q[..., MLA_NOPE:], cos_d, sin_d)], -1)
    k_lat, v_lat = mla_keys_values(rms_norm(ckv, p['mla_kv_norm']), apply_rope(krope[:, :, None, :], cos_d, sin_d), p)
    k_ctx, v_ctx = mla_keys_values(cckv, ckrope[:, :, None, :], p)
    k_all = jnp.concatenate([k_lat, k_ctx.astype(k_lat.dtype)], 1)
    v_all = jnp.concatenate([v_lat, v_ctx.astype(v_lat.dtype)], 1)
    y_d = dense_attention(q[:, :, :, None, :], k_all, v_all)
    return merge_and_channel_mix(x, y_a, y_b, y_c, y_d, gate_cols, mods, p)

def setup_inputs(seed: int = 0) -> dict:
    key = jax.random.key(seed)
    ks = iter(jax.random.split(key, 48))
    D = D_MODEL

    def nrm(shape, scale=1.0):
        return jax.random.normal(next(ks), shape, F32) * scale

    ret_base = jnp.log(2.0 ** (5.0 + jnp.arange(RET_HEADS, dtype=F32)) - 1.0)
    return {
        'x_prompt': nrm((BATCH, SEQ, D)),
        'x_sample': nrm((DEC_BATCH, DEC_SEQ, D)),
        'cache_win_k': nrm((DEC_BATCH, DEPTH, PAST_LEN, WIN_KV_HEADS, WIN_HD)),
        'cache_win_v': nrm((DEC_BATCH, DEPTH, PAST_LEN, WIN_KV_HEADS, WIN_HD)),
        'cache_mla_ckv': nrm((DEC_BATCH, DEPTH, PAST_LEN, MLA_KV_LORA)),
        'cache_mla_krope': nrm((DEC_BATCH, DEPTH, PAST_LEN, MLA_ROPE)),
        'state_ret_fwd': nrm((DEC_BATCH, DEPTH, RET_HEADS, RET_DK, RET_DV), 0.5),
        'state_ret_bwd': nrm((DEC_BATCH, DEPTH, RET_HEADS, RET_DK, RET_DV), 0.5),
        'c': nrm((DEC_BATCH, D)),
        'c_ctx': nrm((D,)),
        'w_ada': nrm((DEPTH, D, 6 * D), 0.5 * D ** -0.5),
        'b_ada': nrm((DEPTH, 6 * D), 0.02),
        'w_in': nrm((DEPTH, D, IN_COLS), D ** -0.5),
        'hy_conv_w': nrm((DEPTH, 3, 3 * HY_W), 3 ** -0.5),
        'hy_conv_b': nrm((DEPTH, 3 * HY_W), 0.02),
        'hy_w1': nrm((DEPTH, HY_EMB, HY_FFN), HY_EMB ** -0.5),
        'hy_b1': nrm((DEPTH, HY_FFN), 0.02),
        'hy_w2': nrm((DEPTH, HY_FFN, HY_FFN), HY_FFN ** -0.5),
        'hy_b2': nrm((DEPTH, HY_FFN), 0.02),
        'hy_w3': nrm((DEPTH, HY_FFN, 4 * HY_W), 0.05 * HY_FFN ** -0.5),
        'hy_bias': nrm((DEPTH, 2, HY_W), 0.1),
        'win_sink': nrm((DEPTH, WIN_HEADS), 0.5),
        'ret_decay_fwd': ret_base + nrm((DEPTH, RET_HEADS), 0.1),
        'ret_decay_bwd': ret_base + nrm((DEPTH, RET_HEADS), 0.1),
        'mla_q_norm': 1.0 + nrm((DEPTH, MLA_Q_LORA), 0.02),
        'mla_kv_norm': 1.0 + nrm((DEPTH, MLA_KV_LORA), 0.02),
        'mla_w_uq': nrm((DEPTH, MLA_Q_LORA, MLA_HEADS * (MLA_NOPE + MLA_ROPE)), MLA_Q_LORA ** -0.5),
        'mla_w_ukv': nrm((DEPTH, MLA_KV_LORA, MLA_HEADS * (MLA_NOPE + MLA_V)), MLA_KV_LORA ** -0.5),
        'w_br_a': nrm((DEPTH, HY_W, D), BETA * HY_W ** -0.5),
        'w_br_b': nrm((DEPTH, WIN_HEADS * WIN_HD, D), BETA * (WIN_HEADS * WIN_HD) ** -0.5),
        'w_br_c': nrm((DEPTH, RET_HEADS * RET_DV, D), BETA * (RET_HEADS * RET_DV) ** -0.5),
        'w_br_d': nrm((DEPTH, MLA_HEADS * MLA_V, D), BETA * (MLA_HEADS * MLA_V) ** -0.5),
        'w_out': nrm((DEPTH, D, D), BETA * D ** -0.5),
        'ln1_g': 1.0 + nrm((DEPTH, D), 0.02),
        'ln1_b': nrm((DEPTH, D), 0.02),
        'ln2_g': 1.0 + nrm((DEPTH, D), 0.02),
        'ln2_b': nrm((DEPTH, D), 0.02),
        'router_w': nrm((D, N_EXPERTS), D ** -0.5),
        'router_b': nrm((N_EXPERTS,), 0.01),
        'moe_w_gate': nrm((DEPTH, N_EXPERTS, D, D_EXPERT), D ** -0.5),
        'moe_w_up': nrm((DEPTH, N_EXPERTS, D, D_EXPERT), D ** -0.5),
        'moe_w_down': nrm((DEPTH, N_EXPERTS, D_EXPERT, D), BETA * D_EXPERT ** -0.5),
    }

def reference(x_prompt, x_sample, cache_win_k, cache_win_v, cache_mla_ckv, cache_mla_krope,
              state_ret_fwd, state_ret_bwd, c, c_ctx, w_ada, b_ada, w_in,
              hy_conv_w, hy_conv_b, hy_w1, hy_b1, hy_w2, hy_b2, hy_w3, hy_bias,
              win_sink, ret_decay_fwd, ret_decay_bwd, mla_q_norm, mla_kv_norm, mla_w_uq, mla_w_ukv,
              w_br_a, w_br_b, w_br_c, w_br_d, w_out, ln1_g, ln1_b, ln2_g, ln2_b,
              router_w, router_b, moe_w_gate, moe_w_up, moe_w_down):
    xp = x_prompt
    xs = x_sample
    ctx_lists = ([], [], [], [], [], [])
    for l in range(DEPTH):
        p = {
            'w_in': w_in[l], 'hy_conv_w': hy_conv_w[l], 'hy_conv_b': hy_conv_b[l],
            'hy_w1': hy_w1[l], 'hy_b1': hy_b1[l], 'hy_w2': hy_w2[l], 'hy_b2': hy_b2[l],
            'hy_w3': hy_w3[l], 'hy_bias': hy_bias[l], 'win_sink': win_sink[l],
            'ret_decay_fwd': ret_decay_fwd[l], 'ret_decay_bwd': ret_decay_bwd[l],
            'mla_q_norm': mla_q_norm[l], 'mla_kv_norm': mla_kv_norm[l],
            'mla_w_uq': mla_w_uq[l], 'mla_w_ukv': mla_w_ukv[l],
            'w_br_a': w_br_a[l], 'w_br_b': w_br_b[l], 'w_br_c': w_br_c[l], 'w_br_d': w_br_d[l],
            'w_out': w_out[l], 'ln1_g': ln1_g[l], 'ln1_b': ln1_b[l], 'ln2_g': ln2_g[l], 'ln2_b': ln2_b[l],
            'router_w': router_w, 'router_b': router_b,
            'moe_w_gate': moe_w_gate[l], 'moe_w_up': moe_w_up[l], 'moe_w_down': moe_w_down[l],
        }
        mod_ctx = (jax.nn.silu(c_ctx) @ w_ada[l] + b_ada[l])[None, None, :]
        mod_lat = (jax.nn.silu(c) @ w_ada[l] + b_ada[l])[:, None, :]
        xp, ctx_tensors = context_layer(xp, mod_ctx, p)
        for lst, t in zip(ctx_lists, ctx_tensors):
            lst.append(t)
        xs = latent_layer(xs, mod_lat, p, cache_win_k[:, l], cache_win_v[:, l], cache_mla_ckv[:, l],
                          cache_mla_krope[:, l], state_ret_fwd[:, l], state_ret_bwd[:, l])
    new_win_k = jnp.stack(ctx_lists[0], axis=1)
    new_win_v = jnp.stack(ctx_lists[1], axis=1)
    new_mla_ckv = jnp.stack(ctx_lists[2], axis=1)
    new_mla_krope = jnp.stack(ctx_lists[3], axis=1)
    new_ret_fwd = jnp.stack(ctx_lists[4], axis=1)
    new_ret_bwd = jnp.stack(ctx_lists[5], axis=1)
    return (xp, xs, new_win_k, new_win_v, new_mla_ckv, new_mla_krope, new_ret_fwd, new_ret_bwd)


_drawn_inputs = setup_inputs


def setup_inputs(seed=0):
    import zlib

    import numpy as np

    out = dict(_drawn_inputs(seed))
    spreads = {}
    factors = {'cache_win_k': 5.802,
     'cache_win_v': 7.134,
     'cache_mla_ckv': 7.093,
     'cache_mla_krope': 8.0,
     'state_ret_fwd': 160.859,
     'state_ret_bwd': 33.616,
     'hy_conv_w': 4.956,
     'hy_conv_b': 8.0,
     'hy_w1': 3.527,
     'hy_b1': 8.0,
     'hy_w2': 3.463,
     'hy_b2': 8.0,
     'hy_w3': 4.62,
     'hy_bias': 4.621,
     'win_sink': 200.0,
     'mla_q_norm': 27.333,
     'mla_kv_norm': 25.732,
     'mla_w_uq': 3.308,
     'w_br_a': 4.288,
     'w_br_c': 4.541}
    for name, (base, spread) in spreads.items():
        noise = np.random.default_rng([zlib.crc32(name.encode()), seed]).standard_normal(out[name].shape)
        drawn = base * np.exp(spread * noise) if base else spread * noise
        out[name] = jnp.asarray(drawn.astype(out[name].dtype))
    for name, factor in factors.items():
        out[name] = (out[name] * factor).astype(out[name].dtype)
    return out
```

```python
import math
from contextlib import ExitStack

import numpy as np

import concourse.bass as bass
from concourse import mybir

F32 = mybir.dt.float32
F32R = mybir.dt.float32r
BF16 = mybir.dt.bfloat16
ALU = mybir.AluOpType
ACT = mybir.ActivationFunctionType
AX = mybir.AxisListType

P = 128
D = 1024
DT = D // P
DEPTH = 2
LP, LS = 128, 256
TOK = LP + LS
NT = TOK // P
GRID_W = 64
SEG = ((0, LP), (LP, TOK))
HYC = 256
BANDS, HY_FFN = 16, 64
HY_EMB = 1 + 2 * BANDS
HEADS = 4
WIN_HD = 64
NOPE, ROPE, MV = 64, 32, 64
QK = NOPE + ROPE
DV = 128
N_EXPERTS, N_GROUPS, D_EXPERT = 16, 4, 256
EPG = N_EXPERTS // N_GROUPS
ROUTE_SCALE = 2.5
ALPHA = (2.0 * DEPTH) ** 0.25
LN_EPS, RMS_EPS = 1e-5, 1e-6
NEG = -1e30
TWO_PI_A = 6.28125
TWO_PI_B = 2.0 * math.pi - TWO_PI_A
ROUND = 1.5 * 2.0 ** 23
PI_BELOW = 3.1415925
SLOTS = 6
SPLIT_SLOTS = 3
BANKS = 8
ADA_UNITS = 4
ADA_BLOCKS = 6 * D // (ADA_UNITS * P)
ADA_FIRST = 2 * D // (ADA_UNITS * P)
FT = 3
COND_ROWS = 32



def reader(unit):
    if unit.startswith("ada"):
        n = int(unit[3:])
        return f"a{n // ADA_UNITS}" if n % ADA_UNITS == ADA_UNITS - 1 else None
    if unit.startswith("out"):
        return f"out{NT - 1}1" if unit == f"out{DT - 1}" else None
    if unit.startswith("br"):
        return unit[:3] + "3"
    if unit[:2] in ("rv", "rg", "cq"):
        return {"rv": "rv01", "rg": "rg01", "cq": "cq"}[unit[:2]][:2] + (
            str(int(unit[2]) // 2) if unit[:2] != "cq" else "") + str(NT - 1)
    if unit in ("ck", "krope"):
        return f"ck{NT - 1}"
    if unit[0] == "g" and unit[1:].isdigit():
        return "gate" + unit[1:]
    return unit


def gate(d, b):
    return (f"gate{d}{b}", [f"g{d}{b}"], [f"gate{d}{b}"])


def ada(n):
    return (f"a{n}", [f"ada{ADA_UNITS * n + i}" for i in range(ADA_UNITS)], [f"a{n}"])


def mod(n):
    return (f"m{n}", [], [f"m{n}"])


def stages():
    s = [ada(0), ada(1), mod(0), ada(2), mod(1), ada(3), mod(2), mod(3),
         ("hT", [], [f"hT{d}" for d in range(DT)]),
         ("fil1", [], ["fil1"]),
         ("hy", [f"hy{i}" for i in range(6)], [f"hy{i}" for i in range(6)]),
         ("fil2", [], ["fil2"]),
         ("rk", ["rk0", "rk1"], ["rk0", "rk1"]),
         ("rq", ["rq0", "rq1"], ["rq0", "rq1"]),
         ("fil3", [], [f"fil3{t}{o}" for t in range(FT) for o in range(2)]),
         ("vT", [], [f"vT{t}" for t in range(NT)]),
         ("rv0", ["rv0", "rv1"], [f"rv0{t}" for t in range(NT)]),
         ("K", [], [f"K{x}{f}" for f in range(FT) for x in "cs"]),
         ("U0", [], [f"U0{f}" for f in range(FT)]),
         ("rv1", ["rv2", "rv3"], [f"rv1{t}" for t in range(NT)]),
         ("rg0", ["rg0", "rg1"], [f"rg0{t}" for t in range(NT)]),
         ("yv", [], ["yv0", "yv1"]),
         ("rg1", ["rg2", "rg3"], [f"rg1{t}" for t in range(NT)]),
         ("uT", [], [f"uT{t}" for t in range(NT)]),
         ("wq", ["wq0", "wq1"], ["wq0", "wq1"]),
         ("wk", ["wk"], ["wk"]),
         ("wv", ["wv"], ["wv"]),
         ("U1", [], [f"U1{f}" for f in range(FT)])]
    for h in range(HEADS):
        s += [(f"ra{h}", [], [f"ra{h}a", f"ra{h}b"])]
        s += [gate(0, h)]
        s += [(f"ro{h}", [], [f"ro{h}"])]
    s += [("yu", [], ["yu0", "yu1"]),
          ("kr", [], ["kr"]),
          ("qkrot", [], ["pq", "pk"]),
          ("kBo", [], ["kBo"]),
          ada(4),
          ("cq", ["cq0", "cq1"], [f"cq{t}" for t in range(NT)]),
          mod(4),
          ("ck", ["ck", "krope"], [f"ck{t}" for t in range(NT)]),
          ("rs", [], ["rsf", "rsb"])]
    for t in range(NT):
        s += [(f"sB{t}", [], [f"sB{t}{h}" for h in range(HEADS)])]
        if t == 1:
            s += [("dT", [], ["cqT0", "cqT1", "ckT", "krT"])]
        s += [gate(1, t), ada(5 + t)]
        s += [(f"pB{t}", [], [f"pB{t}{h}" for h in range(HEADS)]), mod(5 + t), (f"oB{t}", [], [f"oB{t}"])]
    s += [gate(1, 3),
          ("qD", [], [f"qD{h}" for h in range(HEADS)]),
          ("rK", [], ["rK"]),
          ("kD", [], [f"kD{h}" for h in range(HEADS)]),
          ("vD", [], ["vD0", "vD1"]),
          ("rD", [], ["rD0", "rD1"]),
          gate(2, 0), ada(8), gate(2, 1), mod(8)]
    for t in range(NT):
        s += [(f"sD{t}", [], [f"sD{t}{h}" for h in range(HEADS)])]
        s += [gate(2 + (t + 2) // 4, (t + 2) % 4), ada(9 + t)]
        s += [(f"pD{t}", [], [f"pD{t}{h}" for h in range(HEADS)]), mod(9 + t), (f"oD{t}", [], [f"oD{t}"])]
    s += [gate(3, 1), gate(3, 2), gate(3, 3),
          ("ycT", [], [f"ycT{k}" for k in range(4)]),
          ]
    for d in range(DT):
        if d >= 4:
            s += [gate(d, b) for b in range(4)]
        s += [(f"br{d}", [f"br{d}a", f"br{d}b"], [f"br{d}{b}" for b in range(4)])]
    s += [("g1", [], [f"g1{c}{h}" for c in range(2) for h in range(2)]),
          ("out", [f"out{k}" for k in range(DT)], [f"out{t}{h}" for t in range(NT) for h in range(2)]),
          ("g2", [], [f"g2{c}{h}" for c in range(2) for h in range(2)]),
          ("h2T", [], [f"h2T{d}" for d in range(DT)]),
          ("rt", [], ["rt"]),
          ("cbT", [], ["cbT"])]
    return s


UNITS = [u for _, us, _ in stages() for u in us]
JOBS = [j for _, _, js in stages() for j in js]
UNIT_AT = {u: i for i, u in enumerate(UNITS)}
UNITS_BEFORE = [len(UNITS[s::SLOTS]) for s in range(SLOTS)]
UNITS_LAYER = [n + N_EXPERTS for n in UNITS_BEFORE]
MOE_SLOT = [(len(UNITS) + j) % SLOTS for j in range(SLOTS)]
IN_UNITS = ([f"hy{i}" for i in range(6)] + ["rk0", "rk1", "rq0", "rq1"] + [f"rv{i}" for i in range(4)]
            + [f"rg{i}" for i in range(4)] + ["wq0", "wq1", "wk", "wv", "cq0", "cq1", "ck", "krope"]
            + [f"g{d}{b}" for d in range(DT) for b in range(4)])
SUM_JOBS = [f"sum{t}{h}" for t in range(NT) for h in range(2)]
JOB_AT = {j: i for i, j in enumerate(JOBS)}
JOBS_BEFORE = [len(JOBS[b::BANKS]) for b in range(BANKS)]
GATE_BANK, UP_BANK, SUM_BANK = 0, 1, 2
JOBS_LAYER = [n + (2 * N_EXPERTS if b < SUM_BANK else 1) for b, n in enumerate(JOBS_BEFORE)]

JOB_AT |= {j: BANKS * JOBS_BEFORE[SUM_BANK + n] + SUM_BANK + n for n, j in enumerate(SUM_JOBS)}

PARTS = [("conv_w", 18), ("conv_b", 6), ("hy_bias", 4), ("hy_b1", 1), ("hy_b2", 1), ("hy_w1", HY_FFN),
         ("hy_w2", HY_FFN), ("decay", 12), ("q_norm", 2), ("b_ada", 48), ("sink", HEADS), ("kv_norm", 128),
         ("s0f", 2 * DV), ("s0b", 2 * DV), ("ctx_k", LP), ("ctx_v", 2 * WIN_HD), ("ctx_ckv", LP), ("ctx_kr", LP),
         ("w_uq", 2 * HEADS * QK), ("w_ukv", HEADS * (NOPE + MV))]
PART_AT = {}
_at = 0
for _n, _w in PARTS:
    PART_AT[_n] = (_at, _w)
    _at += _w
N_PARAM = _at
CONSTS = [("fwd_s", 2 * 2 * LS), ("fwd_p", 2 * LP), ("inv_s", 2 * 2 * LS), ("inv_p", 2 * LP), ("zT", TOK),
          ("ident", P), ("perm_b", P), ("perm_d", ROPE), ("cos_b", LS), ("sin_b", LS), ("cos_d", LS), ("sin_d", LS),
          ("mask", 2 * P), ("i_plus_1", LS), ("l_minus_i", LS), ("p_fwd", 1), ("p_bwd", 1), ("tie", EPG * EPG),
          ("row_sel", 2)]
CONST_AT = {}
_at = 0
for _n, _w in CONSTS:
    CONST_AT[_n] = (_at, _w)
    _at += _w
N_CONST = _at


def shape_constants():
    c = {}

    def dft(L):
        w = np.pi * (np.arange(L) + 0.5) / L
        a = np.arange(L)[:, None] * w[None, :]
        return np.cos(a), np.sin(a)

    def by_tile(a):
        return a.reshape(-1, P, a.shape[1]).transpose(1, 0, 2)

    for n, L in (("s", LS), ("p", LP)):
        fc, fs = dft(L)
        c["fwd_" + n] = np.stack([by_tile(fc), by_tile(fs)], 2)
        c["inv_" + n] = np.stack([by_tile(fc.T / L), by_tile(fs.T / L)], 2)
    zs, dec = [], []
    for L in (LP, LS):
        t01 = np.linspace(0.0, 1.0, L, dtype=np.float32)[:, None]
        bands = np.linspace(1e-4, BANDS - 1, BANDS, dtype=np.float32)
        ang = (np.float32(2.0 * math.pi / L) * np.arange(L, dtype=np.float32)[:, None]) * bands[None, :]
        zs.append(np.concatenate([t01, np.cos(ang), -np.sin(ang)], -1))
        deltas = np.abs(np.linspace(math.log(1e-2) / 1.5, math.log(1e-2) / 0.3, HYC, dtype=np.float32))
        d = np.exp(-t01 * deltas[None, :])
        b = d.copy()
        b[0] = 0.0
        dec.append(np.stack([d, b], 1))
    zT = np.zeros((P, TOK))
    zT[:HY_EMB] = np.concatenate(zs, 0).T
    c["zT"] = zT
    decay = np.concatenate(dec, 0).reshape(NT, P, 2 * HYC).transpose(1, 0, 2)
    c["ident"] = np.eye(P)

    def swap(n, half):
        m = np.zeros((n, n))
        for i in range(n):
            j = i + half if (i // half) % 2 == 0 else i - half
            m[j, i] = 1.0
        return m

    def rope(rot):
        nf = rot // 4
        inv = np.float32(10000.0) ** (-np.arange(nf, dtype=np.float32) / nf)
        row = np.repeat(np.arange(LS // GRID_W, dtype=np.float32), GRID_W)
        col = np.tile(np.arange(GRID_W, dtype=np.float32), LS // GRID_W)
        ang = np.concatenate([row[:, None] * inv, col[:, None] * inv], -1)
        co, si = np.cos(ang).T, np.sin(ang).T
        return np.concatenate([co, co], 0), np.concatenate([-si, si], 0)

    c["perm_b"] = swap(P, WIN_HD // 2)
    pd = np.zeros((P, ROPE))
    pd[NOPE:QK] = swap(ROPE, ROPE // 2)
    c["perm_d"] = pd
    cb, sb = rope(WIN_HD)
    c["cos_b"], c["sin_b"] = np.tile(cb, (2, 1)), np.tile(sb, (2, 1))
    cd, sd = rope(ROPE)
    for n, a in (("cos_d", cd), ("sin_d", sd)):
        m = np.zeros((P, LS))
        m[NOPE:QK] = a
        c[n] = m
    i, j = np.arange(P)[:, None], np.arange(P)[None, :]
    c["mask"] = np.stack([np.where(j <= i, 0.0, NEG), np.where(j >= i, 0.0, NEG)], 1)
    c["i_plus_1"] = np.broadcast_to(np.arange(LS) + 1.0, (P, LS))
    c["l_minus_i"] = np.broadcast_to(LS - np.arange(LS) * 1.0, (P, LS))
    c["p_fwd"] = (P - 1.0 - np.arange(P))[:, None]
    c["p_bwd"] = np.arange(P)[:, None] * 1.0
    c["tie"] = np.broadcast_to((np.arange(EPG)[None, :] < np.arange(EPG)[:, None]).astype(float).ravel(), (P, EPG * EPG))
    c["row_sel"] = np.tile(np.concatenate([np.eye(2), np.zeros((COND_ROWS - 2, 2))]), (P // COND_ROWS, 1))
    block = np.concatenate([np.asarray(c[n], np.float32).reshape(P, w) for n, w in CONSTS], 1)
    dist = np.stack([P + i - j, np.maximum(i - j, 0), np.maximum(j - i, 0), P + j - i, i >= j, j >= i], 1)
    return (np.ascontiguousarray(block), np.ascontiguousarray(dist.astype(np.float32)),
            np.ascontiguousarray(decay.astype(np.float32)))


def build(nc, x_in, cond, units_ada, units_in, units_br, units_out, units_moe, params, hy_w3, ln_rows, router_w,
          router_b, consts, dist, hy_decay, y_prompt, y_sample, new_k, new_v, new_ckv, new_krope, new_rf, new_rb):
    comb_dram = nc.dram_tensor("combine_rows", [N_EXPERTS, TOK], F32, kind="Internal").ap()
    with ExitStack() as ctx:
        def sb(name, shape):
            return ctx.enter_context(nc.sbuf_tensor(name, shape, F32))

        def raw_sem(name):
            return ctx.enter_context(nc.semaphore(name))

        psum = ctx.enter_context(nc.psum_tensor("psum", [P, BANKS, 512], F32))
        ring = sb("ring", [P, SLOTS, DT, P])
        X = sb("X", [P, NT, D])
        hT = sb("hT", [P, DT, TOK])
        modT = sb("modT", [P, 48, 2])
        condS = sb("condS", [P, DT, COND_ROWS])
        nmean = sb("nmean", [P, NT, 2])
        prm = sb("prm", [P, N_PARAM])
        cst = sb("cst", [P, N_CONST])
        rw = sb("rw", [P, DT, N_EXPERTS])
        rb = sb("rb", [P, N_EXPERTS])
        R1_at = nc.sbuf_base
        R1 = sb("R1", [P, 10752])
        GR = sb("GR", [P, 6144])
        RE = sb("RE", [P, 3328])
        mixers_at = nc.sbuf_base
        rk = sb("rk", [P, 2, TOK])
        rq = sb("rq", [P, 2, TOK])
        rv = sb("rv", [P, NT, 512])
        rg = sb("rg", [P, NT, 512])
        rqd = sb("rqd", [P, 2, 2, LS])
        kd = sb("kd", [P, 2, HEADS, 64])
        st_out = sb("st_out", [64, 2, HEADS * DV])
        qB = sb("qB", [P, 2, TOK])
        kB = sb("kB", [P, TOK])
        vB = sb("vB", [P, NT, P])
        rt_tmp = sb("rt_tmp", [P, 3, LS])
        yaT = sb("yaT", [P, 2, TOK])
        ybT = sb("ybT", [P, 2, TOK])
        ydT = sb("ydT", [P, 2, TOK])
        mixers_end = nc.sbuf_base
        stats = sb("stats", [P, NT, 2, 6])
        mv = sb("mv", [P, 6, 2])
        rstd = sb("rstd", [P, 6])
        sm = sb("sm", [P, 5, HEADS])
        lg = sb("lg", [P, 12])
        dkc = sb("dkc", [P, 2, HEADS])

        split_at = [mixers_at]

        def split(name, *shape):
            t = nc.alloc_sbuf_tensor_at(name, [P, *shape], F32R, offset=split_at[0])
            split_at[0] += 4 * int(np.prod(shape))
            assert split_at[0] <= mixers_end
            return t

        w_hi, w_lo = split("w_hi", SPLIT_SLOTS, DT * P), split("w_lo", SPLIT_SLOTS, DT * P)
        h_lo = split("h_lo", DT, TOK)
        hid_hi, hid_lo = split("hid_hi", 2, TOK), split("hid_lo", 2, TOK)
        h_hi = nc.alloc_sbuf_tensor_at("h_hi", [P, DT, TOK], F32R, offset=R1_at)

        def region(t, at, *shape):
            n = int(np.prod(shape))
            v = t[:, at:at + n]
            if len(shape) == 2:
                return v.rearrange("p (a b) -> p a b", a=shape[0])
            if len(shape) == 3:
                return v.rearrange("p (a b c) -> p a b c", a=shape[0], b=shape[1])
            return v

        def part(name):
            a, w = PART_AT[name]
            return prm[:, a:a + w]

        def const(name):
            a, w = CONST_AT[name]
            return cst[:, a:a + w]

        Kc, Ks = region(R1, 0, FT, 512), region(R1, 1536, FT, 512)
        zc = region(R1, 3072, 6, TOK)
        U = region(R1, 5376, FT, 2, HYC)
        Yc, Ys = region(R1, 6912, FT, HYC), region(R1, 7680, FT, HYC)
        vtok = region(R1, 8448, NT, HYC)
        hyA, hyB = region(R1, 9216, FT, HYC), region(R1, 9984, FT, HYC)
        xn1 = region(R1, 5376, NT, D)
        dtok = region(R1, 0, NT, 416)
        cqT = region(R1, 1248, 2, TOK)
        ckvT = region(R1, 2016, TOK)
        krr = region(R1, 2400, TOK)
        qD = region(R1, 2784, HEADS, TOK)
        kD = region(R1, 4320, HEADS, 512)
        vD = region(R1, 6368, 4, HEADS * MV)
        xn2 = region(R1, 0, NT, D)
        g2bc = region(R1, 3072, 2, D)
        cb = region(R1, 5120, 2, TOK)
        hid = region(R1, 5888, 2, TOK)
        sg = region(R1, 6656, 2, TOK)
        rtb = region(R1, 7680, 1024)
        merged = region(R1, 7680, DT, TOK)
        hs, hd = region(GR, 0, FT, 512), region(GR, 1536, FT, 512)
        hydec = region(GR, 3072, NT, 512)
        ftmp = region(GR, 4608, 512)
        w3 = region(GR, 5120, 1024)
        gates = region(GR, 0, 16, TOK)
        lnr = region(GR, 0, 4, D)
        g1bc = region(GR, 4096, 2, D)
        E = region(RE, 0, HEADS, 4, P)
        AT = region(RE, 2048, 2, 640)
        dst = region(RE, 2048, 6, P)
        S = region(RE, 0, HEADS, TOK)
        PT = region(RE, 1536, HEADS, TOK)
        mt = region(RE, 0, 2, TOK)
        mt2 = region(RE, 768, 2, TOK)
        fa = region(RE, 0, TOK)
        fb = rt_tmp[:, :, :].rearrange("p a b -> p (a b)")[:, 0:TOK]
        ycT = rv[:, :, :].rearrange("p a b -> p (a b)")[:, 0:4 * TOK].rearrange("p (a b) -> p a b", a=4)
        ident = const("ident")
        uq = part("w_uq").rearrange("p (a b) -> p a b", a=2)
        ukv = part("w_ukv").rearrange("p (a b) -> p a b", a=HEADS)
        comb = region(R1, 7680, NT, N_EXPERTS)
        combT = region(R1, 7680 + 64, TOK)
        scores = region(R1, 7680 + 512, NT * N_GROUPS, EPG)
        kout = region(R1, 9216, P)
        fc = region(RE, TOK, TOK)
        sqj = region(RE, 2048, 256)
        upd = region(RE, 0, 2, 512)
        mod_rows = ([region(R1, 512 * n, 512) for n in range(ADA_FIRST)]
                    + [region(R1, 9472 + 512 * (n % 2), 512) for n in range(ADA_FIRST, ADA_BLOCKS)])
        rows = region(R1, 7680 + 1024, 640)
        comb_rows = comb_dram.rearrange("(a b) (c n) -> a b c n", b=2, c=1)

        slot_loaded = [raw_sem(f"slot_loaded{s}") for s in range(SLOTS)]
        layer_free = raw_sem("layer_free")
        filled = [raw_sem(f"bank_filled{b}") for b in range(BANKS)]
        drained = [raw_sem(f"bank_drained{b}") for b in range(BANKS)]
        zeros = ctx.enter_context(nc.sbuf_tensor("zeros", [P, 512], BF16))

        per_layer = {}

        def sem(name, increments):
            s = raw_sem(name)
            per_layer[name] = increments
            return s

        def nth(l, s, k):
            return l * per_layer[s.name] + k

        ada_used = sem("ada_used", ADA_BLOCKS * (ADA_UNITS - 1))
        mod_rows_ready = sem("mod_rows_ready", ADA_BLOCKS)
        out_used = sem("out_used", DT - 1)
        down_used = sem("down_used", 2 * N_EXPERTS)
        w_hi_ready = sem("w_hi_ready", 6 * N_EXPERTS)
        w_lo_ready = sem("w_lo_ready", 6 * N_EXPERTS)
        h_split = sem("h_split", DT)
        zeros_ready = raw_sem("zeros_ready")
        settled = raw_sem("settled")
        cst_ready = raw_sem("cst_ready")
        cond_ready = raw_sem("cond_ready")
        y_stored = raw_sem("y_stored")
        prm_ready = sem("prm_ready", 16)
        rows_ready = sem("rows_ready", 48)
        lnr_ready = sem("lnr_ready", 16)
        arg_ready = sem("arg_ready", 2)
        sin_ready = sem("sin_ready", 2)
        var_ready = sem("var_ready", 17)
        rstd_ready = sem("rstd_ready", 11)
        xn_ready = sem("xn_ready", 2)
        mod_ready = sem("mod_ready", ADA_BLOCKS)
        hT_even, hT_odd = sem("hT_even", 8), sem("hT_odd", 8)
        taps_ready = sem("taps_ready", 6)
        K_ready = sem("K_ready", 6)
        conv_ready = sem("conv_ready", 1)
        vtok_ready = sem("vtok_ready", 6)
        U_ready = sem("U_ready", 6)
        Yc_ready, Ys_ready = sem("Yc_ready", 2), sem("Ys_ready", 2)
        u_ready = sem("u_ready", 1)
        ya_ready = sem("ya_ready", 1)
        rk_ready, rq_ready = sem("rk_ready", 2), sem("rq_ready", 2)
        rv_ready, rg_ready = sem("rv_ready", 6), sem("rg_ready", 6)
        E_act, E_ready = sem("E_act", 1), sem("E_ready", 1)
        rqd_ready = sem("rqd_ready", 1)
        AT_ready = sem("AT_ready", 4)
        o_ready = sem("o_ready", 4)
        yc_ready = sem("yc_ready", 4)
        kd_ready = sem("kd_ready", 1)
        st_ready = sem("st_ready", 2)
        qB_raw, kB_raw, vB_ready = sem("qB_raw", 2), sem("kB_raw", 1), sem("vB_ready", 1)
        qkB_ready = sem("qkB_ready", 1)
        kout_ready = sem("kout_ready", 1)
        ms_ready = sem("ms_ready", 1)
        dtok_raw = sem("dtok_raw", 3)
        dtok_ready = sem("dtok_ready", 1)
        dT_ready = sem("dT_ready", 3)
        krr_ready = sem("krr_ready", 1)
        qD_ready = sem("qD_ready", 4)
        qrot_ready = sem("qrot_ready", 2)
        kD_nope, kD_rope = sem("kD_nope", 4), sem("kD_rope", 1)
        vD_ready = sem("vD_ready", 2)
        smax_ready = sem("smax_ready", 6)
        exp_ready = sem("exp_ready", 6)
        prob_ready = sem("prob_ready", 6)
        PT_ready = sem("PT_ready", 24)
        yb_ready, yd_ready = sem("yb_ready", 3), sem("yd_ready", 3)
        gate_ready = sem("gate_ready", 32)
        merged_ready = sem("merged_ready", 8)
        g1_ready, g2_ready = sem("g1_ready", 4), sem("g2_ready", 4)
        scores_ready = sem("scores_ready", 1)
        comb_ready = sem("comb_ready", 1)
        combT_ready = sem("combT_ready", 1)
        comb_stored = sem("comb_stored", 16)
        cb_ready = [sem(f"cb_ready{i}", 8 * 16) for i in range(2)]
        silu_ready = sem("silu_ready", 32)
        hid_ready = sem("hid_ready", 32)
        x2_ready = sem("x2_ready", 1)
        outs_stored = sem("outs_stored", 6 * 16)



        def settle(eng):
            eng.sem_inc(settled, 1)

        def bank(job):
            return JOB_AT[job] % BANKS

        def filling(l, job):
            return l * JOBS_LAYER[bank(job)] + JOB_AT[job] // BANKS + 2

        def draining(l, job):
            return l * JOBS_LAYER[bank(job)] + JOB_AT[job] // BANKS + 1

        def slot_of(unit):
            return UNIT_AT[unit] % SLOTS

        def loading(l, unit):
            s = slot_of(unit)
            return l * (16 * UNITS_LAYER[s]) + 16 * (UNIT_AT[unit] // SLOTS + 1)



        block = ctx.enter_context(nc.Block())

        @block.sync
        def _(sp):
            sp.dma_start(cst[:], consts).then_inc(cst_ready, 16)
            sp.dma_start(rw[:], router_w).then_inc(cst_ready, 16)
            sp.dma_start(rb[:], router_b).then_inc(cst_ready, 16)
            sp.dma_start(condS[:], cond).then_inc(cst_ready, 16)
            sp.dma_start(X[:], x_in).then_inc(cst_ready, 16)

            def source(l, u):
                if u.startswith("ada"):
                    return units_ada[l, int(u[3:])]
                if u.startswith("br"):
                    return units_br[l, 2 * int(u[2]) + "ab".index(u[3])]
                if u.startswith("out"):
                    return units_out[l, int(u[3:])]
                return units_in[l, IN_UNITS.index(u)]

            def slot(s):
                return ring[:, s, :, :].rearrange("p a b -> p (a b)")

            def wait_read(sp, l, u):
                if (job := reader(u)) is not None:
                    sp.wait_ge(filled[bank(job)], filling(l, job))
                    psum[:, bank(job), :]
                elif u.startswith("ada"):
                    n = int(u[3:])
                    sp.wait_ge(ada_used, nth(l, ada_used, (ADA_UNITS - 1) * (n // ADA_UNITS) + n % ADA_UNITS + 1))
                else:
                    sp.wait_ge(out_used, nth(l, out_used, int(u[3:]) + 1))

            with sp.Fori(0, DEPTH) as l:
                for i, u in enumerate(UNITS):
                    s = i % SLOTS
                    if i >= SLOTS:
                        wait_read(sp, l, UNITS[i - SLOTS])
                    else:
                        sp.wait_ge(w_lo_ready, nth(l, w_lo_ready, MOE_SLOT.index(s) + 1))
                    src = source(l, u)
                    sp.dma_start(slot(s)[:, 0:src.shape[1]], src).then_inc(slot_loaded[s], 16)
                    if i == 1:
                        sp.dma_start(prm[:], params[l]).then_inc(prm_ready, 16)
                for j, s in enumerate(MOE_SLOT):
                    wait_read(sp, l, UNITS[len(UNITS) - SLOTS + j])
                    sp.dma_start(slot(s), units_moe[l, 0, j]).then_inc(slot_loaded[s], 16)
                with sp.Fori(1, N_EXPERTS) as e:
                    for j, s in enumerate(MOE_SLOT):
                        sp.wait_ge(w_lo_ready, l * (6 * N_EXPERTS) + e * 6 + j + 1)
                        sp.dma_start(slot(s), units_moe[l, e, j]).then_inc(slot_loaded[s], 16)
            sp.wait_ge(x2_ready, DEPTH)
            sp.dma_start(y_prompt, X[:, 0, :]).then_inc(y_stored, 16)
            sp.dma_start(y_sample, X[:, 1:NT, :]).then_inc(y_stored, 16)
            sp.wait_ge(y_stored, 32)
            sp.wait_ge(outs_stored, DEPTH * 6 * 16)

        @block.tensor
        def _(pe):
            for b in range(BANKS):
                pe.sem_inc(drained[b], 1)
                pe.sem_inc(filled[b], 1)
            pe.sem_inc(down_used, 2)
            pe.sem_inc(w_lo_ready, SLOTS)
            pe.sem_inc(layer_free, 1)
            pe.wait_ge(cst_ready, 80)
            pe.wait_ge(cond_ready, 1)
            pe.wait_ge(zeros_ready, 1)
            layer = ExitStack()
            l = layer.enter_context(pe.Fori(0, DEPTH))
            mm = nc.tensor.matmul




            def project(u, job):
                pe.wait_ge(slot_loaded[slot_of(u)], loading(l, u))
                w = ring[:, slot_of(u), :, :]
                pe.wait_ge(drained[bank(job)], draining(l, job))
                o = psum[:, bank(job), :]
                for k in range(DT):
                    i = mm(o[:, 0:TOK], w[:, k, :], hT[:, k, :], start=k == 0, stop=k == DT - 1)
                i.then_inc(filled[bank(job)], 1)
            def project_rows(us, job):
                s = UNIT_AT[us[0]] % SLOTS
                for u in us:
                    pe.wait_ge(slot_loaded[slot_of(u)], loading(l, u))
                    ring[:, slot_of(u), :, :]
                for t in range(NT):
                    pe.wait_ge(drained[bank(f"{job}{t}")], draining(l, f"{job}{t}"))
                    o = psum[:, bank(f"{job}{t}"), :]
                    for k in range(DT):
                        i = mm(o[:, 0:256], hT[:, k, t * P:(t + 1) * P], ring[:, s:s + 2, k, :],
                               start=k == 0, stop=k == DT - 1)
                    i.then_inc(filled[bank(f"{job}{t}")], 1)

            def turn_rows(job, parts):
                pe.wait_ge(drained[bank(job)], draining(l, job))
                o = psum[:, bank(job), :]
                at = 0
                for a in parts:
                    n, m = a.shape[0], a.shape[1]
                    i = nc.tensor.transpose(o[0:m, at:at + n], a, ident[0:n, 0:n])
                    at += n
                i.then_inc(filled[bank(job)], 1)

            def do_gate(d, b):
                project(f"g{d}{b}", f"gate{d}{b}")

            def dft(order):
                pe.wait_ge(vtok_ready, nth(l, vtok_ready, 3 * order + 3))
                for f in range(FT):
                    pe.wait_ge(drained[bank(f"U{order}{f}")], draining(l, f"U{order}{f}"))
                    o = psum[:, bank(f"U{order}{f}"), :]
                    for cs in range(2):
                        if f == 0:
                            i = mm(o[:, cs * HYC:(cs + 1) * HYC], fwd_p[:, cs, :], vtok[:, 0, :], start=True, stop=True)
                        else:
                            for tt in range(2):
                                i = mm(o[:, cs * HYC:(cs + 1) * HYC], fwd_s[:, tt, cs, (f - 1) * P:f * P],
                                       vtok[:, 1 + tt, :], start=tt == 0, stop=tt == 1)
                    i.then_inc(filled[bank(f"U{order}{f}")], 1)

            def idft(order, name):
                pe.wait_ge(Yc_ready, nth(l, Yc_ready, order + 1))
                pe.wait_ge(Ys_ready, nth(l, Ys_ready, order + 1))
                for ct in range(2):
                    pe.wait_ge(drained[bank(f"{name}{ct}")], draining(l, f"{name}{ct}"))
                    o = psum[:, bank(f"{name}{ct}"), :]
                    cols = slice(ct * P, (ct + 1) * P)
                    mm(o[:, 0:LP], Yc[:, 0, cols], inv_p[:, 0, :], start=True, stop=False)
                    mm(o[:, 0:LP], Ys[:, 0, cols], inv_p[:, 1, :], start=False, stop=True)
                    for kt in range(2):
                        mm(o[:, LP:TOK], Yc[:, 1 + kt, cols], inv_s[:, kt, 0, :], start=kt == 0, stop=False)
                        i = mm(o[:, LP:TOK], Ys[:, 1 + kt, cols], inv_s[:, kt, 1, :], start=False, stop=kt == 1)
                    i.then_inc(filled[bank(f"{name}{ct}")], 1)

            def modulation(us, job):
                pe.wait_ge(drained[bank(job)], draining(l, job))
                o = psum[:, bank(job), :]
                for n, u in enumerate(us):
                    pe.wait_ge(slot_loaded[slot_of(u)], loading(l, u))
                    w = ring[:, slot_of(u), :, :]
                    settle(pe)
                    groups = P // COND_ROWS
                    for k in range(DT):
                        r = slice(COND_ROWS * (k % groups), COND_ROWS * (k % groups + 1))
                        i = mm(o[r, n * P:(n + 1) * P], condS[:, k, :], w[:, k, :], start=k < groups,
                               stop=k >= DT - groups, skip_group_check=True)
                    if n == len(us) - 1:
                        i.then_inc(filled[bank(job)], 1)
                    else:
                        i.then_inc(ada_used, 1)

            def modulation_columns(n):
                pe.wait_ge(mod_rows_ready, nth(l, mod_rows_ready, n + 1))
                pe.wait_ge(drained[bank(f"m{n}")], draining(l, f"m{n}"))
                o = psum[:, bank(f"m{n}"), :]
                for j in range(ADA_UNITS):
                    i = mm(o[:, 2 * j:2 * j + 2], mod_rows[n][:, j * P:(j + 1) * P], const("row_sel"),
                           start=True, stop=True)
                i.then_inc(filled[bank(f"m{n}")], 1)

            def rows_of(job, col, ready):
                pe.wait_ge(mod_ready, nth(l, mod_ready, ready))
                for c in range(2):
                    for h in range(2):
                        pe.wait_ge(drained[bank(f"{job}{c}{h}")], draining(l, f"{job}{c}{h}"))
                        o = psum[:, bank(f"{job}{c}{h}"), :]
                        for d in range(4):
                            i = mm(o[:, d * P:(d + 1) * P],
                                   modT[:, col + 4 * h + d, c:c + 1].to_broadcast([P, P]), ident, start=True, stop=True)
                        i.then_inc(filled[bank(f"{job}{c}{h}")], 1)

            def attend_scores(n, t):
                for h in range(HEADS):
                    pe.wait_ge(drained[bank(f"s{n}{t}{h}")], draining(l, f"s{n}{t}{h}"))
                    o = psum[:, bank(f"s{n}{t}{h}"), :]
                    if n == "B":
                        p = slice(64 * (h // 2), 64 * (h // 2) + 64)
                        q = qB[p, h % 2, t * P:(t + 1) * P]
                        if t == 0:
                            i = mm(o[:, 0:P], q, kB[p, 0:P], start=True, stop=True)
                        else:
                            mm(o[:, 0:LS], q, kB[p, LP:TOK], start=True, stop=True)
                            i = mm(o[:, LS:TOK], q, part("ctx_k")[p, :], start=True, stop=True)
                    else:
                        q = qD[0:QK, h, t * P:(t + 1) * P]
                        keys = kD[0:QK, h, 0:P] if t == 0 else kD[0:QK, h, LP:512]
                        i = mm(o[:, 0:P if t == 0 else TOK], q, keys, start=True, stop=True)
                    i.then_inc(filled[bank(f"s{n}{t}{h}")], 1)

            def attend_turn(n, t):
                pe.wait_ge(prob_ready, nth(l, prob_ready, (0 if n == "B" else 3) + t + 1))
                for h in range(HEADS):
                    turn_rows(f"p{n}{t}{h}", [S[:, h, c * P:(c + 1) * P] for c in range(1 if t == 0 else 3)])

            def attend_out(n, t):
                pe.wait_ge(PT_ready, nth(l, PT_ready, (0 if n == "B" else 12) + 4 * t + 4))
                pe.wait_ge(drained[bank(f"o{n}{t}")], draining(l, f"o{n}{t}"))
                o = psum[:, bank(f"o{n}{t}"), :]
                for h in range(HEADS):
                    p = slice(64 * (h % 2), 64 * (h % 2) + 64)
                    tiles = [0] if t == 0 else [1, 2, 3]
                    for c, kt in enumerate(tiles):
                        if n == "B":
                            kv = slice(64 * (h // 2), 64 * (h // 2) + 64)
                            v = part("ctx_v")[:, kv] if kt == 3 else vB[:, kt, kv]
                        else:
                            v = vD[:, kt, h * MV:(h + 1) * MV]
                        i = mm(o[p, (h // 2) * P:(h // 2) * P + P], v, PT[:, h, c * P:(c + 1) * P],
                               start=c == 0, stop=c == len(tiles) - 1)
                i.then_inc(filled[bank(f"o{n}{t}")], 1)

            fwd_s = const("fwd_s").rearrange("p (a b c) -> p a b c", a=2, b=2)
            fwd_p = const("fwd_p").rearrange("p (a b) -> p a b", a=2)
            inv_s = const("inv_s").rearrange("p (a b c) -> p a b c", a=2, b=2)
            inv_p = const("inv_p").rearrange("p (a b) -> p a b", a=2)

            for name, us, js in stages():
                if name == "fil1":
                    pe.wait_ge(prm_ready, nth(l, prm_ready, 16))
                    pe.wait_ge(drained[bank("fil1")], draining(l, "fil1"))
                    o = psum[:, bank("fil1"), :]
                    settle(pe)
                    mm(o[0:HY_FFN, 0:TOK], part("hy_w1")[0:HY_EMB, :], const("zT")[0:HY_EMB, :],
                            start=True, stop=True).then_inc(filled[bank("fil1")], 1)
                elif name[0] == "a":
                    modulation(us, name)
                elif name[0] == "m":
                    modulation_columns(int(name[1:]))
                elif name == "fil2":
                    pe.wait_ge(sin_ready, nth(l, sin_ready, 1))
                    pe.wait_ge(drained[bank("fil2")], draining(l, "fil2"))
                    o = psum[:, bank("fil2"), :]
                    settle(pe)
                    mm(o[0:HY_FFN, 0:TOK], part("hy_w2")[0:HY_FFN, :], fa[0:HY_FFN, :],
                            start=True, stop=True).then_inc(filled[bank("fil2")], 1)
                elif name in ("hT", "h2T"):
                    xn = xn1 if name == "hT" else xn2
                    pe.wait_ge(xn_ready, nth(l, xn_ready, 1 if name == "hT" else 2))
                    for d in range(DT):
                        turn_rows(f"{name}{d}", [xn[:, t, d * P:(d + 1) * P] for t in range(NT)])
                elif name == "fil3":
                    pe.wait_ge(sin_ready, nth(l, sin_ready, 2))
                    pe.wait_ge(rows_ready, nth(l, rows_ready, 48))
                    for t in range(FT):
                        for o in range(2):
                            pe.wait_ge(drained[bank(f"fil3{t}{o}")], draining(l, f"fil3{t}{o}"))
                            mm(psum[:, bank(f"fil3{t}{o}"), :], fb[0:HY_FFN, t * P:(t + 1) * P],
                                    w3[0:HY_FFN, o * 512:(o + 1) * 512], start=True, stop=True).then_inc(filled[bank(f"fil3{t}{o}")], 1)
                elif name == "K":
                    pe.wait_ge(taps_ready, nth(l, taps_ready, 6))
                    for f in range(FT):
                        for cs, taps in ((0, hs), (1, hd)):
                            job = "K" + "cs"[cs] + str(f)
                            pe.wait_ge(drained[bank(job)], draining(l, job))
                            o = psum[:, bank(job), :]
                            if f == 0:
                                i = mm(o, fwd_p[:, cs, :], taps[:, 0, :], start=True, stop=True)
                            else:
                                for tt in range(2):
                                    i = mm(o, fwd_s[:, tt, cs, (f - 1) * P:f * P], taps[:, 1 + tt, :],
                                           start=tt == 0, stop=tt == 1)
                            i.then_inc(filled[bank(job)], 1)
                elif name == "hy":
                    pe.wait_ge(hT_even, nth(l, hT_even, 4))
                    pe.wait_ge(hT_odd, nth(l, hT_odd, 4))
                    for i6 in range(6):
                        project(f"hy{i6}", f"hy{i6}")
                elif name in ("rk", "rq", "wq"):
                    for u in us:
                        project(u, u)
                elif name == "wk":
                    project("wk", "wk")
                elif name == "wv":
                    pe.wait_ge(slot_loaded[slot_of("wv")], loading(l, "wv"))
                    w = ring[:, slot_of("wv"), :, :]
                    pe.wait_ge(drained[bank("wv")], draining(l, "wv"))
                    o = psum[:, bank("wv"), :]
                    for t in range(NT):
                        for k in range(DT):
                            i = mm(o[:, t * P:(t + 1) * P], hT[:, k, t * P:(t + 1) * P], w[:, k, :],
                                   start=k == 0, stop=k == DT - 1)
                    i.then_inc(filled[bank("wv")], 1)
                elif name == "vT":
                    pe.wait_ge(conv_ready, nth(l, conv_ready, 1))
                    for t in range(NT):
                        turn_rows(f"vT{t}", [zc[:, c, t * P:(t + 1) * P] for c in range(2)])
                elif name == "uT":
                    pe.wait_ge(u_ready, nth(l, u_ready, 1))
                    for t in range(NT):
                        turn_rows(f"uT{t}", [zc[:, c, t * P:(t + 1) * P] for c in range(2)])
                elif name in ("U0", "U1"):
                    dft(int(name[1]))
                elif name == "yv":
                    idft(0, "yv")
                elif name == "yu":
                    idft(1, "yu")
                elif name in ("rv0", "rv1", "rg0", "rg1", "cq"):
                    project_rows(us, name)
                elif name == "ck":
                    pe.wait_ge(slot_loaded[slot_of("ck")], loading(l, "ck"))
                    pe.wait_ge(slot_loaded[slot_of("krope")], loading(l, "krope"))
                    w1, w2 = ring[:, slot_of("ck"), :, :], ring[:, slot_of("krope"), :, :]
                    for t in range(NT):
                        pe.wait_ge(drained[bank(f"ck{t}")], draining(l, f"ck{t}"))
                        o = psum[:, bank(f"ck{t}"), :]
                        for k in range(DT):
                            mm(o[:, 0:P], hT[:, k, t * P:(t + 1) * P], w1[:, k, :], start=k == 0, stop=k == DT - 1)
                        for k in range(DT):
                            i = mm(o[:, P:P + ROPE], hT[:, k, t * P:(t + 1) * P], w2[:, k, 0:ROPE],
                                   start=k == 0, stop=k == DT - 1)
                        i.then_inc(filled[bank(f"ck{t}")], 1)
                elif name.startswith("ra"):
                    h = int(name[2])
                    if h == 0:
                        pe.wait_ge(rk_ready, nth(l, rk_ready, 2))
                        pe.wait_ge(rq_ready, nth(l, rq_ready, 2))
                    p, j = slice(64 * (h % 2), 64 * (h % 2) + 64), h // 2
                    pe.wait_ge(drained[bank(f"ra{h}a")], draining(l, f"ra{h}a"))
                    o = psum[:, bank(f"ra{h}a"), :]
                    mm(o[:, 0:LS], rk[p, j, LP:LP + P], rq[p, j, LP:TOK], start=True, stop=True)
                    mm(o[:, LS:TOK], rk[p, j, 0:P], rq[p, j, 0:P], start=True, stop=True).then_inc(filled[bank(f"ra{h}a")], 1)
                    pe.wait_ge(drained[bank(f"ra{h}b")], draining(l, f"ra{h}b"))
                    o = psum[:, bank(f"ra{h}b"), :]
                    mm(o[:, 0:LS], rk[p, j, LP + P:TOK], rq[p, j, LP:TOK], start=True, stop=True).then_inc(filled[bank(f"ra{h}b")], 1)
                elif name.startswith("ro"):
                    h = int(name[2])
                    if h == 0:
                        pe.wait_ge(rv_ready, nth(l, rv_ready, 6))
                        pe.wait_ge(rqd_ready, nth(l, rqd_ready, 1))
                    pe.wait_ge(AT_ready, nth(l, AT_ready, h + 1))
                    p, j = slice(64 * (h % 2), 64 * (h % 2) + 64), h // 2
                    A = AT[:, h % 2, :]
                    v = [rv[:, t, h * DV:(h + 1) * DV] for t in range(NT)]
                    s0 = [part(x).rearrange("p (a b) -> p a b", a=2)[p, j, :] for x in ("s0f", "s0b")]
                    pe.wait_ge(drained[bank(f"ro{h}")], draining(l, f"ro{h}"))
                    o = psum[:, bank(f"ro{h}"), :]
                    mm(o[:, 0:P], A[:, LS:TOK], v[0], start=True, stop=True)
                    for t in range(2):
                        oc = o[:, (1 + t) * P:(2 + t) * P]
                        mm(oc, A[:, t * P:(t + 1) * P], v[1], start=True, stop=False)
                        mm(oc, A[:, TOK + t * P:TOK + (t + 1) * P], v[2], start=False, stop=False)
                        mm(oc, rqd[p, 0, j, t * P:(t + 1) * P], s0[0], start=False, stop=False)
                        i = mm(oc, rqd[p, 1, j, t * P:(t + 1) * P], s0[1], start=False, stop=True)
                    i.then_inc(filled[bank(f"ro{h}")], 1)
                elif name == "kr":
                    turn_rows("kr", [rk[:, j, 0:P] for j in range(2)])
                elif name == "rs":
                    pe.wait_ge(kd_ready, nth(l, kd_ready, 1))
                    for x in range(2):
                        pe.wait_ge(drained[bank("rs" + "fb"[x])], draining(l, "rs" + "fb"[x]))
                        o = psum[:, bank("rs" + "fb"[x]), :]
                        for h in range(HEADS):
                            i = mm(o[0:64, h * DV:(h + 1) * DV], kd[:, x, h, :], rv[:, 0, h * DV:(h + 1) * DV],
                                   start=True, stop=True)
                        i.then_inc(filled[bank("rs" + "fb"[x])], 1)
                elif name == "qkrot":
                    pe.wait_ge(qB_raw, nth(l, qB_raw, 2))
                    pe.wait_ge(kB_raw, nth(l, kB_raw, 1))
                    pe.wait_ge(drained[bank("pq")], draining(l, "pq"))
                    o = psum[:, bank("pq"), :]
                    for j in range(2):
                        i = mm(o[:, j * LS:(j + 1) * LS], const("perm_b"), qB[:, j, LP:TOK], start=True, stop=True)
                    i.then_inc(filled[bank("pq")], 1)
                    pe.wait_ge(drained[bank("pk")], draining(l, "pk"))
                    mm(psum[:, bank("pk"), :][:, 0:LS], const("perm_b"), kB[:, LP:TOK], start=True, stop=True).then_inc(filled[bank("pk")], 1)
                elif name == "kBo":
                    turn_rows("kBo", [kB[:, 0:P]])
                elif name == "dT":
                    pe.wait_ge(dtok_ready, nth(l, dtok_ready, 1))
                    for j in range(2):
                        turn_rows(f"cqT{j}", [dtok[:, t, j * P:(j + 1) * P] for t in range(NT)])
                    turn_rows("ckT", [dtok[:, t, 256:384] for t in range(NT)])
                    turn_rows("krT", [dtok[:, t, 320:416] for t in range(NT)])
                elif name == "qD":
                    pe.wait_ge(dT_ready, nth(l, dT_ready, 3))
                    for h in range(HEADS):
                        pe.wait_ge(drained[bank(f"qD{h}")], draining(l, f"qD{h}"))
                        o = psum[:, bank(f"qD{h}"), :]
                        for k in range(2):
                            i = mm(o[0:QK, 0:TOK], uq[:, k, h * QK:(h + 1) * QK], cqT[:, k, :],
                                   start=k == 0, stop=k == 1)
                        i.then_inc(filled[bank(f"qD{h}")], 1)
                elif name == "rK":
                    pe.wait_ge(krr_ready, nth(l, krr_ready, 1))
                    pe.wait_ge(drained[bank("rK")], draining(l, "rK"))
                    o = psum[:, bank("rK"), :]
                    settle(pe)
                    mm(o[NOPE:QK, 0:LS], const("perm_d")[NOPE:QK, :], krr[NOPE:QK, LP:TOK],
                            start=True, stop=True).then_inc(filled[bank("rK")], 1)
                elif name == "kD":
                    for h in range(HEADS):
                        pe.wait_ge(drained[bank(f"kD{h}")], draining(l, f"kD{h}"))
                        o = psum[:, bank(f"kD{h}"), :]
                        w = ukv[:, h, 0:NOPE]
                        mm(o[0:NOPE, 0:TOK], w, ckvT, start=True, stop=True)
                        mm(o[0:NOPE, TOK:512], w, part("ctx_ckv"), start=True, stop=True).then_inc(filled[bank(f"kD{h}")], 1)
                elif name == "vD":
                    for x in range(2):
                        pe.wait_ge(drained[bank(f"vD{x}")], draining(l, f"vD{x}"))
                        o = psum[:, bank(f"vD{x}"), :]
                        for y in range(2):
                            kt = 2 * x + y
                            src = part("ctx_ckv") if kt == 3 else ckvT[:, kt * P:(kt + 1) * P]
                            i = mm(o[:, y * 256:(y + 1) * 256], src, ukv[:, :, NOPE:NOPE + MV], start=True, stop=True)
                        i.then_inc(filled[bank(f"vD{x}")], 1)
                elif name == "rD":
                    pe.wait_ge(qD_ready, nth(l, qD_ready, 4))
                    for x in range(2):
                        pe.wait_ge(drained[bank(f"rD{x}")], draining(l, f"rD{x}"))
                        o = psum[:, bank(f"rD{x}"), :]
                        settle(pe)
                        for y in range(2):
                            i = mm(o[NOPE:QK, y * LS:(y + 1) * LS], const("perm_d")[NOPE:QK, :],
                                   qD[NOPE:QK, 2 * x + y, LP:TOK], start=True, stop=True)
                        i.then_inc(filled[bank(f"rD{x}")], 1)
                elif name[:2] in ("sB", "sD"):
                    n, t = name[1], int(name[2])
                    if name == "sB0":
                        pe.wait_ge(qkB_ready, nth(l, qkB_ready, 1))
                        pe.wait_ge(vB_ready, nth(l, vB_ready, 1))
                    if name == "sD0":
                        pe.wait_ge(qrot_ready, nth(l, qrot_ready, 2))
                        pe.wait_ge(kD_nope, nth(l, kD_nope, 4))
                        pe.wait_ge(kD_rope, nth(l, kD_rope, 1))
                        pe.wait_ge(vD_ready, nth(l, vD_ready, 2))
                    attend_scores(n, t)
                elif name[:2] in ("pB", "pD"):
                    attend_turn(name[1], int(name[2]))
                elif name[:2] in ("oB", "oD"):
                    attend_out(name[1], int(name[2]))
                elif name == "ycT":
                    pe.wait_ge(yc_ready, nth(l, yc_ready, 4))
                    for k in range(4):
                        turn_rows(f"ycT{k}", [rg[:, t, k * P:(k + 1) * P] for t in range(NT)])
                elif name.startswith("gate"):
                    do_gate(int(name[4]), int(name[5]))
                elif name.startswith("br"):
                    d = int(name[2])
                    if d == 0:
                        pe.wait_ge(ya_ready, nth(l, ya_ready, 1))
                        pe.wait_ge(yb_ready, nth(l, yb_ready, 3))
                        pe.wait_ge(o_ready, nth(l, o_ready, 4))
                        pe.wait_ge(yd_ready, nth(l, yd_ready, 3))
                    pe.wait_ge(slot_loaded[slot_of(f"br{d}a")], loading(l, f"br{d}a"))
                    pe.wait_ge(slot_loaded[slot_of(f"br{d}b")], loading(l, f"br{d}b"))
                    wa, wb = ring[:, slot_of(f"br{d}a"), :, :], ring[:, slot_of(f"br{d}b"), :, :]
                    src = [yaT[:, 0, :], yaT[:, 1, :], ybT[:, 0, :], ybT[:, 1, :],
                           ycT[:, 0, :], ycT[:, 1, :], ycT[:, 2, :], ycT[:, 3, :], ydT[:, 0, :], ydT[:, 1, :]]
                    at = 0
                    for b, n in enumerate((2, 2, 4, 2)):
                        pe.wait_ge(drained[bank(f"br{d}{b}")], draining(l, f"br{d}{b}"))
                        o = psum[:, bank(f"br{d}{b}"), :]
                        for k in range(n):
                            w = (wa if at < 5 else wb)[:, at % 5, :]
                            i = mm(o[:, 0:TOK], w, src[at], start=k == 0, stop=k == n - 1)
                            at += 1
                        i.then_inc(filled[bank(f"br{d}{b}")], 1)
                elif name == "g1":
                    rows_of("g1", 16, 6)
                elif name == "g2":
                    rows_of("g2", 40, ADA_BLOCKS)
                elif name == "out":
                    pe.wait_ge(merged_ready, nth(l, merged_ready, 8))
                    for j in js:
                        pe.wait_ge(drained[bank(j)], draining(l, j))
                        psum[:, bank(j), :]
                    for k in range(DT):
                        pe.wait_ge(slot_loaded[slot_of(f"out{k}")], loading(l, f"out{k}"))
                        w = ring[:, slot_of(f"out{k}"), :, :].rearrange("p a b -> p (a b)")
                        for n, (t, h) in enumerate((t, h) for t in range(NT) for h in range(2)):
                            i = mm(psum[:, bank(js[n]), :], merged[:, k, t * P:(t + 1) * P], w[:, h * 512:(h + 1) * 512],
                                   start=k == 0, stop=k == DT - 1, skip_group_check=True)
                            if k == DT - 1:
                                i.then_inc(filled[bank(js[n])], 1)
                        if k < DT - 1:
                            i.then_inc(out_used, 1)
                elif name == "rt":
                    pe.wait_ge(hT_even, nth(l, hT_even, 8))
                    pe.wait_ge(hT_odd, nth(l, hT_odd, 8))
                    pe.wait_ge(drained[bank("rt")], draining(l, "rt"))
                    o = psum[:, bank("rt"), :]
                    for t in range(NT):
                        for k in range(DT):
                            i = mm(o[:, t * 16:(t + 1) * 16], hT[:, k, t * P:(t + 1) * P], rw[:, k, :],
                                   start=k == 0, stop=k == DT - 1)
                    i.then_inc(filled[bank("rt")], 1)
                elif name == "cbT":
                    pe.wait_ge(comb_ready, nth(l, comb_ready, 1))
                    turn_rows("cbT", [comb[:, t, :] for t in range(NT)])
                else:
                    raise AssertionError(name)

            pe.wait_ge(h_split, nth(l, h_split, DT))
            for b in range(SUM_BANK, BANKS):
                pe.wait_ge(drained[b], l * JOBS_LAYER[b] + JOBS_BEFORE[b] + 1)
                mm(psum[:, b, :], zeros[:, 0:P], zeros[:, :], start=True, stop=False, skip_group_check=True)
            with pe.Fori(0, N_EXPERTS) as e:
                for f in range(2):
                    for x, b in ((0, GATE_BANK), (1, UP_BANK)):
                        j = 2 * f + x
                        pe.wait_ge(w_lo_ready, l * (6 * N_EXPERTS) + e * 6 + SLOTS + j + 1)
                        hi, lo = w_hi[:, j % SPLIT_SLOTS, :], w_lo[:, j % SPLIT_SLOTS, :]
                        pe.wait_ge(drained[b], l * JOBS_LAYER[b] + e * 2 + JOBS_BEFORE[b] + f + 1)
                        o = psum[:, b, 0:TOK]
                        for k in range(DT):
                            c = slice(k * P, (k + 1) * P)
                            mm(o, hi[:, c], h_hi[:, k, :], start=k == 0, stop=False)
                            mm(o, hi[:, c], h_lo[:, k, :], start=False, stop=False)
                            i = mm(o, lo[:, c], h_hi[:, k, :], start=False, stop=k == DT - 1)
                        i.then_inc(filled[b], 1)
                for f in range(2):
                    j = 4 + f
                    pe.wait_ge(w_lo_ready, l * (6 * N_EXPERTS) + e * 6 + SLOTS + j + 1)
                    hi, lo = w_hi[:, j % SPLIT_SLOTS, :], w_lo[:, j % SPLIT_SLOTS, :]
                    pe.wait_ge(hid_ready, l * 32 + e * 2 + f + 1)
                    for t in range(NT):
                        a_hi, a_lo = hid_hi[:, f, t * P:(t + 1) * P], hid_lo[:, f, t * P:(t + 1) * P]
                        for h in range(2):
                            o, c = psum[:, SUM_BANK + 2 * t + h, :], slice(h * 512, (h + 1) * 512)
                            mm(o, a_hi, hi[:, c], start=False, stop=False, skip_group_check=True)
                            mm(o, a_hi, lo[:, c], start=False, stop=False, skip_group_check=True)
                            i = mm(o, a_lo, hi[:, c], start=False, stop=False, skip_group_check=True)
                    i.then_inc(down_used, 1)
            for b in range(SUM_BANK, BANKS):
                mm(psum[:, b, :], zeros[:, 0:P], zeros[:, :], start=False, stop=True,
                   skip_group_check=True).then_inc(filled[b], 1)
            layer.close()


        @block.gpsimd
        def _(pool):
            nc.gpsimd.memset(zeros[:], 0.0).then_inc(zeros_ready, 1)
            layer = ExitStack()
            l = layer.enter_context(pool.Fori(0, DEPTH))

            def product_s(order):
                pool.wait_ge(U_ready, nth(l, U_ready, 3 * order + 3))
                pool.wait_ge(K_ready, nth(l, K_ready, 6))
                if order == 1:
                    pool.wait_ge(filled[bank("yv1")], filling(l, "yv1"))
                    psum[:, bank("yv1"), :]
                o = slice(order * HYC, (order + 1) * HYC)
                nc.gpsimd.tensor_tensor(Ys, U[:, :, 0, :], Ks[:, :, o], ALU.mult)
                nc.gpsimd.tensor_tensor(hyB, U[:, :, 1, :], Kc[:, :, o], ALU.mult)
                pool.drain()
                nc.gpsimd.tensor_tensor(Ys, Ys, hyB, ALU.add).then_inc(Ys_ready, 1)

            pool.wait_ge(layer_free, l + 1)
            settle(pool)
            pool.dma_start(w3[0:HY_FFN, :], hy_w3[l]).then_inc(rows_ready, 16)
            pool.dma_start(hydec, hy_decay).then_inc(rows_ready, 16)
            pool.dma_start(dst, dist).then_inc(rows_ready, 16)
            for name, us, js in stages():
                if name == "U0":
                    product_s(0)
                elif name == "U1":
                    product_s(1)
                elif name == "wv":
                    pool.wait_ge(vB_ready, nth(l, vB_ready, 1))
                    settle(pool)
                    pool.dma_start(new_v[l], vB[:, 0, :]).then_inc(outs_stored, 16)
                elif name == "kBo":
                    pool.wait_ge(kout_ready, nth(l, kout_ready, 1))
                    settle(pool)
                    pool.dma_start(new_k[l], kout).then_inc(outs_stored, 16)
                elif name == "rs":
                    pool.wait_ge(st_ready, nth(l, st_ready, 2))
                    settle(pool)
                    pool.dma_start(new_rf[l].rearrange("h k v -> k h v"),
                                   st_out[:, 0, :].rearrange("k (h v) -> k h v", h=HEADS)).then_inc(outs_stored, 16)
                    pool.dma_start(new_rb[l].rearrange("h k v -> k h v"),
                                   st_out[:, 1, :].rearrange("k (h v) -> k h v", h=HEADS)).then_inc(outs_stored, 16)
                elif name == "dT":
                    pool.wait_ge(dtok_ready, nth(l, dtok_ready, 1))
                    settle(pool)
                    pool.dma_start(new_ckv[l], dtok[:, 0, 256:384]).then_inc(outs_stored, 16)
                    pool.dma_start(new_krope[l], dtok[:, 0, 384:416]).then_inc(outs_stored, 16)
            pool.wait_ge(merged_ready, nth(l, merged_ready, 8))
            settle(pool)
            pool.dma_start(lnr, ln_rows[l]).then_inc(lnr_ready, 16)
            pool.wait_ge(filled[bank(f"h2T{DT - 1}")], filling(l, f"h2T{DT - 1}"))
            psum[:, bank(f"h2T{DT - 1}"), :]
            pool.wait_ge(hT_even, nth(l, hT_even, 8))
            pool.wait_ge(hT_odd, nth(l, hT_odd, 8))
            settle(pool)
            for d in range(DT):
                nc.gpsimd.tensor_copy(h_hi[:, d, :], hT[:, d, :])
                pool.drain()
                nc.gpsimd.tensor_tensor(h_lo[:, d, :], hT[:, d, :], h_hi[:, d, :].bitcast(F32), ALU.subtract)
                pool.drain().then_inc(h_split, 1)
            pool.wait_ge(combT_ready, nth(l, combT_ready, 1))
            settle(pool)
            pool.dma_start(comb_dram, combT[0:N_EXPERTS, :]).then_inc(comb_stored, 16)
            pool.wait_ge(comb_stored, nth(l, comb_stored, 16))
            settle(pool)
            for i in range(2):
                pool.dma_start(cb[:, i, :], comb_dram[i:i + 1, :].to_broadcast([P, TOK])).then_inc(cb_ready[i], 16)
            with pool.Fori(1, N_EXPERTS // 2) as it:
                for i in range(2):
                    pool.wait_ge(hid_ready, l * 32 + it * 4 + 2 * i - 2)
                    settle(pool)
                    pool.dma_start(cb[:, i, :], comb_rows[it, i].to_broadcast([P, TOK])).then_inc(cb_ready[i], 16)
            layer.close()

        @block.scalar
        def _(act):
            F = nc.scalar.activation
            act.wait_ge(cst_ready, 80)
            F(condS[:], condS[:], ACT.Silu).then_inc(cond_ready, 1)
            layer = ExitStack()
            l = None
            var_turn = [NT]

            def rsqrt(a, b, value):
                act.wait_ge(var_ready, value)
                F(rstd[:, a:b], mv[:, a:b, 1], ACT.Ln)
                act.drain()
                return F(rstd[:, a:b], rstd[:, a:b], ACT.Exp, scale=-0.5)

            def next_var():
                var_turn[0] += 1
                return nth(l, var_ready, var_turn[0])

            def plain_norm(xn, t, value):
                rsqrt(NT + t, NT + t + 1, value)
                act.drain()
                F(nmean[:, t, 1:2], nmean[:, t, 0:1], ACT.Identity, scale=rstd[:, NT + t:NT + t + 1])
                act.drain()
                F(xn[:, t, :], X[:, t, :], ACT.Identity, scale=rstd[:, NT + t:NT + t + 1], bias=nmean[:, t, 1:2])

            def norms(xn):
                rsqrt(0, 1, next_var()).then_inc(rstd_ready, 1)
                rsqrt(1, 2, next_var()).then_inc(rstd_ready, 1)
                plain_norm(xn, 0, next_var())
                rsqrt(2, 3, next_var()).then_inc(rstd_ready, 1)
                plain_norm(xn, 1, next_var())
                plain_norm(xn, 2, next_var())
                act.drain().then_inc(xn_ready, 1)

            def take_gate(d, b):
                if d >= 4:
                    act.wait_ge(merged_ready, nth(l, merged_ready, d - 3))
                act.wait_ge(filled[bank(f"gate{d}{b}")], filling(l, f"gate{d}{b}"))
                F(gates[:, 4 * (d % 4) + b, :], psum[:, bank(f"gate{d}{b}"), 0:TOK], ACT.Sigmoid).then_inc(drained[bank(f"gate{d}{b}")], 1)
                act.drain().then_inc(gate_ready, 1)

            for t in range(NT):
                plain_norm(xn1, t, t + 1)
            act.drain().then_inc(xn_ready, 1)
            l = layer.enter_context(act.Fori(0, DEPTH))
            for name, us, js in stages():
                if name[0] == "a":
                    n = int(name[1:])
                    if n in (ADA_FIRST, ADA_FIRST + 1):
                        act.wait_ge(Yc_ready, nth(l, Yc_ready, 2))
                        act.wait_ge(Ys_ready, nth(l, Ys_ready, 2))
                    elif n > ADA_FIRST:
                        act.wait_ge(filled[bank(f"m{n - 2}")], filling(l, f"m{n - 2}"))
                        psum[:, bank(f"m{n - 2}"), :]
                    act.wait_ge(filled[bank(name)], filling(l, name))
                    F(mod_rows[n], psum[:, bank(name), :], ACT.Copy).then_inc(drained[bank(name)], 1)
                    act.drain().then_inc(mod_rows_ready, 1)
                elif name in ("hT", "h2T"):
                    act.wait_ge(mod_ready, nth(l, mod_ready, ADA_FIRST if name == "hT" else ADA_BLOCKS))
                    s, sc = (0, 8) if name == "hT" else (24, 32)
                    for d in range(1, DT, 2):
                        act.wait_ge(filled[bank(js[d])], filling(l, js[d]))
                        o = psum[:, bank(js[d]), :]
                        for c, (a, b) in enumerate(SEG):
                            i = F(hT[:, d, a:b], o[:, a:b], ACT.Identity, scale=modT[:, sc + d, c:c + 1],
                                  bias=modT[:, s + d, c:c + 1])
                        i.then_inc(drained[bank(js[d])], 1)
                        act.drain().then_inc(hT_odd, 1)
                elif name in ("fil1", "fil2"):
                    x = int(name[3]) - 1
                    act.wait_ge(arg_ready, nth(l, arg_ready, x + 1))
                    r = (fa, fb)[x][0:HY_FFN, :]
                    F(r, r, ACT.Sin).then_inc(sin_ready, 1)
                    if x == 0:
                        continue
                    act.wait_ge(prm_ready, nth(l, prm_ready, 16))
                    F(lg[:], part("decay"), ACT.Sigmoid)
                    act.drain()
                    F(lg[:], lg[:], ACT.Ln)
                    act.drain()
                    act.wait_ge(rows_ready, nth(l, rows_ready, 48))
                    act.wait_ge(filled[bank("fil2")], filling(l, "fil2"))
                    psum[:, bank("fil2"), :]
                    for h in range(HEADS):
                        F(E[:, h, 0:2, :], dst[:, 0:2, :], ACT.Exp, scale=lg[:, 4 + h:5 + h])
                        F(E[:, h, 2:4, :], dst[:, 2:4, :], ACT.Exp, scale=lg[:, h:h + 1])
                    for j in range(2):
                        F(rqd[:, 0, j, :], const("i_plus_1"), ACT.Exp, scale=lg[:, 8 + j:9 + j])
                        F(rqd[:, 1, j, :], const("l_minus_i"), ACT.Exp, scale=lg[:, 10 + j:11 + j])
                    F(dkc[:, 0, :], lg[:, 0:4], ACT.Exp, scale=const("p_fwd"))
                    F(dkc[:, 1, :], lg[:, 4:8], ACT.Exp, scale=const("p_bwd")).then_inc(E_act, 1)
                elif name == "K":
                    for j in js:
                        f = int(j[2])
                        act.wait_ge(filled[bank(j)], filling(l, j))
                        F((Kc if j[1] == "c" else Ks)[:, f, :], psum[:, bank(j), :], ACT.Copy).then_inc(drained[bank(j)], 1)
                        act.drain().then_inc(K_ready, 1)
                elif name == "rk":
                    for j in range(2):
                        act.wait_ge(filled[bank(f"rk{j}")], filling(l, f"rk{j}"))
                        F(rk[:, j, :], psum[:, bank(f"rk{j}"), 0:TOK], ACT.Copy, scale=64.0 ** -0.5).then_inc(drained[bank(f"rk{j}")], 1)
                        act.drain().then_inc(rk_ready, 1)
                elif name == "rq":
                    for j in range(2):
                        act.wait_ge(filled[bank(f"rq{j}")], filling(l, f"rq{j}"))
                        F(rq[:, j, :], psum[:, bank(f"rq{j}"), 0:TOK], ACT.Copy).then_inc(drained[bank(f"rq{j}")], 1)
                        act.drain().then_inc(rq_ready, 1)
                elif name in ("rv0", "rv1"):
                    if name == "rv0":
                        act.wait_ge(layer_free, l + 1)
                    c = 256 * int(name[2])
                    for t in range(NT):
                        act.wait_ge(filled[bank(f"{name}{t}")], filling(l, f"{name}{t}"))
                        F(rv[:, t, c:c + 256], psum[:, bank(f"{name}{t}"), 0:256], ACT.Copy).then_inc(drained[bank(f"{name}{t}")], 1)
                        act.drain().then_inc(rv_ready, 1)
                elif name in ("rg0", "rg1"):
                    c = 256 * int(name[2])
                    for t in range(NT):
                        act.wait_ge(filled[bank(f"{name}{t}")], filling(l, f"{name}{t}"))
                        F(rg[:, t, c:c + 256], psum[:, bank(f"{name}{t}"), 0:256], ACT.Silu).then_inc(drained[bank(f"{name}{t}")], 1)
                        act.drain().then_inc(rg_ready, 1)
                elif name in ("U0", "U1"):
                    for f in range(FT):
                        if name == "U1" and f == 0:
                            act.wait_ge(Yc_ready, nth(l, Yc_ready, 1))
                            act.wait_ge(Ys_ready, nth(l, Ys_ready, 1))
                        act.wait_ge(filled[bank(f"{name}{f}")], filling(l, f"{name}{f}"))
                        F(U[:, f, :, :].rearrange("p a b -> p (a b)"), psum[:, bank(f"{name}{f}"), :], ACT.Copy).then_inc(drained[bank(f"{name}{f}")], 1)
                        act.drain().then_inc(U_ready, 1)
                elif name == "wq":
                    for j in range(2):
                        act.wait_ge(filled[bank(f"wq{j}")], filling(l, f"wq{j}"))
                        F(qB[:, j, :], psum[:, bank(f"wq{j}"), 0:TOK], ACT.Copy).then_inc(drained[bank(f"wq{j}")], 1)
                        act.drain().then_inc(qB_raw, 1)
                elif name == "wk":
                    act.wait_ge(filled[bank("wk")], filling(l, "wk"))
                    F(kB[:], psum[:, bank("wk"), 0:TOK], ACT.Copy).then_inc(drained[bank("wk")], 1)
                    act.drain().then_inc(kB_raw, 1)
                elif name == "wv":
                    act.wait_ge(filled[bank("wv")], filling(l, "wv"))
                    F(vB[:].rearrange("p a b -> p (a b)"), psum[:, bank("wv"), 0:TOK], ACT.Copy).then_inc(drained[bank("wv")], 1)
                    act.drain().then_inc(vB_ready, 1)
                elif name.startswith("gate"):
                    take_gate(int(name[4]), int(name[5]))
                elif name.startswith("ro"):
                    rsqrt(0, NT, next_var()).then_inc(rstd_ready, 1)
                elif name == "rs":
                    for x in range(2):
                        act.wait_ge(filled[bank(js[x])], filling(l, js[x]))
                        F(st_out[:, x, :], psum[:, bank(js[x]), :][0:64, :], ACT.Copy).then_inc(drained[bank(js[x])], 1)
                        act.drain().then_inc(st_ready, 1)
                    act.wait_ge(dtok_raw, nth(l, dtok_raw, 3))
                    for t in range(NT):
                        F(sqj[:, 0:256], dtok[:, t, 0:256], ACT.Square, accum_out=mv[:, t, 1:2])
                        act.drain()
                        F(sqj[:, 0:128], dtok[:, t, 256:384], ACT.Square, accum_out=mv[:, 3 + t, 1:2])
                        act.drain()
                    F(mv[:, 0:3, 1], mv[:, 0:3, 1], ACT.Copy, scale=1.0 / 256)
                    i = F(mv[:, 3:6, 1], mv[:, 3:6, 1], ACT.Copy, scale=1.0 / 128)
                    i.then_inc(ms_ready, 1)
                    rsqrt(0, 2 * NT, next_var()).then_inc(rstd_ready, 1)
                elif name[:2] in ("sB", "sD"):
                    k = (0 if name[1] == "B" else 3) + int(name[2])
                    nk = P if name[2] == "0" else TOK
                    act.wait_ge(smax_ready, nth(l, smax_ready, k + 1))
                    for h in range(HEADS):
                        F(S[:, h, 0:nk], S[:, h, 0:nk], ACT.Exp, bias=sm[:, 0, h:h + 1], accum_out=sm[:, 1, h:h + 1])
                    if name[1] == "B":
                        F(sm[:, 2, :], sm[:, 2, :], ACT.Exp)
                    act.drain().then_inc(exp_ready, 1)
                elif name[:2] in ("pB", "pD"):
                    n = P if name[2] == "0" else TOK
                    for h in (1, 3):
                        act.wait_ge(filled[bank(js[h])], filling(l, js[h]))
                        F(PT[:, h, 0:n], psum[:, bank(js[h]), :][:, 0:n], ACT.Copy).then_inc(drained[bank(js[h])], 1)
                        act.drain().then_inc(PT_ready, 1)
                elif name == "dT":
                    for j in range(2):
                        act.wait_ge(filled[bank(js[j])], filling(l, js[j]))
                        F(cqT[:, j, :], psum[:, bank(js[j]), :][:, 0:TOK], ACT.Identity, scale=part("q_norm")[:, j:j + 1]).then_inc(drained[bank(js[j])], 1)
                        act.drain().then_inc(dT_ready, 1)
                    act.wait_ge(filled[bank("ckT")], filling(l, "ckT"))
                    F(ckvT, psum[:, bank("ckT"), 0:TOK], ACT.Copy).then_inc(drained[bank("ckT")], 1)
                    act.drain().then_inc(dT_ready, 1)
                elif name == "qD":
                    for h in range(HEADS):
                        act.wait_ge(filled[bank(js[h])], filling(l, js[h]))
                        F(qD[0:QK, h, :], psum[:, bank(js[h]), :][0:QK, 0:TOK], ACT.Copy).then_inc(drained[bank(js[h])], 1)
                        act.drain().then_inc(qD_ready, 1)
                elif name == "kD":
                    for h in range(HEADS):
                        act.wait_ge(filled[bank(js[h])], filling(l, js[h]))
                        F(kD[0:NOPE, h, :], psum[:, bank(js[h]), :][0:NOPE, :], ACT.Copy).then_inc(drained[bank(js[h])], 1)
                        act.drain().then_inc(kD_nope, 1)
                elif name == "vD":
                    for x in range(2):
                        act.wait_ge(filled[bank(js[x])], filling(l, js[x]))
                        F(vD[:, 2 * x:2 * x + 2, :].rearrange("p a b -> p (a b)"), psum[:, bank(js[x]), :], ACT.Copy).then_inc(drained[bank(js[x])], 1)
                        act.drain().then_inc(vD_ready, 1)
                elif name == "ycT":
                    for k in range(4):
                        act.wait_ge(filled[bank(js[k])], filling(l, js[k]))
                        F(ycT[:, k, :], psum[:, bank(js[k]), :][:, 0:TOK], ACT.Copy).then_inc(drained[bank(js[k])], 1)
                        act.drain().then_inc(o_ready, 1)
                elif name in ("g1", "g2"):
                    out = g1bc if name == "g1" else g2bc
                    if name == "g2":
                        act.wait_ge(filled[bank("oD2")], filling(l, "oD2"))
                        psum[:, bank("oD2"), :]
                    else:
                        act.wait_ge(merged_ready, nth(l, merged_ready, 8))
                    for c in range(2):
                        for h in range(2):
                            act.wait_ge(filled[bank(f"{name}{c}{h}")], filling(l, f"{name}{c}{h}"))
                            F(out[:, c, h * 512:(h + 1) * 512], psum[:, bank(f"{name}{c}{h}"), :], ACT.Copy).then_inc(drained[bank(f"{name}{c}{h}")], 1)
                            act.drain().then_inc(g1_ready if name == "g1" else g2_ready, 1)
                elif name == "rt":
                    act.wait_ge(filled[bank("rt")], filling(l, "rt"))
                    F(scores.rearrange("p a b -> p (a b)"), psum[:, bank("rt"), 0:NT * N_EXPERTS], ACT.Sigmoid).then_inc(drained[bank("rt")], 1)
                    act.drain().then_inc(scores_ready, 1)
                if name == "g2":
                    norms(xn2)
            with act.Fori(0, N_EXPERTS) as e:
                def high_part(j):
                    s = MOE_SLOT[j]
                    act.wait_ge(slot_loaded[s], l * (16 * UNITS_LAYER[s]) + e * 16 + 16 * (UNITS_BEFORE[s] + 1))
                    if j in (0, 3, 4, 5):
                        b = (UP_BANK, 0, 0, GATE_BANK, UP_BANK, GATE_BANK)[j]
                        f = (0, 0, 0, 1, 1, 2)[j]
                        act.wait_ge(filled[b], l * JOBS_LAYER[b] + e * 2 + JOBS_BEFORE[b] + f + 1)
                    else:
                        act.wait_ge(down_used, l * 32 + e * 2 + j)
                    F(w_hi[:, j % SPLIT_SLOTS, :], ring[:, s, :, :].rearrange("p a b -> p (a b)"), ACT.Copy)
                    act.drain().then_inc(w_hi_ready, 1)

                def silu_gate(f):
                    b = GATE_BANK
                    act.wait_ge(filled[b], l * JOBS_LAYER[b] + e * 2 + JOBS_BEFORE[b] + f + 2)
                    F(sg[:, f, :], psum[:, b, 0:TOK], ACT.Silu).then_inc(drained[b], 1)
                    act.drain().then_inc(silu_ready, 1)

                high_part(0)
                high_part(1)
                high_part(2)
                silu_gate(0)
                high_part(3)
                high_part(4)
                silu_gate(1)
                high_part(5)
            norms(xn1)
            layer.close()

        @block.vector
        def _(dve):
            V = nc.vector
            dve.wait_ge(cst_ready, 80)
            layer = ExitStack()
            rs_turn = [0]


            def variance(t, row):
                for h in range(2):
                    V.bn_stats(stats[:, t, h, :], X[:, t, h * 512:(h + 1) * 512])
                dve.drain()
                V.bn_aggr(mv[:, row, :], stats[:, t, :, :].rearrange("p a b -> p (a b)"))
                dve.drain()
                V.tensor_scalar(mv[:, row, 1:2], mv[:, row, 1:2], LN_EPS, None, ALU.add)
                if row >= NT:
                    V.tensor_scalar(nmean[:, t, 0:1], mv[:, row, 0:1], -1.0, None, ALU.mult)
                dve.drain().then_inc(var_ready, 1)

            def sine_argument(job, bias, r, n):
                dve.wait_ge(filled[bank(job)], filling(l, job))
                o = psum[:, bank(job), :]
                V.tensor_scalar(r, o[0:HY_FFN, 0:TOK], bias, None, ALU.add).then_inc(drained[bank(job)], 1)
                dve.drain()
                V.tensor_scalar(n, r, 1.0 / (2.0 * math.pi), ROUND, ALU.mult, ALU.add)
                dve.drain()
                V.tensor_scalar(n, n, ROUND, None, ALU.subtract)
                dve.drain()
                V.scalar_tensor_tensor(out=r, in0=n, scalar=-TWO_PI_A, in1=r, op0=ALU.mult, op1=ALU.add)
                dve.drain()
                V.scalar_tensor_tensor(out=r, in0=n, scalar=-TWO_PI_B, in1=r, op0=ALU.mult, op1=ALU.add)
                dve.drain()
                V.tensor_scalar(r, r, PI_BELOW, -PI_BELOW, ALU.min, ALU.max)
                dve.drain().then_inc(arg_ready, 1)


            def product_c(order):
                dve.wait_ge(U_ready, nth(l, U_ready, 3 * order + 3))
                dve.wait_ge(K_ready, nth(l, K_ready, 6))
                o = slice(order * HYC, (order + 1) * HYC)
                V.tensor_tensor(Yc, U[:, :, 0, :], Kc[:, :, o], ALU.mult)
                V.tensor_tensor(hyA, U[:, :, 1, :], Ks[:, :, o], ALU.mult)
                dve.drain()
                V.tensor_tensor(Yc, Yc, hyA, ALU.subtract)
                dve.drain().then_inc(Yc_ready, 1)

            def scaled_sum(js, gbc, t):
                for h in range(2):
                    c = slice(h * 512, h * 512 + 512)
                    j = js[2 * t + h]
                    dve.wait_ge(filled[bank(j)], filling(l, j))
                    V.tensor_tensor(upd[:, h, :], psum[:, bank(j), :], gbc[:, min(t, 1), c],
                                    ALU.mult).then_inc(drained[bank(j)], 1)
                dve.drain()
                V.scalar_tensor_tensor(out=X[:, t, :], in0=X[:, t, :], scalar=ALPHA,
                                       in1=upd.rearrange("p a b -> p (a b)"), op0=ALU.mult, op1=ALU.add)
                dve.drain()

            def norm_rows(t, g_row):
                rs_turn[0] += 1
                dve.wait_ge(rstd_ready, nth(l, rstd_ready, rs_turn[0]))
                V.scalar_tensor_tensor(out=X[:, t, :], in0=X[:, t, :], scalar=mv[:, t, 0:1], in1=lnr[:, g_row, :],
                                       op0=ALU.subtract, op1=ALU.mult)
                dve.drain()
                V.scalar_tensor_tensor(out=X[:, t, :], in0=X[:, t, :], scalar=rstd[:, t:t + 1],
                                       in1=lnr[:, g_row + 1, :], op0=ALU.mult, op1=ALU.add)
                dve.drain()

            def update(js, gbc, g_row):
                scaled_sum(js, gbc, 0)
                variance(0, 0)
                scaled_sum(js, gbc, 1)
                variance(1, 1)
                norm_rows(0, g_row)
                variance(0, NT)
                scaled_sum(js, gbc, 2)
                variance(2, 2)
                norm_rows(1, g_row)
                variance(1, NT + 1)
                norm_rows(2, g_row)
                variance(2, NT + 2)

            for t in range(NT):
                variance(t, NT + t)
            l = layer.enter_context(dve.Fori(0, DEPTH))
            dve.wait_ge(prm_ready, nth(l, prm_ready, 16))
            for name, us, js in stages():
                if name[0] == "m":
                    n = int(name[1:])
                    at = ADA_UNITS * n
                    m = modT[:, at:at + ADA_UNITS, :]
                    bias = part("b_ada")[:, at:at + ADA_UNITS].rearrange("p (a b) -> p a b", b=1).to_broadcast(
                        [P, ADA_UNITS, 2])
                    o = psum[:, bank(name), 0:2 * ADA_UNITS].rearrange("p (a b) -> p a b", b=2)
                    dve.wait_ge(filled[bank(name)], filling(l, name))
                    if at // DT in (1, 4):
                        V.scalar_tensor_tensor(out=m, in0=o, scalar=1.0, in1=bias, op0=ALU.add,
                                               op1=ALU.add).then_inc(drained[bank(name)], 1)
                    else:
                        V.tensor_tensor(m, o, bias, ALU.add).then_inc(drained[bank(name)], 1)
                    dve.drain().then_inc(mod_ready, 1)
                elif name in ("hT", "h2T"):
                    s, sc = (0, 8) if name == "hT" else (24, 32)
                    for d in range(0, DT, 2):
                        dve.wait_ge(filled[bank(js[d])], filling(l, js[d]))
                        o = psum[:, bank(js[d]), :]
                        for c, (a, b) in enumerate(SEG):
                            i = V.tensor_scalar(hT[:, d, a:b], o[:, a:b], modT[:, sc + d, c:c + 1],
                                                modT[:, s + d, c:c + 1], ALU.mult, ALU.add)
                        i.then_inc(drained[bank(js[d])], 1)
                        dve.drain().then_inc(hT_even, 1)
                elif name == "fil1":
                    sine_argument("fil1", part("hy_b1")[0:HY_FFN, :], fa[0:HY_FFN, :], fb[0:HY_FFN, :])
                elif name == "fil2":
                    dve.wait_ge(sin_ready, nth(l, sin_ready, 1))
                    sine_argument("fil2", part("hy_b2")[0:HY_FFN, :], fb[0:HY_FFN, :], fc[0:HY_FFN, :])
                elif name == "fil3":
                    dve.wait_ge(rows_ready, nth(l, rows_ready, 48))
                    for j in js:
                        t, o = int(j[4]), int(j[5])
                        dve.wait_ge(filled[bank(j)], filling(l, j))
                        V.tensor_tensor(ftmp, psum[:, bank(j), :], hydec[:, t, :], ALU.mult).then_inc(drained[bank(j)], 1)
                        dve.drain()
                        c = slice(o * HYC, (o + 1) * HYC)
                        V.tensor_tensor(hs[:, t, c], ftmp[:, 0:HYC], ftmp[:, HYC:512], ALU.add)
                        V.tensor_tensor(hd[:, t, c], ftmp[:, 0:HYC], ftmp[:, HYC:512], ALU.subtract)
                        dve.drain().then_inc(taps_ready, 1)
                    dve.wait_ge(E_act, nth(l, E_act, 1))
                    for x in (1, 2):
                        V.tensor_tensor(E[:, :, x, :], E[:, :, x, :],
                                        dst[:, 3 + x:4 + x, :].to_broadcast([P, HEADS, P]), ALU.mult)
                    dve.drain()
                    V.tensor_tensor(E[:, :, 1, :], E[:, :, 1, :], E[:, :, 2, :], ALU.add)
                    dve.drain()
                    V.tensor_copy(E[:, :, 2, :], E[:, :, 1, :])
                    dve.drain().then_inc(E_ready, 1)
                elif name == "hy":
                    cw = part("conv_w").rearrange("p (a b) -> p a b", a=6)
                    for n in range(6):
                        dve.wait_ge(filled[bank(js[n])], filling(l, js[n]))
                        o = psum[:, bank(js[n]), :]
                        z = zc[:, n, :]
                        V.tensor_scalar(z, o[:, 0:TOK], cw[:, n, 1:2], part("conv_b")[:, n:n + 1], ALU.mult, ALU.add)
                        dve.drain()
                        for a, b in SEG:
                            V.scalar_tensor_tensor(out=z[:, a + 1:b], in0=o[:, a:b - 1], scalar=cw[:, n, 0:1],
                                                   in1=z[:, a + 1:b], op0=ALU.mult, op1=ALU.add)
                        dve.drain()
                        for a, b in SEG:
                            i = V.scalar_tensor_tensor(out=z[:, a:b - 1], in0=o[:, a + 1:b], scalar=cw[:, n, 2:3],
                                                       in1=z[:, a:b - 1], op0=ALU.mult, op1=ALU.add)
                        i.then_inc(drained[bank(js[n])], 1)
                    dve.drain().then_inc(conv_ready, 1)
                elif name in ("vT", "uT"):
                    for t in range(NT):
                        dve.wait_ge(filled[bank(f"{name}{t}")], filling(l, f"{name}{t}"))
                        V.tensor_copy(vtok[:, t, :], psum[:, bank(f"{name}{t}"), 0:HYC]).then_inc(drained[bank(f"{name}{t}")], 1)
                        dve.drain().then_inc(vtok_ready, 1)
                elif name in ("rv1", "wq"):
                    if name == "rv1":
                        product_c(0)
                        dve.wait_ge(rq_ready, nth(l, rq_ready, 2))
                        for x in range(2):
                            V.tensor_tensor(rqd[:, x, :, :], rqd[:, x, :, :], rq[:, :, LP:TOK], ALU.mult)
                        dve.drain().then_inc(rqd_ready, 1)
                elif name == "yv":
                    for c in range(2):
                        dve.wait_ge(filled[bank(f"yv{c}")], filling(l, f"yv{c}"))
                        V.scalar_tensor_tensor(out=zc[:, c, :], in0=zc[:, c, :], scalar=part("hy_bias")[:, c:c + 1],
                                               in1=psum[:, bank(f"yv{c}"), :][:, 0:TOK], op0=ALU.mult,
                                               op1=ALU.add).then_inc(drained[bank(f"yv{c}")], 1)
                    dve.drain()
                    V.tensor_tensor(zc[:, 0:2, :], zc[:, 0:2, :], zc[:, 2:4, :], ALU.mult)
                    dve.drain().then_inc(u_ready, 1)
                elif name == "U1":
                    product_c(1)
                elif name == "yu":
                    for c in range(2):
                        dve.wait_ge(filled[bank(f"yu{c}")], filling(l, f"yu{c}"))
                        V.scalar_tensor_tensor(out=zc[:, c, :], in0=zc[:, c, :], scalar=part("hy_bias")[:, 2 + c:3 + c],
                                               in1=psum[:, bank(f"yu{c}"), :][:, 0:TOK], op0=ALU.mult,
                                               op1=ALU.add).then_inc(drained[bank(f"yu{c}")], 1)
                    dve.drain()
                    V.tensor_tensor(yaT[:], zc[:, 0:2, :], zc[:, 4:6, :], ALU.mult)
                    dve.drain().then_inc(ya_ready, 1)
                elif name.startswith("ra"):
                    h = int(name[2])
                    A = AT[:, h % 2, :]
                    dve.wait_ge(filled[bank(f"ra{h}a")], filling(l, f"ra{h}a"))
                    o = psum[:, bank(f"ra{h}a"), :]
                    V.tensor_tensor(A[:, 0:LS], o[:, 0:LS], E[:, h, 2:4, :].rearrange("p a b -> p (a b)"), ALU.mult)
                    V.tensor_tensor(A[:, LS:TOK], o[:, LS:TOK], E[:, h, 2, :], ALU.mult).then_inc(drained[bank(f"ra{h}a")], 1)
                    dve.wait_ge(filled[bank(f"ra{h}b")], filling(l, f"ra{h}b"))
                    o = psum[:, bank(f"ra{h}b"), :]
                    V.tensor_tensor(A[:, TOK:640], o[:, 0:LS],
                                              E[:, h, 0:2, :].rearrange("p a b -> p (a b)"), ALU.mult).then_inc(drained[bank(f"ra{h}b")], 1)
                    dve.drain().then_inc(AT_ready, 1)
                elif name.startswith("ro"):
                    h = int(name[2])
                    dve.wait_ge(filled[bank(name)], filling(l, name))
                    o = psum[:, bank(name), :]
                    for t in range(NT):
                        V.bn_stats(stats[:, t, 0, :], o[:, t * P:(t + 1) * P])
                    dve.drain()
                    for t in range(NT):
                        V.bn_aggr(mv[:, t, :], stats[:, t, 0, :])
                    dve.drain()
                    V.tensor_scalar(mv[:, 0:NT, 1], mv[:, 0:NT, 1], LN_EPS, None, ALU.add)
                    dve.drain().then_inc(var_ready, 1)
                    dve.wait_ge(rg_ready, nth(l, rg_ready, 6))
                    for t in range(NT):
                        r = rg[:, t, h * DV:(h + 1) * DV]
                        i = V.scalar_tensor_tensor(out=r, in0=o[:, t * P:(t + 1) * P], scalar=mv[:, t, 0:1], in1=r,
                                                   op0=ALU.subtract, op1=ALU.mult)
                    i.then_inc(drained[bank(name)], 1)
                    rs_turn[0] += 1
                    dve.drain()
                    dve.wait_ge(rstd_ready, nth(l, rstd_ready, rs_turn[0]))
                    for t in range(NT):
                        r = rg[:, t, h * DV:(h + 1) * DV]
                        V.tensor_scalar(r, r, rstd[:, t:t + 1], None, ALU.mult)
                    dve.drain().then_inc(yc_ready, 1)
                elif name == "kr":
                    dve.wait_ge(filled[bank("kr")], filling(l, "kr"))
                    o = psum[:, bank("kr"), :][:, 0:256].rearrange("p (a b) -> p a b", a=HEADS)
                    for x in range(2):
                        i = V.tensor_tensor(kd[:, x, :, :], o,
                                            dkc[:, x, :].rearrange("p (a b) -> p a b", b=1).to_broadcast([P, HEADS, 64]),
                                            ALU.mult)
                    i.then_inc(drained[bank("kr")], 1)
                    dve.drain().then_inc(kd_ready, 1)
                elif name == "qkrot":
                    dve.wait_ge(filled[bank("pq")], filling(l, "pq"))
                    o = psum[:, bank("pq"), :]
                    sb_, cb_ = const("sin_b"), const("cos_b")
                    for j in range(2):
                        i = V.tensor_tensor(rt_tmp[:, j, :], o[:, j * LS:(j + 1) * LS], sb_, ALU.mult)
                        V.tensor_tensor(qB[:, j, LP:TOK], qB[:, j, LP:TOK], cb_, ALU.mult)
                    dve.drain()
                    dve.sem_inc(drained[bank("pq")], 1)
                    dve.wait_ge(filled[bank("pk")], filling(l, "pk"))
                    V.tensor_tensor(rt_tmp[:, 2, :], psum[:, bank("pk"), :][:, 0:LS], sb_, ALU.mult).then_inc(drained[bank("pk")], 1)
                    V.tensor_tensor(kB[:, LP:TOK], kB[:, LP:TOK], cb_, ALU.mult)
                    dve.drain()
                    V.tensor_tensor(qB[:, :, LP:TOK], qB[:, :, LP:TOK], rt_tmp[:, 0:2, :], ALU.add)
                    V.tensor_tensor(kB[:, LP:TOK], kB[:, LP:TOK], rt_tmp[:, 2, :], ALU.add)
                    dve.drain().then_inc(qkB_ready, 1)
                elif name == "kBo":
                    dve.wait_ge(filled[bank("kBo")], filling(l, "kBo"))
                    V.tensor_copy(kout, psum[:, bank("kBo"), 0:P]).then_inc(drained[bank("kBo")], 1)
                    dve.drain().then_inc(kout_ready, 1)
                elif name in ("cq", "ck"):
                    for t in range(NT):
                        a, b = (0, 256) if name == "cq" else (256, 416)
                        dve.wait_ge(filled[bank(f"{name}{t}")], filling(l, f"{name}{t}"))
                        V.tensor_copy(dtok[:, t, a:b], psum[:, bank(f"{name}{t}"), :][:, 0:b - a]).then_inc(drained[bank(f"{name}{t}")], 1)
                        if name == "ck":
                            dve.drain().then_inc(dtok_raw, 1)
                    if name == "ck":
                        dve.wait_ge(ms_ready, nth(l, ms_ready, 1))
                        V.tensor_scalar(mv[:, :, 1], mv[:, :, 1], RMS_EPS, None, ALU.add)
                        dve.drain().then_inc(var_ready, 1)
                        rs_turn[0] += 1
                        dve.wait_ge(rstd_ready, nth(l, rstd_ready, rs_turn[0]))
                        for t in range(NT):
                            V.tensor_scalar(dtok[:, t, 0:256], dtok[:, t, 0:256], rstd[:, t:t + 1], None, ALU.mult)
                            V.scalar_tensor_tensor(out=dtok[:, t, 256:384], in0=dtok[:, t, 256:384],
                                                   scalar=rstd[:, 3 + t:4 + t], in1=part("kv_norm"),
                                                   op0=ALU.mult, op1=ALU.mult)
                        dve.drain().then_inc(dtok_ready, 1)
                elif name[:2] in ("sB", "sD"):
                    n, t = name[1], int(name[2])
                    nk = P if t == 0 else TOK
                    scale = (WIN_HD if n == "B" else QK) ** -0.5
                    for h in range(HEADS):
                        dve.wait_ge(filled[bank(js[h])], filling(l, js[h]))
                        V.tensor_scalar(S[:, h, 0:nk], psum[:, bank(js[h]), :][:, 0:nk], scale, None, ALU.mult).then_inc(drained[bank(js[h])], 1)
                    dve.drain()
                    if n == "B" and t:
                        c = slice(P, 2 * P) if t == 1 else slice(0, P)
                        m = const("mask").rearrange("p (a b) -> p a b", a=2)[:, t - 1:t, :].to_broadcast([P, HEADS, P])
                        V.tensor_tensor(S[:, :, c], S[:, :, c], m, ALU.add)
                        dve.drain()
                    V.tensor_reduce(sm[:, 0, :], S[:, :, 0:nk], AX.X, ALU.max)
                    dve.drain()
                    if n == "B":
                        V.tensor_tensor(sm[:, 0, :], sm[:, 0, :], part("sink"), ALU.max)
                        dve.drain()
                        V.tensor_tensor(sm[:, 2, :], part("sink"), sm[:, 0, :], ALU.subtract)
                        dve.drain()
                    V.tensor_scalar(sm[:, 0, :], sm[:, 0, :], -1.0, None, ALU.mult)
                    dve.drain().then_inc(smax_ready, 1)
                    k = (0 if n == "B" else 3) + t
                    dve.wait_ge(exp_ready, nth(l, exp_ready, k + 1))
                    if n == "B":
                        V.tensor_tensor(sm[:, 1, :], sm[:, 1, :], sm[:, 2, :], ALU.add)
                        dve.drain()
                    V.reciprocal(sm[:, 3, :], sm[:, 1, :])
                    dve.drain()
                    for h in range(HEADS):
                        V.tensor_scalar(S[:, h, 0:nk], S[:, h, 0:nk], sm[:, 3, h:h + 1], None, ALU.mult)
                    dve.drain().then_inc(prob_ready, 1)
                elif name[:2] in ("pB", "pD"):
                    w = P if name[2] == "0" else TOK
                    for h in (0, 2):
                        dve.wait_ge(filled[bank(js[h])], filling(l, js[h]))
                        V.tensor_copy(PT[:, h, 0:w], psum[:, bank(js[h]), :][:, 0:w]).then_inc(drained[bank(js[h])], 1)
                        dve.drain().then_inc(PT_ready, 1)
                elif name[:2] in ("oB", "oD"):
                    t = int(name[2])
                    out, ready = (ybT, yb_ready) if name[1] == "B" else (ydT, yd_ready)
                    dve.wait_ge(filled[bank(name)], filling(l, name))
                    V.tensor_copy(out[:, :, t * P:(t + 1) * P], psum[:, bank(name), 0:256].rearrange("p (a b) -> p a b", a=2)).then_inc(drained[bank(name)], 1)
                    dve.drain().then_inc(ready, 1)
                elif name == "dT":
                    dve.wait_ge(filled[bank("krT")], filling(l, "krT"))
                    V.tensor_copy(krr[NOPE:QK, :], psum[:, bank("krT"), :][NOPE:QK, 0:TOK]).then_inc(drained[bank("krT")], 1)
                    dve.drain().then_inc(krr_ready, 1)
                elif name == "rK":
                    r = slice(NOPE, QK)
                    dve.wait_ge(filled[bank("rK")], filling(l, "rK"))
                    V.tensor_tensor(rt_tmp[r, 0, :], psum[:, bank("rK"), :][r, 0:LS], const("sin_d")[r, :],
                                              ALU.mult).then_inc(drained[bank("rK")], 1)
                    V.tensor_tensor(krr[r, LP:TOK], krr[r, LP:TOK], const("cos_d")[r, :], ALU.mult)
                    dve.drain()
                    V.tensor_tensor(krr[r, LP:TOK], krr[r, LP:TOK], rt_tmp[r, 0, :], ALU.add)
                    dve.drain()
                    for h in range(HEADS):
                        V.tensor_copy(kD[r, h, 0:TOK], krr[r, :])
                        V.tensor_copy(kD[r, h, TOK:512], part("ctx_kr")[r, :])
                    dve.drain().then_inc(kD_rope, 1)
                elif name == "rD":
                    r = slice(NOPE, QK)
                    for x in range(2):
                        dve.wait_ge(filled[bank(js[x])], filling(l, js[x]))
                        o = psum[:, bank(js[x]), :]
                        for y in range(2):
                            i = V.tensor_tensor(rt_tmp[r, y, :], o[r, y * LS:(y + 1) * LS], const("sin_d")[r, :], ALU.mult)
                        i.then_inc(drained[bank(js[x])], 1)
                        for y in range(2):
                            q = qD[r, 2 * x + y, LP:TOK]
                            V.tensor_tensor(q, q, const("cos_d")[r, :], ALU.mult)
                        dve.drain()
                        q = qD[r, 2 * x:2 * x + 2, LP:TOK]
                        V.tensor_tensor(q, q, rt_tmp[r, 0:2, :], ALU.add)
                        dve.drain().then_inc(qrot_ready, 1)
                elif name.startswith("br"):
                    d = int(name[2])
                    if d == 0:
                        dve.wait_ge(outs_stored, nth(l, outs_stored, 6 * 16))
                    dve.wait_ge(gate_ready, nth(l, gate_ready, 4 * d + 4))
                    for b in range(4):
                        g = gates[:, 4 * (d % 4) + b, :]
                        out = merged[:, d, :] if b == 0 else mt[:, b % 2, :]
                        dve.wait_ge(filled[bank(js[b])], filling(l, js[b]))
                        V.tensor_tensor(out, psum[:, bank(js[b]), :][:, 0:TOK], g, ALU.mult).then_inc(drained[bank(js[b])], 1)
                        dve.drain()
                        if b:
                            V.tensor_tensor(merged[:, d, :], merged[:, d, :], out, ALU.add)
                    dve.drain().then_inc(merged_ready, 1)
                elif name == "out":
                    dve.wait_ge(g1_ready, nth(l, g1_ready, 4))
                    dve.wait_ge(lnr_ready, nth(l, lnr_ready, 16))
                    update(js, g1bc, 0)
                elif name == "rt":
                    dve.wait_ge(scores_ready, nth(l, scores_ready, 1))
                    G = NT * N_GROUPS
                    b3 = rows[:, 0:48]
                    bg = b3.rearrange("p (g e) -> p g e", e=EPG)
                    sc = scores.rearrange("p g e -> p (g e)")
                    V.tensor_tensor(b3.rearrange("p (t e) -> p t e", t=NT), sc.rearrange("p (t e) -> p t e", t=NT),
                                    rb[:].rearrange("p (a e) -> p a e", a=1).to_broadcast([P, NT, N_EXPERTS]), ALU.add)
                    dve.drain()

                    def ranks(v, n, rank, big, ties):
                        shape = [P, n, EPG, EPG]
                        mine = v.rearrange("p g (e a) -> p g e a", a=1).to_broadcast(shape)
                        other = v.rearrange("p g (a e) -> p g a e", a=1).to_broadcast(shape)
                        B = big.rearrange("p (g e a) -> p g e a", e=EPG, a=EPG)
                        T = ties.rearrange("p (g e a) -> p g e a", e=EPG, a=EPG)
                        V.tensor_tensor(B, other, mine, ALU.is_gt)
                        V.tensor_tensor(T, other, mine, ALU.is_equal)
                        dve.drain()
                        V.tensor_tensor(T, T, const("tie").rearrange("p (g e a) -> p g e a", g=1, e=EPG)
                                        .to_broadcast(shape), ALU.mult)
                        dve.drain()
                        V.tensor_tensor(B, B, T, ALU.add)
                        dve.drain()
                        V.tensor_reduce(rank, B, AX.X, ALU.add)
                        dve.drain()

                    rank, sel = rows[:, 48:96].rearrange("p (g e) -> p g e", e=EPG), rows[:, 96:144]
                    selg = sel.rearrange("p (g e) -> p g e", e=EPG)
                    ranks(bg, G, rank, rows[:, 256:448], rows[:, 448:640])
                    V.tensor_scalar(selg, rank, 2.0, None, ALU.is_lt)
                    dve.drain()
                    V.tensor_tensor(rank, selg, bg, ALU.mult)
                    dve.drain()
                    gsum, grank = rows[:, 144:156], rows[:, 156:168]
                    V.tensor_reduce(gsum, rank, AX.X, ALU.add)
                    dve.drain()
                    ranks(gsum.rearrange("p (t g) -> p t g", t=NT), NT, grank.rearrange("p (t g) -> p t g", t=NT),
                          rows[:, 256:304], rows[:, 448:496])
                    V.tensor_scalar(grank, grank, 0.0, None, ALU.is_equal)
                    dve.drain()
                    V.tensor_tensor(selg, selg, grank.rearrange("p (g a) -> p g a", a=1).to_broadcast([P, G, EPG]),
                                    ALU.mult)
                    dve.drain()
                    V.tensor_tensor(sel, sel, sc, ALU.mult)
                    dve.drain()
                    wsum = rows[:, 168:171]
                    V.tensor_reduce(wsum, sel.rearrange("p (t e) -> p t e", t=NT), AX.X, ALU.add)
                    dve.drain()
                    V.reciprocal(wsum, wsum)
                    V.tensor_scalar(sel, sel, ROUTE_SCALE, None, ALU.mult)
                    dve.drain()
                    V.tensor_tensor(comb, sel.rearrange("p (t e) -> p t e", t=NT),
                                    wsum.rearrange("p (t a) -> p t a", a=1).to_broadcast([P, NT, N_EXPERTS]), ALU.mult)
                    dve.drain().then_inc(comb_ready, 1)
                elif name == "cbT":
                    dve.wait_ge(filled[bank("cbT")], filling(l, "cbT"))
                    V.tensor_copy(combT[0:N_EXPERTS, :], psum[:, bank("cbT"), :][0:N_EXPERTS, 0:TOK]).then_inc(drained[bank("cbT")], 1)
                    dve.drain().then_inc(combT_ready, 1)
            with dve.Fori(0, N_EXPERTS // 2) as it:
                for i in range(2):
                    def low_part(j):
                        dve.wait_ge(w_hi_ready, l * (6 * N_EXPERTS) + it * 12 + 6 * i + j + 1)
                        V.tensor_tensor(w_lo[:, j % SPLIT_SLOTS, :],
                                        ring[:, MOE_SLOT[j], :, :].rearrange("p a b -> p (a b)"),
                                        w_hi[:, j % SPLIT_SLOTS, :].bitcast(F32), ALU.subtract)
                        dve.drain().then_inc(w_lo_ready, 1)

                    def hidden(f):
                        b = UP_BANK
                        n = 2 * i + f
                        dve.wait_ge(filled[b], l * JOBS_LAYER[b] + it * 4 + JOBS_BEFORE[b] + n + 2)
                        dve.wait_ge(silu_ready, l * 32 + it * 4 + n + 1)
                        V.tensor_tensor(hid[:, f, :], psum[:, b, 0:TOK], sg[:, f, :], ALU.mult).then_inc(drained[b], 1)
                        dve.drain()
                        if f == 0:
                            dve.wait_ge(cb_ready[i], l * 128 + it * 16 + 16)
                        V.tensor_tensor(hid[:, f, :], hid[:, f, :], cb[:, i, :], ALU.mult)
                        dve.drain()
                        V.tensor_copy(hid_hi[:, f, :], hid[:, f, :])
                        dve.drain()
                        V.tensor_tensor(hid_lo[:, f, :], hid[:, f, :], hid_hi[:, f, :].bitcast(F32), ALU.subtract)
                        dve.drain().then_inc(hid_ready, 1)

                    low_part(0)
                    low_part(1)
                    low_part(2)
                    low_part(3)
                    hidden(0)
                    low_part(4)
                    low_part(5)
                    hidden(1)
            dve.wait_ge(g2_ready, nth(l, g2_ready, 4))
            update(SUM_JOBS, g2bc, 2)
            dve.drain().then_inc(x2_ready, 1)
            dve.sem_inc(layer_free, 1)
            layer.close()


def kernel(**inputs):
    import concourse.bacc as bacc
    from concourse.bass_utils import run_bass_kernel_spmd

    a = {k: np.asarray(v) for k, v in inputs.items()}

    def k_tiles(w):
        n = w.shape[2] // P
        return np.ascontiguousarray(w.reshape(w.shape[0], DT, P, n, P).transpose(0, 3, 2, 1, 4)).reshape(
            w.shape[0], n, P, DT * P)

    w_in = a["w_in"]
    at = np.cumsum([0, 768, 256, 128, 128, 256, 256, 512, 512, 256, 128, 32, 4096])
    hy, wq, wk, wv, rq, rk, rv, rg, cq, ck, kr, g = (w_in[:, :, at[i]:at[i + 1]] for i in range(12))
    wq = wq.reshape(DEPTH, D, 4, 64)[:, :, [0, 2, 1, 3]].reshape(DEPTH, D, 256)
    kr = np.concatenate([kr, np.zeros((DEPTH, D, P - ROPE), np.float32)], 2)
    g = g.reshape(DEPTH, D, 4, DT, P).transpose(0, 1, 3, 2, 4).reshape(DEPTH, D, 4 * D)
    arrays = {
        "units_ada": k_tiles(a["w_ada"]),
        "units_in": k_tiles(np.concatenate([hy, rk, rq, rv, rg, wq, wk, wv, cq, ck, kr, g], 2)),
        "units_out": np.ascontiguousarray(a["w_out"].reshape(DEPTH, DT, P, D)),
        "hy_w3": np.ascontiguousarray(a["hy_w3"]),
        "router_w": np.ascontiguousarray(a["router_w"].reshape(DT, P, N_EXPERTS).transpose(1, 0, 2)),
        "router_b": np.ascontiguousarray(np.broadcast_to(a["router_b"], (P, N_EXPERTS))),
    }
    br = np.concatenate([a["w_br_a"], a["w_br_b"], a["w_br_c"], a["w_br_d"]], 1)
    arrays["units_br"] = np.ascontiguousarray(
        br.reshape(DEPTH, 2, 5, P, DT, P).transpose(0, 4, 1, 3, 2, 5)).reshape(DEPTH, 2 * DT, P, 5 * P)
    up = [a[n].reshape(DEPTH, N_EXPERTS, DT, P, 2, P).transpose(0, 1, 4, 3, 2, 5).reshape(DEPTH, N_EXPERTS, 2, P, D)
          for n in ("moe_w_gate", "moe_w_up")]
    gu = np.stack(up, 3).reshape(DEPTH, N_EXPERTS, 4, P, D)
    down = a["moe_w_down"].reshape(DEPTH, N_EXPERTS, 2, P, D)
    arrays["units_moe"] = np.ascontiguousarray(np.concatenate([gu, down], 2))
    arrays["ln_rows"] = np.ascontiguousarray(np.broadcast_to(
        np.stack([a["ln1_g"], a["ln1_b"], a["ln2_g"], a["ln2_b"]], 1)[:, None], (DEPTH, P, 4, D)))
    arrays["x_in"] = np.ascontiguousarray(np.concatenate([a["x_prompt"][0], a["x_sample"][0]], 0)
                                          .reshape(NT, P, D).transpose(1, 0, 2))
    arrays["cond"] = np.zeros((P, DT, COND_ROWS), np.float32)
    arrays["cond"][:, :, 0] = a["c_ctx"].reshape(DT, P).T
    arrays["cond"][:, :, 1] = a["c"][0].reshape(DT, P).T

    def rows(x, n=P, at=0):
        out = np.zeros((DEPTH, P, int(np.prod(x.shape[2:]))), np.float32)
        out[:, at:at + x.shape[1]] = x.reshape(x.shape[0], x.shape[1], -1)
        return out

    def wide(x):
        return np.broadcast_to(x[:, None], (DEPTH, P) + x.shape[1:])

    def pairs(x):
        return np.stack([np.repeat(x[:, [2 * j, 2 * j + 1]], 64, 1) for j in range(2)], 2)

    def state(x):
        return x[0].reshape(DEPTH, 2, 2, 64, DV).transpose(0, 2, 3, 1, 4).reshape(DEPTH, P, 2, DV)

    df, db = a["ret_decay_fwd"], a["ret_decay_bwd"]
    p = {
        "conv_w": a["hy_conv_w"].reshape(DEPTH, 3, 6, P).transpose(0, 3, 2, 1),
        "conv_b": a["hy_conv_b"].reshape(DEPTH, 6, P).transpose(0, 2, 1),
        "hy_bias": a["hy_bias"].reshape(DEPTH, 4, P).transpose(0, 2, 1),
        "hy_b1": a["hy_b1"][:, :, None], "hy_b2": a["hy_b2"][:, :, None],
        "hy_w1": a["hy_w1"], "hy_w2": a["hy_w2"],
        "decay": np.concatenate([wide(df), wide(db), pairs(df), pairs(db)], 2),
        "q_norm": a["mla_q_norm"].reshape(DEPTH, 2, P).transpose(0, 2, 1),
        "b_ada": a["b_ada"].reshape(DEPTH, 48, P).transpose(0, 2, 1),
        "sink": wide(a["win_sink"]), "kv_norm": wide(a["mla_kv_norm"]),
        "s0f": state(a["state_ret_fwd"]), "s0b": state(a["state_ret_bwd"]),
        "ctx_k": a["cache_win_k"][0].reshape(DEPTH, LP, P).transpose(0, 2, 1),
        "ctx_v": a["cache_win_v"][0].reshape(DEPTH, LP, P),
        "ctx_ckv": a["cache_mla_ckv"][0].transpose(0, 2, 1),
        "w_uq": a["mla_w_uq"].reshape(DEPTH, 2, P, HEADS * QK).transpose(0, 2, 1, 3),
        "w_ukv": a["mla_w_ukv"],
    }
    p["ctx_kr"] = None
    blocks = []
    for name, w in PARTS:
        if name == "ctx_kr":
            b = rows(a["cache_mla_krope"][0].transpose(0, 2, 1), at=NOPE)
        else:
            b = rows(np.asarray(p[name]))
        assert b.shape[2] == w, name
        blocks.append(b)
    arrays["params"] = np.ascontiguousarray(np.concatenate(blocks, 2))
    arrays["consts"], arrays["dist"], arrays["hy_decay"] = shape_constants()

    nc = bacc.Bacc("TRN2", target_bir_lowering=False, num_devices=1)
    args = {n: nc.dram_tensor(n, v.shape, mybir.dt.from_np(v.dtype), kind="ExternalInput").ap()
            for n, v in arrays.items()}
    outs = {"y_prompt": (P, D), "y_sample": (P, 2, D), "new_k": (DEPTH, P, P), "new_v": (DEPTH, P, P),
            "new_ckv": (DEPTH, P, P), "new_krope": (DEPTH, P, ROPE), "new_rf": (DEPTH, HEADS, 64, DV),
            "new_rb": (DEPTH, HEADS, 64, DV)}
    for n, shape in outs.items():
        args[n] = nc.dram_tensor(n, shape, F32, kind="ExternalOutput").ap()
    build(nc, **args)
    r = run_bass_kernel_spmd(nc, [arrays], core_ids=[0]).results[0]
    return (r["y_prompt"].reshape(1, LP, D), r["y_sample"].transpose(1, 0, 2).reshape(1, LS, D),
            r["new_k"].reshape(1, DEPTH, LP, 2, 64), r["new_v"].reshape(1, DEPTH, LP, 2, 64),
            r["new_ckv"].reshape(1, DEPTH, LP, P), r["new_krope"].reshape(1, DEPTH, LP, ROPE),
            r["new_rf"].reshape(1, DEPTH, HEADS, 64, DV), r["new_rb"].reshape(1, DEPTH, HEADS, 64, DV))
```

```python
import math
from contextlib import ExitStack

import numpy as np

import concourse.bass as bass
from concourse import mybir

F32 = mybir.dt.float32
F32R = mybir.dt.float32r
BF16 = mybir.dt.bfloat16
ALU = mybir.AluOpType
ACT = mybir.ActivationFunctionType
AX = mybir.AxisListType

P = 128
D = 1024
DT = D // P
DEPTH = 2
LP, LS = 128, 256
TOK = LP + LS
NT = TOK // P
GRID_W = 64
SEG = ((0, LP), (LP, TOK))
HYC = 256
BANDS, HY_FFN = 16, 64
HY_EMB = 1 + 2 * BANDS
HEADS = 4
WIN_HD = 64
NOPE, ROPE, MV = 64, 32, 64
QK = NOPE + ROPE
DV = 128
N_EXPERTS, N_GROUPS, D_EXPERT = 16, 4, 256
EPG = N_EXPERTS // N_GROUPS
ROUTE_SCALE = 2.5
ALPHA = (2.0 * DEPTH) ** 0.25
LN_EPS, RMS_EPS = 1e-5, 1e-6
NEG = -1e30
TWO_PI_A = 6.28125
TWO_PI_B = 2.0 * math.pi - TWO_PI_A
ROUND = 1.5 * 2.0 ** 23
PI_BELOW = 3.1415925
SLOTS = 6
MIX_SLOTS = 4
SPLIT_SLOTS = 3
OUT_HELD = 4
BANKS = 8
ADA_UNITS = 2
ADA_BLOCKS = 6 * D // (ADA_UNITS * P)
ADA_FIRST = 2 * D // (ADA_UNITS * P)
FT = 3
GROUP = 32
GROUPS = P // GROUP



def reader(unit):
    if unit.startswith("ada"):
        n = int(unit[3:])
        return f"a{n // ADA_UNITS}" if n % ADA_UNITS == ADA_UNITS - 1 else None
    if unit.startswith("out"):
        return f"out{NT - 1}1" if unit == f"out{DT - 1}" else None
    if unit.startswith("br"):
        return unit[:3] + "3"
    if unit[:2] in ("rv", "rg", "cq", "ck"):
        n = int(unit[2])
        return None if n % 2 == 0 else unit[:2] + (str(n // 2) if unit[0] == "r" else "") + str(NT - 1)
    if unit == "krope":
        return "krp"
    if unit[0] == "g" and unit[1:].isdigit():
        return "gate" + unit[1:]
    return unit


def gate(d, b):
    return (f"gate{d}{b}", [f"g{d}{b}"], [f"gate{d}{b}"])


def ada(n):
    return (f"a{n}", [f"ada{ADA_UNITS * n + i}" for i in range(ADA_UNITS)], [f"a{n}"])


def mod(n):
    return (f"m{n}", [], [f"m{n}"])


def stages():
    s = [ada(n) for n in range(ADA_FIRST)] + [mod(n) for n in range(ADA_FIRST)] + [
         ("hT", [], [f"hT{d}" for d in range(DT)]),
         ("fil1", [], ["fil1"]),
         ("hy", [f"hy{i}" for i in range(6)], [f"hy{i}" for i in range(6)]),
         ("fil2", [], ["fil2"]),
         ("rk", ["rk0", "rk1"], ["rk0", "rk1"]),
         ("rq", ["rq0", "rq1"], ["rq0", "rq1"]),
         ("fil3", [], [f"fil3{t}{o}" for t in range(FT) for o in range(2)]),
         ("vT", [], [f"vT{t}" for t in range(NT)]),
         ("rv0", ["rv0", "rv1"], [f"rv0{t}" for t in range(NT)]),
         ("K", [], [f"K{x}{f}" for f in range(FT) for x in "cs"]),
         ("U0", [], [f"U0{f}" for f in range(FT)]),
         ("rv1", ["rv2", "rv3"], [f"rv1{t}" for t in range(NT)]),
         ("rg0", ["rg0", "rg1"], [f"rg0{t}" for t in range(NT)]),
         ("yv", [], ["yv0", "yv1"]),
         ("rg1", ["rg2", "rg3"], [f"rg1{t}" for t in range(NT)]),
         ("uT", [], [f"uT{t}" for t in range(NT)]),
         ("wq", ["wq0", "wq1"], ["wq0", "wq1"]),
         ("wk", ["wk"], ["wk"]),
         ("U1", [], [f"U1{f}" for f in range(FT)])]
    for h in range(HEADS):
        s += [(f"ra{h}", [], [f"ra{h}a", f"ra{h}b"])]
        s += [gate(0, h)]
        s += [(f"ro{h}", [], [f"ro{h}"])]
    blocks = iter(range(ADA_FIRST, ADA_BLOCKS))

    def block():
        n = next(blocks)
        return [ada(n)] + ([mod(n - 1)] if n > ADA_FIRST else [])

    s += [("yu", [], ["yu0", "yu1"]),
          ("kr", [], ["kr"]),
          ("qkrot", [], ["pq", "pk"]),
          ("kBo", [], ["kBo"]),
          ("cq", ["cq0", "cq1"], [f"cq{t}" for t in range(NT)]), *block(),
          ("ck", ["ck0", "ck1"], [f"ck{t}" for t in range(NT)]), *block(),
          ("krp", ["krope"], ["krp"]), *block(),
          ("rs", [], ["rsf", "rsb"])]
    for t in range(NT):
        s += [(f"sB{t}", [], [f"sB{t}{h}" for h in range(HEADS)])]
        if t == 2:
            s += [("dT", [], ["cqT0", "cqT1", "ckT", "krO"])]
        for d, b in ([(1, 0)], [(1, 1), (1, 2)], [(1, 3)])[t]:
            s += [gate(d, b), *block()]
        s += [(f"pB{t}", [], [f"pB{t}{h}" for h in range(HEADS)]), (f"oB{t}", [], [f"oB{t}"])]
    s += [("qD", [], [f"qD{h}" for h in range(HEADS)]), *block(),
          ("rK", [], ["rK"]),
          ("kD", [], [f"kD{h}" for h in range(HEADS)]), *block(),
          ("vD", [], ["vD0", "vD1"]),
          ("rD", [], ["rD0", "rD1"]), gate(2, 0), *block(), *block()]
    for t in range(NT):
        s += [(f"sD{t}", [], [f"sD{t}{h}" for h in range(HEADS)])]
        for d, b in ([(2, 1), (2, 2)], [(2, 3), (3, 0)], [(3, 1), (3, 2)])[t]:
            s += [gate(d, b)] + (block() if (d, b) != (3, 2) else [])
        s += [(f"pD{t}", [], [f"pD{t}{h}" for h in range(HEADS)]), (f"oD{t}", [], [f"oD{t}"])]
    s += [mod(ADA_BLOCKS - 1), gate(3, 3),
          ("ycT", [], [f"ycT{k}" for k in range(4)])]
    for d in range(DT):
        if d >= 4:
            s += [gate(d, b) for b in range(4)]
        s += [(f"br{d}", [f"br{d}a", f"br{d}b"], [f"br{d}{b}" for b in range(4)])]
    s += [("g1", [], [f"g1{c}{h}" for c in range(2) for h in range(2)]),
          ("out", [f"out{k}" for k in range(DT)], [f"out{t}{h}" for t in range(NT) for h in range(2)]),
          ("g2", [], [f"g2{c}{h}" for c in range(2) for h in range(2)]),
          ("h2T", [], [f"h2T{d}" for d in range(DT)]),
          ("rt", [], ["rt"]),
          ("rl", [], ["rl"]),
          ("cbT", [], ["cbT"])]
    return s


UNITS = [u for _, us, _ in stages() for u in us]
JOBS = [j for _, _, js in stages() for j in js]
UNIT_AT = {u: i for i, u in enumerate(UNITS)}
UNITS_BEFORE = [len(UNITS[s::MIX_SLOTS]) if s < MIX_SLOTS else 0 for s in range(SLOTS)]
UNITS_LAYER = [n + N_EXPERTS for n in UNITS_BEFORE]
MOE_SLOT = [(MIX_SLOTS + j) % SLOTS for j in range(SLOTS)]
IN_UNITS = ([f"hy{i}" for i in range(6)] + ["rk0", "rk1", "rq0", "rq1"] + [f"rv{i}" for i in range(4)]
            + [f"rg{i}" for i in range(4)] + ["wq0", "wq1", "wk", "cq0", "cq1", "ck0", "ck1", "krope"]
            + [f"g{d}{b}" for d in range(DT) for b in range(4)])
SPLIT_UNITS = [u for u in UNITS if u in IN_UNITS]
HALF_UNITS = [u for u in SPLIT_UNITS if reader(u) is None]
SPLIT_AT = {}
_read, _next = set(), 0
for _n, _us, _ in stages():
    SPLIT_AT[_n] = []
    for _more in ([], _us[:-1]):
        _read |= set(_more)
        while (_n[0] not in "ampo" and _next < len(SPLIT_UNITS)
               and (_next < 2 or SPLIT_UNITS[_next - 2] in _read)
               and UNITS[UNIT_AT[SPLIT_UNITS[_next]] - MIX_SLOTS] in _read):
            SPLIT_AT[_n].append(SPLIT_UNITS[_next])
            _next += 1
    _read |= set(_us)
assert _next == len(SPLIT_UNITS)
SUM_JOBS = [f"sum{t}{h}" for t in range(NT) for h in range(2)]
JOB_AT = {j: i for i, j in enumerate(JOBS)}
JOBS_BEFORE = [len(JOBS[b::BANKS]) for b in range(BANKS)]
assert JOB_AT["cbT"] % BANKS > 1
GATE_BANK, UP_BANK, SUM_BANK = 0, 1, 2
JOBS_LAYER = [n + (2 * N_EXPERTS if b < SUM_BANK else 1) for b, n in enumerate(JOBS_BEFORE)]

JOB_AT |= {j: BANKS * JOBS_BEFORE[SUM_BANK + n] + SUM_BANK + n for n, j in enumerate(SUM_JOBS)}

PARTS = [("conv_w", 18), ("conv_b", 6), ("hy_bias", 4), ("hy_b1", 1), ("hy_b2", 1), ("hy_w1", HY_FFN),
         ("hy_w2", HY_FFN), ("decay", 12), ("q_norm", 2), ("b_ada", 48), ("sink", HEADS), ("kv_norm", 128),
         ("s0f", 2 * DV), ("s0b", 2 * DV), ("ctx_k", LP), ("ctx_v", 2 * WIN_HD), ("ctx_ckv", LP), ("ctx_kr", LP),
         ("w_uq", 2 * HEADS * QK), ("w_ukv", HEADS * (NOPE + MV))]
PART_AT = {}
_at = 0
for _n, _w in PARTS:
    PART_AT[_n] = (_at, _w)
    _at += _w
N_PARAM = _at
CONSTS = [("fwd_s", 2 * 2 * LS), ("fwd_p", 2 * LP), ("inv_s", 2 * 2 * LS), ("inv_p", 2 * LP), ("zT", TOK),
          ("ident", P), ("perm_b", P), ("perm_d", ROPE), ("cos_b", LS), ("sin_b", LS), ("cos_d", LS), ("sin_d", LS),
          ("mask", 2 * P), ("i_plus_1", LS), ("l_minus_i", LS), ("p_fwd", 1), ("p_bwd", 1), ("tie", EPG * EPG),
          ("row_sel", 2), ("expert_sel", N_EXPERTS)]
CONST_AT = {}
_at = 0
for _n, _w in CONSTS:
    CONST_AT[_n] = (_at, _w)
    _at += _w
N_CONST = _at


def shape_constants():
    c = {}

    def dft(L):
        w = np.pi * (np.arange(L) + 0.5) / L
        a = np.arange(L)[:, None] * w[None, :]
        return np.cos(a), np.sin(a)

    def by_tile(a):
        return a.reshape(-1, P, a.shape[1]).transpose(1, 0, 2)

    for n, L in (("s", LS), ("p", LP)):
        fc, fs = dft(L)
        c["fwd_" + n] = np.stack([by_tile(fc), by_tile(fs)], 2)
        c["inv_" + n] = np.stack([by_tile(fc.T / L), by_tile(fs.T / L)], 2)
    zs, dec = [], []
    for L in (LP, LS):
        t01 = np.linspace(0.0, 1.0, L, dtype=np.float32)[:, None]
        bands = np.linspace(1e-4, BANDS - 1, BANDS, dtype=np.float32)
        ang = (np.float32(2.0 * math.pi / L) * np.arange(L, dtype=np.float32)[:, None]) * bands[None, :]
        zs.append(np.concatenate([t01, np.cos(ang), -np.sin(ang)], -1))
        deltas = np.abs(np.linspace(math.log(1e-2) / 1.5, math.log(1e-2) / 0.3, HYC, dtype=np.float32))
        d = np.exp(-t01 * deltas[None, :])
        b = d.copy()
        b[0] = 0.0
        dec.append(np.stack([d, b], 1))
    zT = np.zeros((P, TOK))
    zT[:HY_EMB] = np.concatenate(zs, 0).T
    c["zT"] = zT
    decay = np.concatenate(dec, 0).reshape(NT, P, 2 * HYC).transpose(1, 0, 2)
    c["ident"] = np.eye(P)

    def swap(n, half):
        m = np.zeros((n, n))
        for i in range(n):
            j = i + half if (i // half) % 2 == 0 else i - half
            m[j, i] = 1.0
        return m

    def rope(rot):
        nf = rot // 4
        inv = np.float32(10000.0) ** (-np.arange(nf, dtype=np.float32) / nf)
        row = np.repeat(np.arange(LS // GRID_W, dtype=np.float32), GRID_W)
        col = np.tile(np.arange(GRID_W, dtype=np.float32), LS // GRID_W)
        ang = np.concatenate([row[:, None] * inv, col[:, None] * inv], -1)
        co, si = np.cos(ang).T, np.sin(ang).T
        return np.concatenate([co, co], 0), np.concatenate([-si, si], 0)

    c["perm_b"] = swap(P, WIN_HD // 2)
    pd = np.zeros((P, ROPE))
    pd[NOPE:QK] = swap(ROPE, ROPE // 2)
    c["perm_d"] = pd
    cb, sb = rope(WIN_HD)
    c["cos_b"], c["sin_b"] = np.tile(cb, (2, 1)), np.tile(sb, (2, 1))
    cd, sd = rope(ROPE)
    for n, a in (("cos_d", cd), ("sin_d", sd)):
        m = np.zeros((P, LS))
        m[NOPE:QK] = a
        c[n] = m
    i, j = np.arange(P)[:, None], np.arange(P)[None, :]
    c["mask"] = np.stack([np.where(j <= i, 0.0, NEG), np.where(j >= i, 0.0, NEG)], 1)
    c["i_plus_1"] = np.broadcast_to(np.arange(LS) + 1.0, (P, LS))
    c["l_minus_i"] = np.broadcast_to(LS - np.arange(LS) * 1.0, (P, LS))
    c["p_fwd"] = (P - 1.0 - np.arange(P))[:, None]
    c["p_bwd"] = np.arange(P)[:, None] * 1.0
    c["tie"] = np.broadcast_to((np.arange(EPG)[None, :] < np.arange(EPG)[:, None]).astype(float).ravel(), (P, EPG * EPG))
    for n, w in (("row_sel", 2), ("expert_sel", N_EXPERTS)):
        c[n] = np.tile(np.eye(GROUP)[:, :w], (GROUPS, 1))
    block = np.concatenate([np.asarray(c[n], np.float32).reshape(P, w) for n, w in CONSTS], 1)
    dist = np.stack([P + i - j, np.maximum(i - j, 0), np.maximum(j - i, 0), P + j - i, i >= j, j >= i], 1)
    return (np.ascontiguousarray(block), np.ascontiguousarray(dist.astype(np.float32)),
            np.ascontiguousarray(decay.astype(np.float32)))


def build(nc, x_in, cond, units_ada, units_in, units_br, units_out, units_moe, params, hy_w3, ln_rows, router_w,
          router_b, consts, dist, hy_decay, y_prompt, y_sample, new_k, new_v, new_ckv, new_krope, new_rf, new_rb):
    x_dram = nc.dram_tensor("x_of_layer", [P, NT, D], F32, kind="Internal").ap()
    comb_dram = nc.dram_tensor("combine_rows", [N_EXPERTS, TOK], F32, kind="Internal").ap()
    with ExitStack() as ctx:
        def sb(name, shape):
            return ctx.enter_context(nc.sbuf_tensor(name, shape, F32))

        def raw_sem(name):
            return ctx.enter_context(nc.semaphore(name))

        psum = ctx.enter_context(nc.psum_tensor("psum", [P, BANKS, 512], F32))
        ring_at = -(-nc.sbuf_base // 32) * 32
        ring = sb("ring", [P, SLOTS, DT, P])
        X_at = nc.sbuf_base
        X = sb("X", [P, NT, D])
        hT_at = nc.sbuf_base
        sb("hT", [P, DT, TOK])
        modT = sb("modT", [P, 48, 2])
        condS = sb("condS", [P, DT, GROUP])
        nmean = sb("nmean", [P, NT, 2])
        prm = sb("prm", [P, N_PARAM])
        cst = sb("cst", [P, N_CONST])
        rw = sb("rw", [P, DT, GROUP])
        rb = sb("rb", [P, N_EXPERTS])
        R1_at = nc.sbuf_base
        R1 = sb("R1", [P, 10752])
        GR = sb("GR", [P, 6144])
        RE = sb("RE", [P, 3328])
        mixers_at = nc.sbuf_base
        rk = sb("rk", [P, 2, TOK])
        rq = sb("rq", [P, 2, TOK])
        rv = sb("rv", [P, NT, 512])
        rg = sb("rg", [P, NT, 512])
        rqd = sb("rqd", [P, 2, 2, LS])
        kd = sb("kd", [P, 2, HEADS, 64])
        st_out = sb("st_out", [64, 2, HEADS * DV])
        qB = sb("qB", [P, 2, TOK])
        kB = sb("kB", [P, TOK])
        vB = sb("vB", [P, NT, P])
        rt_tmp = sb("rt_tmp", [P, 3, LS])
        yaT = sb("yaT", [P, 2, TOK])
        ybT = sb("ybT", [P, 2, TOK])
        ydT = sb("ydT", [P, 2, TOK])
        mixers_end = nc.sbuf_base
        stats = sb("stats", [P, NT, 2, 6])
        mv = sb("mv", [P, 6, 2])
        rstd = sb("rstd", [P, 6])
        sm = sb("sm", [P, 5, HEADS])
        lg = sb("lg", [P, 12])
        dkc = sb("dkc", [P, 2, HEADS])

        split_at = [mixers_at]

        def split(name, *shape):
            t = nc.alloc_sbuf_tensor_at(name, [P, *shape], F32R, offset=split_at[0])
            split_at[0] += 4 * int(np.prod(shape))
            assert split_at[0] <= mixers_end
            return t

        w_hi, w_lo = split("w_hi", SPLIT_SLOTS, DT * P), split("w_lo", SPLIT_SLOTS, DT * P)
        h_lo = split("h_lo", DT, TOK)
        hid_hi, hid_lo = split("hid_hi", 2, TOK), split("hid_lo", 2, TOK)
        x_hi = nc.alloc_sbuf_tensor_at("x_hi", [P, DT, TOK], F32R, offset=hT_at)
        h_hi = x_hi
        x_lo = nc.alloc_sbuf_tensor_at("x_lo", [P, DT, TOK], F32R, offset=X_at)
        ring_lo = nc.alloc_sbuf_tensor_at("ring_lo", [P, MIX_SLOTS, DT * P], F32R, offset=ring_at)
        u_hi = nc.alloc_sbuf_tensor_at("u_hi", [P, SLOTS - MIX_SLOTS, DT * P], F32R,
                                       offset=ring_at + 4 * MIX_SLOTS * DT * P)

        def region(t, at, *shape):
            n = int(np.prod(shape))
            v = t[:, at:at + n]
            if len(shape) == 2:
                return v.rearrange("p (a b) -> p a b", a=shape[0])
            if len(shape) == 3:
                return v.rearrange("p (a b c) -> p a b c", a=shape[0], b=shape[1])
            return v

        def part(name):
            a, w = PART_AT[name]
            return prm[:, a:a + w]

        def const(name):
            a, w = CONST_AT[name]
            return cst[:, a:a + w]

        Kc, Ks = region(R1, 0, FT, 512), region(R1, 1536, FT, 512)
        zc = region(R1, 3072, 6, TOK)
        U = region(R1, 5376, FT, 2, HYC)
        Yc, Ys = region(R1, 6912, FT, HYC), region(R1, 7680, FT, HYC)
        vtok = region(R1, 8448, NT, HYC)
        hyA, hyB = region(R1, 9216, FT, HYC), region(R1, 9984, FT, HYC)
        xn1 = region(R1, 5376, NT, D)
        h32 = region(R1, 0, DT, TOK)
        h2 = region(RE, 0, DT, TOK)
        dtok = region(R1, 0, NT, 416)
        cqT = region(R1, 1248, 2, TOK)
        ckvT = region(R1, 2016, TOK)
        krr = region(R1, 2400, TOK)
        qD = region(R1, 2784, HEADS, TOK)
        kD = region(R1, 4320, HEADS, 512)
        vD = region(R1, 6368, 4, HEADS * MV)
        xn2 = region(R1, 0, NT, D)
        g2bc = region(R1, 3072, 2, D)
        cb = region(R1, 5120, 2, TOK)
        hid = region(R1, 5888, 2, TOK)
        sg = region(R1, 6656, 2, TOK)
        rtb = region(R1, 7680, 1024)
        merged = region(R1, 7680, DT, TOK)
        hs, hd = region(GR, 0, FT, 512), region(GR, 1536, FT, 512)
        hydec = region(GR, 3072, NT, 512)
        ftmp = region(GR, 4608, 512)
        w3 = region(GR, 5120, 1024)
        gates = region(GR, 0, 16, TOK)
        lnr = region(GR, 0, 4, D)
        g1bc = region(GR, 4096, 2, D)
        E = region(RE, 0, HEADS, 4, P)
        AT = region(RE, 2048, 2, 640)
        dst = region(RE, 2048, 6, P)
        S = region(RE, 0, HEADS, TOK)
        PT = region(RE, 1536, HEADS, TOK)
        mt = region(RE, 0, 2, TOK)
        mt2 = region(RE, 768, 2, TOK)
        fa = region(RE, 0, TOK)
        fb = rt_tmp[:, :, :].rearrange("p a b -> p (a b)")[:, 0:TOK]
        ycT = rv[:, :, :].rearrange("p a b -> p (a b)")[:, 0:4 * TOK].rearrange("p (a b) -> p a b", a=4)
        ident = const("ident")
        uq = part("w_uq").rearrange("p (a b) -> p a b", a=2)
        ukv = part("w_ukv").rearrange("p (a b) -> p a b", a=HEADS)
        comb = region(R1, 7680, NT, N_EXPERTS)
        combT = region(R1, 7680 + 64, TOK)
        scores = region(R1, 7680 + 512, NT * N_GROUPS, EPG)
        kout = region(R1, 9216, P)
        fc = region(RE, TOK, TOK)
        sqj = region(RE, 2048, 256)
        upd = region(RE, 0, 2, 512)
        mod_rows = ([region(R1, ADA_UNITS * P * n, ADA_UNITS * P) for n in range(ADA_FIRST)]
                    + [region(R1, 9472 + ADA_UNITS * P * (n % 2), ADA_UNITS * P) for n in range(ADA_FIRST, ADA_BLOCKS)])
        rows = region(R1, 7680 + 1024, 640)
        rt_rows = region(R1, 9472, TOK)
        comb_rows = comb_dram.rearrange("(a b) (c n) -> a b c n", b=2, c=1)

        slot_loaded = [raw_sem(f"slot_loaded{s}") for s in range(SLOTS)]
        layer_free = raw_sem("layer_free")
        filled = [raw_sem(f"bank_filled{b}") for b in range(BANKS)]
        drained = [raw_sem(f"bank_drained{b}") for b in range(BANKS)]
        zeros = ctx.enter_context(nc.sbuf_tensor("zeros", [P, 512], BF16))

        per_layer = {}

        def sem(name, increments):
            s = raw_sem(name)
            per_layer[name] = increments
            return s

        def nth(l, s, k):
            return l * per_layer[s.name] + k

        ada_used = sem("ada_used", ADA_BLOCKS * (ADA_UNITS - 1))
        mod_rows_ready = sem("mod_rows_ready", ADA_BLOCKS)
        out_used = sem("out_used", DT - 1)
        half_used = sem("half_used", len(HALF_UNITS))
        u_hi_ready = sem("u_hi_ready", len(SPLIT_UNITS))
        u_lo_ready = sem("u_lo_ready", len(SPLIT_UNITS))
        x_hi_ready = sem("x_hi_ready", 2 * DT)
        x_split = sem("x_split", DT)
        x_stored = sem("x_stored", 16)
        x_loaded = sem("x_loaded", 16)
        kro_ready = sem("kro_ready", 1)
        down_used = sem("down_used", 2 * N_EXPERTS)
        w_hi_ready = sem("w_hi_ready", 6 * N_EXPERTS)
        w_lo_ready = sem("w_lo_ready", 6 * N_EXPERTS)
        h_split = sem("h_split", DT)
        zeros_ready = raw_sem("zeros_ready")
        settled = raw_sem("settled")
        cst_ready = raw_sem("cst_ready")
        cond_ready = raw_sem("cond_ready")
        y_stored = raw_sem("y_stored")
        prm_ready = sem("prm_ready", 16)
        rows_ready = sem("rows_ready", 48)
        lnr_ready = sem("lnr_ready", 16)
        arg_ready = sem("arg_ready", 2)
        sin_ready = sem("sin_ready", 2)
        var_ready = sem("var_ready", 16)
        rstd_ready = sem("rstd_ready", 11)
        xn_ready = sem("xn_ready", 2)
        mod_ready = sem("mod_ready", ADA_BLOCKS)
        hT_even, hT_odd = sem("hT_even", 8), sem("hT_odd", 8)
        taps_ready = sem("taps_ready", 6)
        K_ready = sem("K_ready", 6)
        conv_ready = sem("conv_ready", 1)
        vtok_ready = sem("vtok_ready", 6)
        U_ready = sem("U_ready", 6)
        Yc_ready, Ys_ready = sem("Yc_ready", 2), sem("Ys_ready", 2)
        u_ready = sem("u_ready", 1)
        ya_ready = sem("ya_ready", 1)
        rk_ready, rq_ready = sem("rk_ready", 2), sem("rq_ready", 2)
        rv_ready, rg_ready = sem("rv_ready", 6), sem("rg_ready", 6)
        E_act, E_ready = sem("E_act", 1), sem("E_ready", 1)
        rqd_ready = sem("rqd_ready", 1)
        AT_ready = sem("AT_ready", 4)
        o_ready = sem("o_ready", 4)
        yc_ready = sem("yc_ready", 4)
        kd_ready = sem("kd_ready", 1)
        st_ready = sem("st_ready", 2)
        qB_raw, kB_raw, vB_ready = sem("qB_raw", 2), sem("kB_raw", 1), sem("vB_ready", NT)
        qkB_ready = sem("qkB_ready", 1)
        kout_ready = sem("kout_ready", 1)
        dtok_raw = sem("dtok_raw", 3)
        dtok_ready = sem("dtok_ready", 1)
        dT_ready = sem("dT_ready", 3)
        krr_ready = sem("krr_ready", 1)
        qD_ready = sem("qD_ready", 4)
        qrot_ready = sem("qrot_ready", 2)
        kD_nope, kD_rope = sem("kD_nope", 4), sem("kD_rope", 1)
        vD_ready = sem("vD_ready", 2)
        smax_ready = sem("smax_ready", 6)
        exp_ready = sem("exp_ready", 6)
        prob_ready = sem("prob_ready", 6)
        PT_ready = sem("PT_ready", 24)
        yb_ready, yd_ready = sem("yb_ready", 3), sem("yd_ready", 3)
        gate_ready = sem("gate_ready", 32)
        merged_ready = sem("merged_ready", 8)
        g1_ready, g2_ready = sem("g1_ready", 4), sem("g2_ready", 4)
        rt_rows_ready = sem("rt_rows_ready", 1)
        scores_ready = sem("scores_ready", 1)
        comb_ready = sem("comb_ready", 1)
        combT_ready = sem("combT_ready", 1)
        comb_stored = sem("comb_stored", 16)
        cb_ready = [sem(f"cb_ready{i}", 8 * 16) for i in range(2)]
        silu_ready = sem("silu_ready", 32)
        hid_ready = sem("hid_ready", 32)
        x2_ready = sem("x2_ready", 1)
        outs_stored = sem("outs_stored", 6 * 16)



        def settle(eng):
            eng.sem_inc(settled, 1)

        def bank(job):
            return JOB_AT[job] % BANKS

        def filling(l, job):
            return l * JOBS_LAYER[bank(job)] + JOB_AT[job] // BANKS + 2

        def draining(l, job):
            return l * JOBS_LAYER[bank(job)] + JOB_AT[job] // BANKS + 1

        def slot_of(unit):
            return UNIT_AT[unit] % MIX_SLOTS

        def loading(l, unit):
            s = slot_of(unit)
            return l * (16 * UNITS_LAYER[s]) + 16 * (UNIT_AT[unit] // MIX_SLOTS + 1)

        def wait_read(eng, l, u):
            if (job := reader(u)) is not None:
                eng.wait_ge(filled[bank(job)], filling(l, job))
                psum[:, bank(job), :]
            elif u.startswith("ada"):
                n = int(u[3:])
                eng.wait_ge(ada_used, nth(l, ada_used, (ADA_UNITS - 1) * (n // ADA_UNITS) + n % ADA_UNITS + 1))
            elif u in HALF_UNITS:
                eng.wait_ge(half_used, nth(l, half_used, HALF_UNITS.index(u) + 1))
            else:
                eng.wait_ge(out_used, nth(l, out_used, int(u[3:]) + 1))



        block = ctx.enter_context(nc.Block())

        @block.sync
        def _(sp):
            sp.dma_start(cst[:], consts).then_inc(cst_ready, 16)
            sp.dma_start(rw[:], router_w).then_inc(cst_ready, 16)
            sp.dma_start(rb[:], router_b).then_inc(cst_ready, 16)
            sp.dma_start(condS[:], cond).then_inc(cst_ready, 16)
            sp.dma_start(X[:], x_in).then_inc(cst_ready, 16)

            def source(l, u):
                if u.startswith("ada"):
                    return units_ada[l, int(u[3:])]
                if u.startswith("br"):
                    return units_br[l, 2 * int(u[2]) + "ab".index(u[3])]
                if u.startswith("out"):
                    return units_out[l, int(u[3:])]
                return units_in[l, IN_UNITS.index(u)]

            def slot(s):
                return ring[:, s, :, :].rearrange("p a b -> p (a b)")

            with sp.Fori(0, DEPTH) as l:
                for i, u in enumerate(UNITS):
                    s = i % MIX_SLOTS
                    if i >= MIX_SLOTS:
                        wait_read(sp, l, UNITS[i - MIX_SLOTS])
                    else:
                        sp.wait_ge(w_lo_ready, nth(l, w_lo_ready, MOE_SLOT.index(s) + 1))
                    src = source(l, u)
                    sp.dma_start(slot(s)[:, 0:src.shape[1]], src).then_inc(slot_loaded[s], 16)
                    if i == 1:
                        sp.dma_start(prm[:], params[l]).then_inc(prm_ready, 16)
                for j, s in enumerate(MOE_SLOT):
                    if s < MIX_SLOTS:
                        wait_read(sp, l, UNITS[max(i for i in range(s, len(UNITS), MIX_SLOTS))])
                    else:
                        wait_read(sp, l, SPLIT_UNITS[-1])
                    sp.dma_start(slot(s), units_moe[l, 0, j]).then_inc(slot_loaded[s], 16)
                with sp.Fori(1, N_EXPERTS) as e:
                    for j, s in enumerate(MOE_SLOT):
                        sp.wait_ge(w_lo_ready, l * (6 * N_EXPERTS) + e * 6 + j + 1)
                        sp.dma_start(slot(s), units_moe[l, e, j]).then_inc(slot_loaded[s], 16)
            sp.wait_ge(x2_ready, DEPTH)
            sp.dma_start(y_prompt, X[:, 0, :]).then_inc(y_stored, 16)
            sp.dma_start(y_sample, X[:, 1:NT, :]).then_inc(y_stored, 16)
            sp.wait_ge(y_stored, 32)
            sp.wait_ge(outs_stored, DEPTH * 6 * 16)

        @block.tensor
        def _(pe):
            for b in range(BANKS):
                pe.sem_inc(drained[b], 1)
                pe.sem_inc(filled[b], 1)
            pe.sem_inc(down_used, 2)
            pe.sem_inc(w_lo_ready, SLOTS)
            pe.sem_inc(layer_free, 1)
            pe.wait_ge(cst_ready, 80)
            pe.wait_ge(cond_ready, 1)
            pe.wait_ge(zeros_ready, 1)
            layer = ExitStack()
            l = layer.enter_context(pe.Fori(0, DEPTH))
            mm = nc.tensor.matmul




            def project(u, job):
                n = SPLIT_UNITS.index(u)
                pe.wait_ge(u_lo_ready, nth(l, u_lo_ready, n + 1))
                hi, lo = u_hi[:, n % 2, :], ring_lo[:, slot_of(u), :]
                pe.wait_ge(drained[bank(job)], draining(l, job))
                o = psum[:, bank(job), 0:TOK]
                for k in range(DT):
                    c = slice(k * P, (k + 1) * P)
                    if n == 0:
                        pe.wait_ge(x_split, nth(l, x_split, k + 1))
                    mm(o, hi[:, c], x_hi[:, k, :], start=k == 0, stop=False)
                    mm(o, hi[:, c], x_lo[:, k, :], start=False, stop=False)
                    i = mm(o, lo[:, c], x_hi[:, k, :], start=False, stop=k == DT - 1)
                i.then_inc(filled[bank(job)], 1)

            def project_rows(us, job):
                for half, u in enumerate(us):
                    n = SPLIT_UNITS.index(u)
                    pe.wait_ge(u_lo_ready, nth(l, u_lo_ready, n + 1))
                    hi, lo = u_hi[:, n % 2, :], ring_lo[:, slot_of(u), :]
                    for t in range(NT):
                        if half == 0:
                            pe.wait_ge(drained[bank(f"{job}{t}")], draining(l, f"{job}{t}"))
                        o = psum[:, bank(f"{job}{t}"), 0:256]
                        for k in range(DT // 2):
                            c = slice(k * 256, (k + 1) * 256)
                            kt = half * DT // 2 + k
                            a_hi, a_lo = x_hi[:, kt, t * P:(t + 1) * P], x_lo[:, kt, t * P:(t + 1) * P]
                            mm(o, a_hi, hi[:, c], start=kt == 0, stop=False, skip_group_check=True)
                            mm(o, a_hi, lo[:, c], start=False, stop=False, skip_group_check=True)
                            i = mm(o, a_lo, hi[:, c], start=False, stop=kt == DT - 1, skip_group_check=True)
                        if half == 1:
                            i.then_inc(filled[bank(f"{job}{t}")], 1)
                    if half == 0:
                        i.then_inc(half_used, 1)

            def turn_rows(job, parts):
                pe.wait_ge(drained[bank(job)], draining(l, job))
                o = psum[:, bank(job), :]
                at = 0
                for a in parts:
                    n, m = a.shape[0], a.shape[1]
                    i = nc.tensor.transpose(o[0:m, at:at + n], a, ident[0:n, 0:n])
                    at += n
                i.then_inc(filled[bank(job)], 1)

            def do_gate(d, b):
                project(f"g{d}{b}", f"gate{d}{b}")

            def dft(order):
                pe.wait_ge(vtok_ready, nth(l, vtok_ready, 3 * order + 3))
                for f in range(FT):
                    pe.wait_ge(drained[bank(f"U{order}{f}")], draining(l, f"U{order}{f}"))
                    o = psum[:, bank(f"U{order}{f}"), :]
                    for cs in range(2):
                        if f == 0:
                            i = mm(o[:, cs * HYC:(cs + 1) * HYC], fwd_p[:, cs, :], vtok[:, 0, :], start=True, stop=True)
                        else:
                            for tt in range(2):
                                i = mm(o[:, cs * HYC:(cs + 1) * HYC], fwd_s[:, tt, cs, (f - 1) * P:f * P],
                                       vtok[:, 1 + tt, :], start=tt == 0, stop=tt == 1)
                    i.then_inc(filled[bank(f"U{order}{f}")], 1)

            def idft(order, name):
                pe.wait_ge(Yc_ready, nth(l, Yc_ready, order + 1))
                pe.wait_ge(Ys_ready, nth(l, Ys_ready, order + 1))
                for ct in range(2):
                    pe.wait_ge(drained[bank(f"{name}{ct}")], draining(l, f"{name}{ct}"))
                    o = psum[:, bank(f"{name}{ct}"), :]
                    cols = slice(ct * P, (ct + 1) * P)
                    mm(o[:, 0:LP], Yc[:, 0, cols], inv_p[:, 0, :], start=True, stop=False)
                    mm(o[:, 0:LP], Ys[:, 0, cols], inv_p[:, 1, :], start=False, stop=True)
                    for kt in range(2):
                        mm(o[:, LP:TOK], Yc[:, 1 + kt, cols], inv_s[:, kt, 0, :], start=kt == 0, stop=False)
                        i = mm(o[:, LP:TOK], Ys[:, 1 + kt, cols], inv_s[:, kt, 1, :], start=False, stop=kt == 1)
                    i.then_inc(filled[bank(f"{name}{ct}")], 1)

            def modulation(us, job):
                pe.wait_ge(drained[bank(job)], draining(l, job))
                o = psum[:, bank(job), :]
                for n, u in enumerate(us):
                    pe.wait_ge(slot_loaded[slot_of(u)], loading(l, u))
                    w = ring[:, slot_of(u), :, :]
                    settle(pe)
                    for k in range(DT):
                        r = slice(GROUP * (k % GROUPS), GROUP * (k % GROUPS + 1))
                        i = mm(o[r, n * P:(n + 1) * P], condS[:, k, :], w[:, k, :], start=k < GROUPS,
                               stop=k >= DT - GROUPS, skip_group_check=True)
                    if n == len(us) - 1:
                        i.then_inc(filled[bank(job)], 1)
                    else:
                        i.then_inc(ada_used, 1)

            def modulation_columns(n):
                pe.wait_ge(mod_rows_ready, nth(l, mod_rows_ready, n + 1))
                pe.wait_ge(drained[bank(f"m{n}")], draining(l, f"m{n}"))
                o = psum[:, bank(f"m{n}"), :]
                for j in range(ADA_UNITS):
                    i = mm(o[:, 2 * j:2 * j + 2], mod_rows[n][:, j * P:(j + 1) * P], const("row_sel"),
                           start=True, stop=True)
                i.then_inc(filled[bank(f"m{n}")], 1)

            def rows_of(job, col, ready):
                pe.wait_ge(mod_ready, nth(l, mod_ready, ready))
                for c in range(2):
                    for h in range(2):
                        pe.wait_ge(drained[bank(f"{job}{c}{h}")], draining(l, f"{job}{c}{h}"))
                        o = psum[:, bank(f"{job}{c}{h}"), :]
                        for d in range(4):
                            i = mm(o[:, d * P:(d + 1) * P],
                                   modT[:, col + 4 * h + d, c:c + 1].to_broadcast([P, P]), ident, start=True, stop=True)
                        i.then_inc(filled[bank(f"{job}{c}{h}")], 1)

            def attend_scores(n, t):
                for h in range(HEADS):
                    pe.wait_ge(drained[bank(f"s{n}{t}{h}")], draining(l, f"s{n}{t}{h}"))
                    o = psum[:, bank(f"s{n}{t}{h}"), :]
                    if n == "B":
                        p = slice(64 * (h // 2), 64 * (h // 2) + 64)
                        q = qB[p, h % 2, t * P:(t + 1) * P]
                        if t == 0:
                            i = mm(o[:, 0:P], q, kB[p, 0:P], start=True, stop=True)
                        else:
                            mm(o[:, 0:LS], q, kB[p, LP:TOK], start=True, stop=True)
                            i = mm(o[:, LS:TOK], q, part("ctx_k")[p, :], start=True, stop=True)
                    else:
                        q = qD[0:QK, h, t * P:(t + 1) * P]
                        keys = kD[0:QK, h, 0:P] if t == 0 else kD[0:QK, h, LP:512]
                        i = mm(o[:, 0:P if t == 0 else TOK], q, keys, start=True, stop=True)
                    i.then_inc(filled[bank(f"s{n}{t}{h}")], 1)

            def attend_turn(n, t):
                pe.wait_ge(prob_ready, nth(l, prob_ready, (0 if n == "B" else 3) + t + 1))
                for h in range(HEADS):
                    turn_rows(f"p{n}{t}{h}", [S[:, h, c * P:(c + 1) * P] for c in range(1 if t == 0 else 3)])

            def attend_out(n, t):
                pe.wait_ge(PT_ready, nth(l, PT_ready, (0 if n == "B" else 12) + 4 * t + 4))
                pe.wait_ge(drained[bank(f"o{n}{t}")], draining(l, f"o{n}{t}"))
                o = psum[:, bank(f"o{n}{t}"), :]
                for h in range(HEADS):
                    p = slice(64 * (h % 2), 64 * (h % 2) + 64)
                    tiles = [0] if t == 0 else [1, 2, 3]
                    for c, kt in enumerate(tiles):
                        if n == "B":
                            kv = slice(64 * (h // 2), 64 * (h // 2) + 64)
                            v = part("ctx_v")[:, kv] if kt == 3 else vB[:, kt, kv]
                        else:
                            v = vD[:, kt, h * MV:(h + 1) * MV]
                        i = mm(o[p, (h // 2) * P:(h // 2) * P + P], v, PT[:, h, c * P:(c + 1) * P],
                               start=c == 0, stop=c == len(tiles) - 1)
                i.then_inc(filled[bank(f"o{n}{t}")], 1)

            fwd_s = const("fwd_s").rearrange("p (a b c) -> p a b c", a=2, b=2)
            fwd_p = const("fwd_p").rearrange("p (a b) -> p a b", a=2)
            inv_s = const("inv_s").rearrange("p (a b c) -> p a b c", a=2, b=2)
            inv_p = const("inv_p").rearrange("p (a b) -> p a b", a=2)

            for name, us, js in stages():
                if name == "fil1":
                    pe.wait_ge(prm_ready, nth(l, prm_ready, 16))
                    pe.wait_ge(drained[bank("fil1")], draining(l, "fil1"))
                    o = psum[:, bank("fil1"), :]
                    settle(pe)
                    mm(o[0:HY_FFN, 0:TOK], part("hy_w1")[0:HY_EMB, :], const("zT")[0:HY_EMB, :],
                            start=True, stop=True).then_inc(filled[bank("fil1")], 1)
                elif name[0] == "a":
                    modulation(us, name)
                elif name[0] == "m":
                    modulation_columns(int(name[1:]))
                elif name == "fil2":
                    pe.wait_ge(sin_ready, nth(l, sin_ready, 1))
                    pe.wait_ge(drained[bank("fil2")], draining(l, "fil2"))
                    o = psum[:, bank("fil2"), :]
                    settle(pe)
                    mm(o[0:HY_FFN, 0:TOK], part("hy_w2")[0:HY_FFN, :], fa[0:HY_FFN, :],
                            start=True, stop=True).then_inc(filled[bank("fil2")], 1)
                elif name in ("hT", "h2T"):
                    xn = xn1 if name == "hT" else xn2
                    pe.wait_ge(xn_ready, nth(l, xn_ready, 1 if name == "hT" else 2))
                    for d in range(DT):
                        turn_rows(f"{name}{d}", [xn[:, t, d * P:(d + 1) * P] for t in range(NT)])
                elif name == "fil3":
                    pe.wait_ge(sin_ready, nth(l, sin_ready, 2))
                    pe.wait_ge(rows_ready, nth(l, rows_ready, 48))
                    for t in range(FT):
                        for o in range(2):
                            pe.wait_ge(drained[bank(f"fil3{t}{o}")], draining(l, f"fil3{t}{o}"))
                            mm(psum[:, bank(f"fil3{t}{o}"), :], fb[0:HY_FFN, t * P:(t + 1) * P],
                                    w3[0:HY_FFN, o * 512:(o + 1) * 512], start=True, stop=True).then_inc(filled[bank(f"fil3{t}{o}")], 1)
                elif name == "K":
                    pe.wait_ge(taps_ready, nth(l, taps_ready, 6))
                    for f in range(FT):
                        for cs, taps in ((0, hs), (1, hd)):
                            job = "K" + "cs"[cs] + str(f)
                            pe.wait_ge(drained[bank(job)], draining(l, job))
                            o = psum[:, bank(job), :]
                            if f == 0:
                                i = mm(o, fwd_p[:, cs, :], taps[:, 0, :], start=True, stop=True)
                            else:
                                for tt in range(2):
                                    i = mm(o, fwd_s[:, tt, cs, (f - 1) * P:f * P], taps[:, 1 + tt, :],
                                           start=tt == 0, stop=tt == 1)
                            i.then_inc(filled[bank(job)], 1)
                elif name == "hy":
                    for i6 in range(6):
                        project(f"hy{i6}", f"hy{i6}")
                elif name in ("rk", "rq", "wq"):
                    for u in us:
                        project(u, u)
                elif name == "wk":
                    project("wk", "wk")
                elif name == "vT":
                    pe.wait_ge(conv_ready, nth(l, conv_ready, 1))
                    for t in range(NT):
                        turn_rows(f"vT{t}", [zc[:, c, t * P:(t + 1) * P] for c in range(2)])
                elif name == "uT":
                    pe.wait_ge(u_ready, nth(l, u_ready, 1))
                    for t in range(NT):
                        turn_rows(f"uT{t}", [zc[:, c, t * P:(t + 1) * P] for c in range(2)])
                elif name in ("U0", "U1"):
                    dft(int(name[1]))
                elif name == "yv":
                    idft(0, "yv")
                elif name == "yu":
                    idft(1, "yu")
                elif name in ("rv0", "rv1", "rg0", "rg1", "cq", "ck"):
                    project_rows(us, name)
                elif name == "krp":
                    project("krope", "krp")
                elif name.startswith("ra"):
                    h = int(name[2])
                    if h == 0:
                        pe.wait_ge(rk_ready, nth(l, rk_ready, 2))
                        pe.wait_ge(rq_ready, nth(l, rq_ready, 2))
                    p, j = slice(64 * (h % 2), 64 * (h % 2) + 64), h // 2
                    pe.wait_ge(drained[bank(f"ra{h}a")], draining(l, f"ra{h}a"))
                    o = psum[:, bank(f"ra{h}a"), :]
                    mm(o[:, 0:LS], rk[p, j, LP:LP + P], rq[p, j, LP:TOK], start=True, stop=True)
                    mm(o[:, LS:TOK], rk[p, j, 0:P], rq[p, j, 0:P], start=True, stop=True).then_inc(filled[bank(f"ra{h}a")], 1)
                    pe.wait_ge(drained[bank(f"ra{h}b")], draining(l, f"ra{h}b"))
                    o = psum[:, bank(f"ra{h}b"), :]
                    mm(o[:, 0:LS], rk[p, j, LP + P:TOK], rq[p, j, LP:TOK], start=True, stop=True).then_inc(filled[bank(f"ra{h}b")], 1)
                elif name.startswith("ro"):
                    h = int(name[2])
                    if h == 0:
                        pe.wait_ge(rv_ready, nth(l, rv_ready, 6))
                        pe.wait_ge(rqd_ready, nth(l, rqd_ready, 1))
                    pe.wait_ge(AT_ready, nth(l, AT_ready, h + 1))
                    p, j = slice(64 * (h % 2), 64 * (h % 2) + 64), h // 2
                    A = AT[:, h % 2, :]
                    v = [rv[:, t, h * DV:(h + 1) * DV] for t in range(NT)]
                    s0 = [part(x).rearrange("p (a b) -> p a b", a=2)[p, j, :] for x in ("s0f", "s0b")]
                    pe.wait_ge(drained[bank(f"ro{h}")], draining(l, f"ro{h}"))
                    o = psum[:, bank(f"ro{h}"), :]
                    mm(o[:, 0:P], A[:, LS:TOK], v[0], start=True, stop=True)
                    for t in range(2):
                        oc = o[:, (1 + t) * P:(2 + t) * P]
                        mm(oc, A[:, t * P:(t + 1) * P], v[1], start=True, stop=False)
                        mm(oc, A[:, TOK + t * P:TOK + (t + 1) * P], v[2], start=False, stop=False)
                        mm(oc, rqd[p, 0, j, t * P:(t + 1) * P], s0[0], start=False, stop=False)
                        i = mm(oc, rqd[p, 1, j, t * P:(t + 1) * P], s0[1], start=False, stop=True)
                    i.then_inc(filled[bank(f"ro{h}")], 1)
                elif name == "kr":
                    turn_rows("kr", [rk[:, j, 0:P] for j in range(2)])
                elif name == "rs":
                    pe.wait_ge(kd_ready, nth(l, kd_ready, 1))
                    for x in range(2):
                        pe.wait_ge(drained[bank("rs" + "fb"[x])], draining(l, "rs" + "fb"[x]))
                        o = psum[:, bank("rs" + "fb"[x]), :]
                        for h in range(HEADS):
                            i = mm(o[0:64, h * DV:(h + 1) * DV], kd[:, x, h, :], rv[:, 0, h * DV:(h + 1) * DV],
                                   start=True, stop=True)
                        i.then_inc(filled[bank("rs" + "fb"[x])], 1)
                elif name == "qkrot":
                    pe.wait_ge(qB_raw, nth(l, qB_raw, 2))
                    pe.wait_ge(kB_raw, nth(l, kB_raw, 1))
                    pe.wait_ge(drained[bank("pq")], draining(l, "pq"))
                    o = psum[:, bank("pq"), :]
                    for j in range(2):
                        i = mm(o[:, j * LS:(j + 1) * LS], const("perm_b"), qB[:, j, LP:TOK], start=True, stop=True)
                    i.then_inc(filled[bank("pq")], 1)
                    pe.wait_ge(drained[bank("pk")], draining(l, "pk"))
                    mm(psum[:, bank("pk"), :][:, 0:LS], const("perm_b"), kB[:, LP:TOK], start=True, stop=True).then_inc(filled[bank("pk")], 1)
                elif name == "kBo":
                    turn_rows("kBo", [kB[:, 0:P]])
                elif name == "dT":
                    pe.wait_ge(dtok_ready, nth(l, dtok_ready, 1))
                    for j in range(2):
                        turn_rows(f"cqT{j}", [dtok[:, t, j * P:(j + 1) * P] for t in range(NT)])
                    turn_rows("ckT", [dtok[:, t, 256:384] for t in range(NT)])
                    pe.wait_ge(krr_ready, nth(l, krr_ready, 1))
                    turn_rows("krO", [krr[:, 0:P]])
                elif name == "qD":
                    pe.wait_ge(dT_ready, nth(l, dT_ready, 3))
                    for h in range(HEADS):
                        pe.wait_ge(drained[bank(f"qD{h}")], draining(l, f"qD{h}"))
                        o = psum[:, bank(f"qD{h}"), :]
                        for k in range(2):
                            i = mm(o[0:QK, 0:TOK], uq[:, k, h * QK:(h + 1) * QK], cqT[:, k, :],
                                   start=k == 0, stop=k == 1)
                        i.then_inc(filled[bank(f"qD{h}")], 1)
                elif name == "rK":
                    pe.wait_ge(krr_ready, nth(l, krr_ready, 1))
                    pe.wait_ge(drained[bank("rK")], draining(l, "rK"))
                    o = psum[:, bank("rK"), :]
                    settle(pe)
                    mm(o[NOPE:QK, 0:LS], const("perm_d")[NOPE:QK, :], krr[NOPE:QK, LP:TOK],
                            start=True, stop=True).then_inc(filled[bank("rK")], 1)
                elif name == "kD":
                    for h in range(HEADS):
                        pe.wait_ge(drained[bank(f"kD{h}")], draining(l, f"kD{h}"))
                        o = psum[:, bank(f"kD{h}"), :]
                        w = ukv[:, h, 0:NOPE]
                        mm(o[0:NOPE, 0:TOK], w, ckvT, start=True, stop=True)
                        mm(o[0:NOPE, TOK:512], w, part("ctx_ckv"), start=True, stop=True).then_inc(filled[bank(f"kD{h}")], 1)
                elif name == "vD":
                    for x in range(2):
                        pe.wait_ge(drained[bank(f"vD{x}")], draining(l, f"vD{x}"))
                        o = psum[:, bank(f"vD{x}"), :]
                        for y in range(2):
                            kt = 2 * x + y
                            src = part("ctx_ckv") if kt == 3 else ckvT[:, kt * P:(kt + 1) * P]
                            i = mm(o[:, y * 256:(y + 1) * 256], src, ukv[:, :, NOPE:NOPE + MV], start=True, stop=True)
                        i.then_inc(filled[bank(f"vD{x}")], 1)
                elif name == "rD":
                    pe.wait_ge(qD_ready, nth(l, qD_ready, 4))
                    for x in range(2):
                        pe.wait_ge(drained[bank(f"rD{x}")], draining(l, f"rD{x}"))
                        o = psum[:, bank(f"rD{x}"), :]
                        settle(pe)
                        for y in range(2):
                            i = mm(o[NOPE:QK, y * LS:(y + 1) * LS], const("perm_d")[NOPE:QK, :],
                                   qD[NOPE:QK, 2 * x + y, LP:TOK], start=True, stop=True)
                        i.then_inc(filled[bank(f"rD{x}")], 1)
                elif name[:2] in ("sB", "sD"):
                    n, t = name[1], int(name[2])
                    if name == "sB0":
                        pe.wait_ge(qkB_ready, nth(l, qkB_ready, 1))
                        pe.wait_ge(vB_ready, nth(l, vB_ready, NT))
                    if name == "sD0":
                        pe.wait_ge(qrot_ready, nth(l, qrot_ready, 2))
                        pe.wait_ge(kD_nope, nth(l, kD_nope, 4))
                        pe.wait_ge(kD_rope, nth(l, kD_rope, 1))
                        pe.wait_ge(vD_ready, nth(l, vD_ready, 2))
                    attend_scores(n, t)
                elif name[:2] in ("pB", "pD"):
                    attend_turn(name[1], int(name[2]))
                elif name[:2] in ("oB", "oD"):
                    attend_out(name[1], int(name[2]))
                elif name == "ycT":
                    pe.wait_ge(yc_ready, nth(l, yc_ready, 4))
                    for k in range(4):
                        turn_rows(f"ycT{k}", [rg[:, t, k * P:(k + 1) * P] for t in range(NT)])
                elif name.startswith("gate"):
                    do_gate(int(name[4]), int(name[5]))
                elif name.startswith("br"):
                    d = int(name[2])
                    if d == 0:
                        pe.wait_ge(ya_ready, nth(l, ya_ready, 1))
                        pe.wait_ge(yb_ready, nth(l, yb_ready, 3))
                        pe.wait_ge(o_ready, nth(l, o_ready, 4))
                        pe.wait_ge(yd_ready, nth(l, yd_ready, 3))
                    pe.wait_ge(slot_loaded[slot_of(f"br{d}a")], loading(l, f"br{d}a"))
                    pe.wait_ge(slot_loaded[slot_of(f"br{d}b")], loading(l, f"br{d}b"))
                    wa, wb = ring[:, slot_of(f"br{d}a"), :, :], ring[:, slot_of(f"br{d}b"), :, :]
                    src = [yaT[:, 0, :], yaT[:, 1, :], ybT[:, 0, :], ybT[:, 1, :],
                           ycT[:, 0, :], ycT[:, 1, :], ycT[:, 2, :], ycT[:, 3, :], ydT[:, 0, :], ydT[:, 1, :]]
                    at = 0
                    for b, n in enumerate((2, 2, 4, 2)):
                        pe.wait_ge(drained[bank(f"br{d}{b}")], draining(l, f"br{d}{b}"))
                        o = psum[:, bank(f"br{d}{b}"), :]
                        for k in range(n):
                            w = (wa if at < 5 else wb)[:, at % 5, :]
                            i = mm(o[:, 0:TOK], w, src[at], start=k == 0, stop=k == n - 1)
                            at += 1
                        i.then_inc(filled[bank(f"br{d}{b}")], 1)
                elif name == "g1":
                    rows_of("g1", 16, 3 * DT // ADA_UNITS)
                elif name == "g2":
                    rows_of("g2", 40, ADA_BLOCKS)
                elif name == "out":
                    pe.wait_ge(merged_ready, nth(l, merged_ready, 8))
                    for j in js:
                        pe.wait_ge(drained[bank(j)], draining(l, j))
                        psum[:, bank(j), :]
                    def out_product(k, t):
                        w = ring[:, slot_of(f"out{k}"), :, :].rearrange("p a b -> p (a b)")
                        for h in range(2):
                            i = mm(psum[:, bank(js[2 * t + h]), :], merged[:, k, t * P:(t + 1) * P],
                                   w[:, h * 512:(h + 1) * 512], start=k == 0, stop=k == DT - 1,
                                   skip_group_check=True)
                            if k == DT - 1:
                                i.then_inc(filled[bank(js[2 * t + h])], 1)
                        if k < DT - 1 and t == NT - 1:
                            i.then_inc(out_used, 1)

                    for k in range(DT - OUT_HELD):
                        pe.wait_ge(slot_loaded[slot_of(f"out{k}")], loading(l, f"out{k}"))
                        for t in range(NT):
                            out_product(k, t)
                    for k in range(DT - OUT_HELD, DT):
                        pe.wait_ge(slot_loaded[slot_of(f"out{k}")], loading(l, f"out{k}"))
                        out_product(k, 0)
                    for t in range(1, NT):
                        for k in range(DT - OUT_HELD, DT):
                            out_product(k, t)
                elif name == "rt":
                    pe.wait_ge(hT_even, nth(l, hT_even, 8))
                    pe.wait_ge(hT_odd, nth(l, hT_odd, 8))
                    pe.wait_ge(drained[bank("rt")], draining(l, "rt"))
                    o = psum[:, bank("rt"), :]
                    settle(pe)
                    for k in range(DT):
                        r = slice(GROUP * (k % GROUPS), GROUP * (k % GROUPS + 1))
                        i = mm(o[r, 0:TOK], rw[:, k, :], h2[:, k, :], start=k < GROUPS, stop=k >= DT - GROUPS,
                               skip_group_check=True)
                    i.then_inc(filled[bank("rt")], 1)
                elif name == "rl":
                    pe.wait_ge(rt_rows_ready, nth(l, rt_rows_ready, 1))
                    pe.wait_ge(drained[bank("rl")], draining(l, "rl"))
                    o = psum[:, bank("rl"), :]
                    for t in range(NT):
                        i = mm(o[:, t * N_EXPERTS:(t + 1) * N_EXPERTS], rt_rows[:, t * P:(t + 1) * P],
                               const("expert_sel"), start=True, stop=True)
                    i.then_inc(filled[bank("rl")], 1)
                elif name == "cbT":
                    pass
                else:
                    raise AssertionError(name)

            def gate_up(e, j, first=False):
                f, b = j // 2, (GATE_BANK, UP_BANK)[j % 2]
                pe.wait_ge(w_lo_ready, l * (6 * N_EXPERTS) + e * 6 + SLOTS + j + 1)
                hi, lo = w_hi[:, j % SPLIT_SLOTS, :], w_lo[:, j % SPLIT_SLOTS, :]
                pe.wait_ge(drained[b], l * JOBS_LAYER[b] + e * 2 + JOBS_BEFORE[b] + f + 1)
                o = psum[:, b, 0:TOK]
                for k in range(DT):
                    c = slice(k * P, (k + 1) * P)
                    if first:
                        pe.wait_ge(h_split, nth(l, h_split, k + 1))
                    mm(o, hi[:, c], h_hi[:, k, :], start=k == 0, stop=False)
                    mm(o, hi[:, c], h_lo[:, k, :], start=False, stop=False)
                    i = mm(o, lo[:, c], h_hi[:, k, :], start=False, stop=k == DT - 1)
                i.then_inc(filled[b], 1)

            def down_tile(f, t):
                hi, lo = w_hi[:, (4 + f) % SPLIT_SLOTS, :], w_lo[:, (4 + f) % SPLIT_SLOTS, :]
                a_hi, a_lo = hid_hi[:, f, t * P:(t + 1) * P], hid_lo[:, f, t * P:(t + 1) * P]
                for h in range(2):
                    o, c = psum[:, SUM_BANK + 2 * t + h, :], slice(h * 512, (h + 1) * 512)
                    mm(o, a_hi, hi[:, c], start=False, stop=False, skip_group_check=True)
                    mm(o, a_hi, lo[:, c], start=False, stop=False, skip_group_check=True)
                    i = mm(o, a_lo, hi[:, c], start=False, stop=False, skip_group_check=True)
                return i

            def down(e, f):
                pe.wait_ge(w_lo_ready, l * (6 * N_EXPERTS) + e * 6 + SLOTS + 4 + f + 1)
                pe.wait_ge(hid_ready, l * 32 + e * 2 + f + 1)
                for t in range(NT):
                    i = down_tile(f, t)
                i.then_inc(down_used, 1)

            def close_tile(t):
                for b in (SUM_BANK + 2 * t, SUM_BANK + 2 * t + 1):
                    mm(psum[:, b, :], zeros[:, 0:P], zeros[:, :], start=False, stop=True,
                       skip_group_check=True).then_inc(filled[b], 1)

            gate_up(0, 0, first=True)
            gate_up(0, 1)
            gate_up(0, 2)
            pe.wait_ge(comb_ready, nth(l, comb_ready, 1))
            turn_rows("cbT", [comb[:, t, :] for t in range(NT)])
            gate_up(0, 3)
            for b in range(SUM_BANK, BANKS):
                pe.wait_ge(drained[b], l * JOBS_LAYER[b] + JOBS_BEFORE[b] + 1)
                mm(psum[:, b, :], zeros[:, 0:P], zeros[:, :], start=True, stop=False, skip_group_check=True)
            down(0, 0)
            down(0, 1)
            with pe.Fori(1, N_EXPERTS - 1) as e:
                for j in range(4):
                    gate_up(e, j)
                down(e, 0)
                down(e, 1)
            last = N_EXPERTS - 1
            for j in range(4):
                gate_up(last, j)
            for f in range(2):
                pe.wait_ge(w_lo_ready, l * (6 * N_EXPERTS) + last * 6 + SLOTS + 4 + f + 1)
                pe.wait_ge(hid_ready, l * 32 + last * 2 + f + 1)
                down_tile(f, 0)
            close_tile(0)
            for t in range(1, NT):
                for f in range(2):
                    i = down_tile(f, t)
                    if t == NT - 1:
                        i.then_inc(down_used, 1)
                close_tile(t)
            layer.close()


        @block.gpsimd
        def _(pool):
            nc.gpsimd.memset(zeros[:], 0.0).then_inc(zeros_ready, 1)
            pool.wait_ge(cst_ready, 80)
            layer = ExitStack()
            l = layer.enter_context(pool.Fori(0, DEPTH))

            def product_s(order):
                pool.wait_ge(U_ready, nth(l, U_ready, 3 * order + 3))
                pool.wait_ge(K_ready, nth(l, K_ready, 6))
                if order == 1:
                    pool.wait_ge(filled[bank("yv1")], filling(l, "yv1"))
                    psum[:, bank("yv1"), :]
                o = slice(order * HYC, (order + 1) * HYC)
                nc.gpsimd.tensor_tensor(Ys, U[:, :, 0, :], Ks[:, :, o], ALU.mult)
                nc.gpsimd.tensor_tensor(hyB, U[:, :, 1, :], Kc[:, :, o], ALU.mult)
                pool.drain()
                nc.gpsimd.tensor_tensor(Ys, Ys, hyB, ALU.add).then_inc(Ys_ready, 1)

            pool.wait_ge(layer_free, l + 1)
            settle(pool)
            pool.dma_start(x_dram, X[:]).then_inc(x_stored, 16)
            pool.dma_start(w3[0:HY_FFN, :], hy_w3[l]).then_inc(rows_ready, 16)
            pool.dma_start(hydec, hy_decay).then_inc(rows_ready, 16)
            pool.dma_start(dst, dist).then_inc(rows_ready, 16)
            for name, us, js in stages():
                if name == "U0":
                    product_s(0)
                elif name == "U1":
                    product_s(1)
                elif name == "kBo":
                    pool.wait_ge(kout_ready, nth(l, kout_ready, 1))
                    settle(pool)
                    pool.dma_start(new_k[l], kout).then_inc(outs_stored, 16)
                elif name == "krp":
                    pool.wait_ge(vB_ready, nth(l, vB_ready, NT))
                    settle(pool)
                    pool.dma_start(new_v[l], vB[:, 0, :]).then_inc(outs_stored, 16)
                elif name == "rs":
                    pool.wait_ge(st_ready, nth(l, st_ready, 2))
                    settle(pool)
                    pool.dma_start(new_rf[l].rearrange("h k v -> k h v"),
                                   st_out[:, 0, :].rearrange("k (h v) -> k h v", h=HEADS)).then_inc(outs_stored, 16)
                    pool.dma_start(new_rb[l].rearrange("h k v -> k h v"),
                                   st_out[:, 1, :].rearrange("k (h v) -> k h v", h=HEADS)).then_inc(outs_stored, 16)
                elif name == "dT":
                    pool.wait_ge(dtok_ready, nth(l, dtok_ready, 1))
                    settle(pool)
                    pool.dma_start(new_ckv[l], dtok[:, 0, 256:384]).then_inc(outs_stored, 16)
                    pool.wait_ge(kro_ready, nth(l, kro_ready, 1))
                    settle(pool)
                    pool.dma_start(new_krope[l], dtok[:, 0, 384:416]).then_inc(outs_stored, 16)
            wait_read(pool, l, SPLIT_UNITS[-1])
            pool.wait_ge(x_stored, nth(l, x_stored, 16))
            settle(pool)
            pool.dma_start(X[:], x_dram).then_inc(x_loaded, 16)
            pool.wait_ge(merged_ready, nth(l, merged_ready, 8))
            settle(pool)
            pool.dma_start(lnr, ln_rows[l]).then_inc(lnr_ready, 16)
            pool.wait_ge(combT_ready, nth(l, combT_ready, 1))
            settle(pool)
            pool.dma_start(comb_dram, combT[0:N_EXPERTS, :]).then_inc(comb_stored, 16)
            pool.wait_ge(comb_stored, nth(l, comb_stored, 16))
            settle(pool)
            for i in range(2):
                pool.dma_start(cb[:, i, :], comb_dram[i:i + 1, :].to_broadcast([P, TOK])).then_inc(cb_ready[i], 16)
            with pool.Fori(1, N_EXPERTS // 2) as it:
                for i in range(2):
                    pool.wait_ge(hid_ready, l * 32 + it * 4 + 2 * i - 2)
                    settle(pool)
                    pool.dma_start(cb[:, i, :], comb_rows[it, i].to_broadcast([P, TOK])).then_inc(cb_ready[i], 16)
            layer.close()

        @block.scalar
        def _(act):
            F = nc.scalar.activation
            act.wait_ge(cst_ready, 80)
            F(condS[:], condS[:], ACT.Silu).then_inc(cond_ready, 1)
            layer = ExitStack()
            l = None
            var_turn = [NT]

            def rsqrt(a, b, value):
                if value is not None:
                    act.wait_ge(var_ready, value)
                F(rstd[:, a:b], mv[:, a:b, 1], ACT.Ln)
                act.drain()
                return F(rstd[:, a:b], rstd[:, a:b], ACT.Exp, scale=-0.5)

            def next_var():
                var_turn[0] += 1
                return nth(l, var_ready, var_turn[0])

            def plain_norm(xn, t, value):
                rsqrt(NT + t, NT + t + 1, value)
                act.drain()
                F(nmean[:, t, 1:2], nmean[:, t, 0:1], ACT.Identity, scale=rstd[:, NT + t:NT + t + 1])
                act.drain()
                F(xn[:, t, :], X[:, t, :], ACT.Identity, scale=rstd[:, NT + t:NT + t + 1], bias=nmean[:, t, 1:2])

            def norms(xn):
                rsqrt(0, 1, next_var()).then_inc(rstd_ready, 1)
                rsqrt(1, 2, next_var()).then_inc(rstd_ready, 1)
                plain_norm(xn, 0, next_var())
                rsqrt(2, 3, next_var()).then_inc(rstd_ready, 1)
                plain_norm(xn, 1, next_var())
                plain_norm(xn, 2, next_var())
                act.drain().then_inc(xn_ready, 1)

            def take_gate(d, b):
                if d >= 4:
                    act.wait_ge(merged_ready, nth(l, merged_ready, d - 3))
                act.wait_ge(filled[bank(f"gate{d}{b}")], filling(l, f"gate{d}{b}"))
                F(gates[:, 4 * (d % 4) + b, :], psum[:, bank(f"gate{d}{b}"), 0:TOK], ACT.Sigmoid).then_inc(drained[bank(f"gate{d}{b}")], 1)
                act.drain().then_inc(gate_ready, 1)

            def high_part(e, j, layer_first=False):
                s = MOE_SLOT[j]
                act.wait_ge(slot_loaded[s], l * (16 * UNITS_LAYER[s]) + e * 16 + 16 * (UNITS_BEFORE[s] + 1))
                if layer_first:
                    pass
                elif j in (1, 2):
                    act.wait_ge(down_used, l * 32 + e * 2 + j)
                else:
                    b, n = {0: (UP_BANK, 0), 3: (GATE_BANK, 1), 4: (UP_BANK, 1), 5: (GATE_BANK, 2)}[j]
                    act.wait_ge(filled[b], l * JOBS_LAYER[b] + e * 2 + JOBS_BEFORE[b] + n + 1)
                F(w_hi[:, j % SPLIT_SLOTS, :], ring[:, s, :, :].rearrange("p a b -> p (a b)"), ACT.Copy)
                act.drain().then_inc(w_hi_ready, 1)

            def silu_gate(e, f):
                b = GATE_BANK
                act.wait_ge(filled[b], l * JOBS_LAYER[b] + e * 2 + JOBS_BEFORE[b] + f + 2)
                F(sg[:, f, :], psum[:, b, 0:TOK], ACT.Silu).then_inc(drained[b], 1)
                act.drain().then_inc(silu_ready, 1)

            for t in range(NT):
                plain_norm(xn1, t, t + 1)
            act.drain().then_inc(xn_ready, 1)
            l = layer.enter_context(act.Fori(0, DEPTH))
            def high_of_unit(u):
                n = SPLIT_UNITS.index(u)
                act.wait_ge(slot_loaded[slot_of(u)], loading(l, u))
                if n >= 2:
                    wait_read(act, l, SPLIT_UNITS[n - 2])
                F(u_hi[:, n % 2, :], ring[:, slot_of(u), :, :].rearrange("p a b -> p (a b)"), ACT.Copy)
                act.drain().then_inc(u_hi_ready, 1)

            for name, us, js in stages():
                for u in SPLIT_AT.get(name, []):
                    high_of_unit(u)
                if name[0] == "a":
                    n = int(name[1:])
                    if n in (ADA_FIRST, ADA_FIRST + 1):
                        act.wait_ge(Yc_ready, nth(l, Yc_ready, 2))
                        act.wait_ge(Ys_ready, nth(l, Ys_ready, 2))
                    elif n > ADA_FIRST:
                        act.wait_ge(filled[bank(f"m{n - 2}")], filling(l, f"m{n - 2}"))
                        psum[:, bank(f"m{n - 2}"), :]
                    act.wait_ge(filled[bank(name)], filling(l, name))
                    F(mod_rows[n], psum[:, bank(name), 0:ADA_UNITS * P], ACT.Copy).then_inc(drained[bank(name)], 1)
                    act.drain().then_inc(mod_rows_ready, 1)
                elif name in ("hT", "h2T"):
                    act.wait_ge(mod_ready, nth(l, mod_ready, ADA_FIRST if name == "hT" else ADA_BLOCKS))
                    s, sc = (0, 8) if name == "hT" else (24, 32)
                    for d in range(1, DT, 2):
                        act.wait_ge(filled[bank(js[d])], filling(l, js[d]))
                        o = psum[:, bank(js[d]), :]
                        h = h32 if name == "hT" else h2
                        for c, (a, b) in enumerate(SEG):
                            i = F(h[:, d, a:b], o[:, a:b], ACT.Identity, scale=modT[:, sc + d, c:c + 1],
                                  bias=modT[:, s + d, c:c + 1])
                        i.then_inc(drained[bank(js[d])], 1)
                        act.drain().then_inc(hT_odd, 1)
                        act.wait_ge(hT_even, nth(l, hT_even, (0 if name == "hT" else 4) + d // 2 + 1))
                        for dd in (d - 1, d):
                            F(x_hi[:, dd, :], h[:, dd, :], ACT.Copy)
                            act.drain().then_inc(x_hi_ready, 1)
                elif name in ("fil1", "fil2"):
                    x = int(name[3]) - 1
                    act.wait_ge(arg_ready, nth(l, arg_ready, x + 1))
                    r = (fa, fb)[x][0:HY_FFN, :]
                    F(r, r, ACT.Sin).then_inc(sin_ready, 1)
                elif name == "K":
                    for j in js:
                        f = int(j[2])
                        act.wait_ge(x_split, nth(l, x_split, DT))
                        act.wait_ge(filled[bank(j)], filling(l, j))
                        F((Kc if j[1] == "c" else Ks)[:, f, :], psum[:, bank(j), :], ACT.Copy).then_inc(drained[bank(j)], 1)
                        act.drain().then_inc(K_ready, 1)
                elif name == "vT":
                    act.wait_ge(prm_ready, nth(l, prm_ready, 16))
                    F(lg[:], part("decay"), ACT.Sigmoid)
                    act.drain()
                    F(lg[:], lg[:], ACT.Ln)
                    act.drain()
                    act.wait_ge(rows_ready, nth(l, rows_ready, 48))
                    act.wait_ge(filled[bank("fil2")], filling(l, "fil2"))
                    psum[:, bank("fil2"), :]
                    for h in range(HEADS):
                        F(E[:, h, 0:2, :], dst[:, 0:2, :], ACT.Exp, scale=lg[:, 4 + h:5 + h])
                        F(E[:, h, 2:4, :], dst[:, 2:4, :], ACT.Exp, scale=lg[:, h:h + 1])
                    for j in range(2):
                        F(rqd[:, 0, j, :], const("i_plus_1"), ACT.Exp, scale=lg[:, 8 + j:9 + j])
                        F(rqd[:, 1, j, :], const("l_minus_i"), ACT.Exp, scale=lg[:, 10 + j:11 + j])
                    F(dkc[:, 0, :], lg[:, 0:4], ACT.Exp, scale=const("p_fwd"))
                    F(dkc[:, 1, :], lg[:, 4:8], ACT.Exp, scale=const("p_bwd")).then_inc(E_act, 1)
                elif name == "rk":
                    for j in range(2):
                        act.wait_ge(filled[bank(f"rk{j}")], filling(l, f"rk{j}"))
                        F(rk[:, j, :], psum[:, bank(f"rk{j}"), 0:TOK], ACT.Copy, scale=64.0 ** -0.5).then_inc(drained[bank(f"rk{j}")], 1)
                        act.drain().then_inc(rk_ready, 1)
                elif name == "rq":
                    for j in range(2):
                        act.wait_ge(filled[bank(f"rq{j}")], filling(l, f"rq{j}"))
                        F(rq[:, j, :], psum[:, bank(f"rq{j}"), 0:TOK], ACT.Copy).then_inc(drained[bank(f"rq{j}")], 1)
                        act.drain().then_inc(rq_ready, 1)
                elif name in ("rv0", "rv1"):
                    if name == "rv0":
                        act.wait_ge(layer_free, l + 1)
                    c = 256 * int(name[2])
                    for t in range(NT):
                        act.wait_ge(filled[bank(f"{name}{t}")], filling(l, f"{name}{t}"))
                        F(rv[:, t, c:c + 256], psum[:, bank(f"{name}{t}"), 0:256], ACT.Copy).then_inc(drained[bank(f"{name}{t}")], 1)
                        act.drain().then_inc(rv_ready, 1)
                elif name in ("rg0", "rg1"):
                    c = 256 * int(name[2])
                    for t in range(NT):
                        act.wait_ge(filled[bank(f"{name}{t}")], filling(l, f"{name}{t}"))
                        F(rg[:, t, c:c + 256], psum[:, bank(f"{name}{t}"), 0:256], ACT.Silu).then_inc(drained[bank(f"{name}{t}")], 1)
                        act.drain().then_inc(rg_ready, 1)
                elif name in ("U0", "U1"):
                    for f in range(FT):
                        if name == "U1" and f == 0:
                            act.wait_ge(Yc_ready, nth(l, Yc_ready, 1))
                            act.wait_ge(Ys_ready, nth(l, Ys_ready, 1))
                        act.wait_ge(filled[bank(f"{name}{f}")], filling(l, f"{name}{f}"))
                        F(U[:, f, :, :].rearrange("p a b -> p (a b)"), psum[:, bank(f"{name}{f}"), :], ACT.Copy).then_inc(drained[bank(f"{name}{f}")], 1)
                        act.drain().then_inc(U_ready, 1)
                elif name == "wq":
                    for j in range(2):
                        act.wait_ge(filled[bank(f"wq{j}")], filling(l, f"wq{j}"))
                        F(qB[:, j, :], psum[:, bank(f"wq{j}"), 0:TOK], ACT.Copy).then_inc(drained[bank(f"wq{j}")], 1)
                        act.drain().then_inc(qB_raw, 1)
                elif name == "wk":
                    act.wait_ge(filled[bank("wk")], filling(l, "wk"))
                    F(kB[:], psum[:, bank("wk"), 0:TOK], ACT.Copy).then_inc(drained[bank("wk")], 1)
                    act.drain().then_inc(kB_raw, 1)
                elif name.startswith("gate"):
                    take_gate(int(name[4]), int(name[5]))
                elif name.startswith("ro"):
                    rsqrt(0, NT, next_var()).then_inc(rstd_ready, 1)
                elif name == "rs":
                    for x in range(2):
                        act.wait_ge(filled[bank(js[x])], filling(l, js[x]))
                        F(st_out[:, x, :], psum[:, bank(js[x]), :][0:64, :], ACT.Copy).then_inc(drained[bank(js[x])], 1)
                        act.drain().then_inc(st_ready, 1)
                elif name[:2] in ("sB", "sD"):
                    k = (0 if name[1] == "B" else 3) + int(name[2])
                    scale = (WIN_HD if name[1] == "B" else QK) ** -0.5
                    nk = P if name[2] == "0" else TOK
                    act.wait_ge(smax_ready, nth(l, smax_ready, k + 1))
                    for h in range(HEADS):
                        F(S[:, h, 0:nk], psum[:, bank(js[h]), 0:nk], ACT.Exp, bias=sm[:, 0, h:h + 1], scale=scale,
                          accum_out=sm[:, 1, h:h + 1]).then_inc(drained[bank(js[h])], 1)
                    if name[1] == "B":
                        F(sm[:, 2, :], sm[:, 2, :], ACT.Exp)
                    act.drain().then_inc(exp_ready, 1)
                elif name[:2] in ("pB", "pD"):
                    n = P if name[2] == "0" else TOK
                    for h in (1, 3):
                        act.wait_ge(filled[bank(js[h])], filling(l, js[h]))
                        F(PT[:, h, 0:n], psum[:, bank(js[h]), :][:, 0:n], ACT.Copy).then_inc(drained[bank(js[h])], 1)
                        act.drain().then_inc(PT_ready, 1)
                    if name == "pB0":
                        act.wait_ge(dtok_raw, nth(l, dtok_raw, 3))
                        for t in range(NT):
                            F(sqj[:, 0:256], dtok[:, t, 0:256], ACT.Square, accum_out=mv[:, t, 1:2])
                            act.drain()
                            F(sqj[:, 0:128], dtok[:, t, 256:384], ACT.Square, accum_out=mv[:, 3 + t, 1:2])
                            act.drain()
                        F(mv[:, 0:3, 1], mv[:, 0:3, 1], ACT.Copy, scale=1.0 / 256, bias=RMS_EPS)
                        F(mv[:, 3:6, 1], mv[:, 3:6, 1], ACT.Copy, scale=1.0 / 128, bias=RMS_EPS)
                        act.drain()
                        rsqrt(0, 2 * NT, None).then_inc(rstd_ready, 1)
                elif name == "dT":
                    for j in range(2):
                        act.wait_ge(filled[bank(js[j])], filling(l, js[j]))
                        F(cqT[:, j, :], psum[:, bank(js[j]), :][:, 0:TOK], ACT.Identity, scale=part("q_norm")[:, j:j + 1]).then_inc(drained[bank(js[j])], 1)
                        act.drain().then_inc(dT_ready, 1)
                    act.wait_ge(filled[bank("ckT")], filling(l, "ckT"))
                    F(ckvT, psum[:, bank("ckT"), 0:TOK], ACT.Copy).then_inc(drained[bank("ckT")], 1)
                    act.drain().then_inc(dT_ready, 1)
                elif name == "qD":
                    for h in range(HEADS):
                        act.wait_ge(filled[bank(js[h])], filling(l, js[h]))
                        F(qD[0:QK, h, :], psum[:, bank(js[h]), :][0:QK, 0:TOK], ACT.Copy).then_inc(drained[bank(js[h])], 1)
                        act.drain().then_inc(qD_ready, 1)
                elif name == "kD":
                    for h in range(HEADS):
                        act.wait_ge(filled[bank(js[h])], filling(l, js[h]))
                        F(kD[0:NOPE, h, :], psum[:, bank(js[h]), :][0:NOPE, :], ACT.Copy).then_inc(drained[bank(js[h])], 1)
                        act.drain().then_inc(kD_nope, 1)
                elif name == "vD":
                    for x in range(2):
                        act.wait_ge(filled[bank(js[x])], filling(l, js[x]))
                        F(vD[:, 2 * x:2 * x + 2, :].rearrange("p a b -> p (a b)"), psum[:, bank(js[x]), :], ACT.Copy).then_inc(drained[bank(js[x])], 1)
                        act.drain().then_inc(vD_ready, 1)
                elif name == "ycT":
                    for k in range(4):
                        act.wait_ge(filled[bank(js[k])], filling(l, js[k]))
                        F(ycT[:, k, :], psum[:, bank(js[k]), :][:, 0:TOK], ACT.Copy).then_inc(drained[bank(js[k])], 1)
                        act.drain().then_inc(o_ready, 1)
                elif name == "out":
                    act.wait_ge(filled[bank("g111")], filling(l, "g111"))
                    psum[:, bank("g111"), :]
                    high_part(0, 0, layer_first=True)
                    high_part(0, 1, layer_first=True)
                    norms(xn2)
                    high_part(0, 2, layer_first=True)
                elif name in ("g1", "g2"):
                    out = g1bc if name == "g1" else g2bc
                    if name == "g2":
                        act.wait_ge(filled[bank("oD2")], filling(l, "oD2"))
                        psum[:, bank("oD2"), :]
                    else:
                        act.wait_ge(merged_ready, nth(l, merged_ready, 8))
                    for c in range(2):
                        for h in range(2):
                            act.wait_ge(filled[bank(f"{name}{c}{h}")], filling(l, f"{name}{c}{h}"))
                            F(out[:, c, h * 512:(h + 1) * 512], psum[:, bank(f"{name}{c}{h}"), :], ACT.Copy).then_inc(drained[bank(f"{name}{c}{h}")], 1)
                            act.drain().then_inc(g1_ready if name == "g1" else g2_ready, 1)
                elif name == "rt":
                    act.wait_ge(filled[bank("rt")], filling(l, "rt"))
                    F(rt_rows, psum[:, bank("rt"), 0:TOK], ACT.Copy).then_inc(drained[bank("rt")], 1)
                    act.drain().then_inc(rt_rows_ready, 1)
                elif name == "rl":
                    act.wait_ge(filled[bank("rl")], filling(l, "rl"))
                    F(scores.rearrange("p a b -> p (a b)"), psum[:, bank("rl"), 0:NT * N_EXPERTS], ACT.Sigmoid).then_inc(drained[bank("rl")], 1)
                    act.drain().then_inc(scores_ready, 1)
            silu_gate(0, 0)
            high_part(0, 3)
            high_part(0, 4)
            silu_gate(0, 1)
            high_part(0, 5)
            with act.Fori(1, N_EXPERTS) as e:
                high_part(e, 0)
                high_part(e, 1)
                high_part(e, 2)
                silu_gate(e, 0)
                high_part(e, 3)
                high_part(e, 4)
                silu_gate(e, 1)
                high_part(e, 5)
            norms(xn1)
            layer.close()

        @block.vector
        def _(dve):
            V = nc.vector
            dve.wait_ge(cst_ready, 80)
            layer = ExitStack()
            rs_turn = [0]


            def variance(t, row):
                for h in range(2):
                    V.bn_stats(stats[:, t, h, :], X[:, t, h * 512:(h + 1) * 512])
                dve.drain()
                V.bn_aggr(mv[:, row, :], stats[:, t, :, :].rearrange("p a b -> p (a b)"))
                dve.drain()
                V.tensor_scalar(mv[:, row, 1:2], mv[:, row, 1:2], LN_EPS, None, ALU.add)
                if row >= NT:
                    V.tensor_scalar(nmean[:, t, 0:1], mv[:, row, 0:1], -1.0, None, ALU.mult)
                dve.drain().then_inc(var_ready, 1)

            def sine_argument(job, bias, r, n):
                dve.wait_ge(filled[bank(job)], filling(l, job))
                o = psum[:, bank(job), :]
                V.tensor_scalar(r, o[0:HY_FFN, 0:TOK], bias, None, ALU.add).then_inc(drained[bank(job)], 1)
                dve.drain()
                V.tensor_scalar(n, r, 1.0 / (2.0 * math.pi), ROUND, ALU.mult, ALU.add)
                dve.drain()
                V.tensor_scalar(n, n, ROUND, None, ALU.subtract)
                dve.drain()
                V.scalar_tensor_tensor(out=r, in0=n, scalar=-TWO_PI_A, in1=r, op0=ALU.mult, op1=ALU.add)
                dve.drain()
                V.scalar_tensor_tensor(out=r, in0=n, scalar=-TWO_PI_B, in1=r, op0=ALU.mult, op1=ALU.add)
                dve.drain()
                V.tensor_scalar(r, r, PI_BELOW, -PI_BELOW, ALU.min, ALU.max)
                dve.drain().then_inc(arg_ready, 1)


            def product_c(order):
                dve.wait_ge(U_ready, nth(l, U_ready, 3 * order + 3))
                dve.wait_ge(K_ready, nth(l, K_ready, 6))
                o = slice(order * HYC, (order + 1) * HYC)
                V.tensor_tensor(Yc, U[:, :, 0, :], Kc[:, :, o], ALU.mult)
                V.tensor_tensor(hyA, U[:, :, 1, :], Ks[:, :, o], ALU.mult)
                dve.drain()
                V.tensor_tensor(Yc, Yc, hyA, ALU.subtract)
                dve.drain().then_inc(Yc_ready, 1)

            def scaled_sum(js, gbc, t):
                for h in range(2):
                    c = slice(h * 512, h * 512 + 512)
                    j = js[2 * t + h]
                    dve.wait_ge(filled[bank(j)], filling(l, j))
                    V.tensor_tensor(upd[:, h, :], psum[:, bank(j), :], gbc[:, min(t, 1), c],
                                    ALU.mult).then_inc(drained[bank(j)], 1)
                dve.drain()
                V.scalar_tensor_tensor(out=X[:, t, :], in0=X[:, t, :], scalar=ALPHA,
                                       in1=upd.rearrange("p a b -> p (a b)"), op0=ALU.mult, op1=ALU.add)
                dve.drain()

            def norm_rows(t, g_row):
                rs_turn[0] += 1
                dve.wait_ge(rstd_ready, nth(l, rstd_ready, rs_turn[0]))
                V.scalar_tensor_tensor(out=X[:, t, :], in0=X[:, t, :], scalar=mv[:, t, 0:1], in1=lnr[:, g_row, :],
                                       op0=ALU.subtract, op1=ALU.mult)
                dve.drain()
                V.scalar_tensor_tensor(out=X[:, t, :], in0=X[:, t, :], scalar=rstd[:, t:t + 1],
                                       in1=lnr[:, g_row + 1, :], op0=ALU.mult, op1=ALU.add)
                dve.drain()

            def update(js, gbc, g_row):
                scaled_sum(js, gbc, 0)
                variance(0, 0)
                scaled_sum(js, gbc, 1)
                variance(1, 1)
                norm_rows(0, g_row)
                variance(0, NT)
                scaled_sum(js, gbc, 2)
                variance(2, 2)
                norm_rows(1, g_row)
                variance(1, NT + 1)
                norm_rows(2, g_row)
                variance(2, NT + 2)

            def low_part(it, i, j):
                dve.wait_ge(w_hi_ready, l * (6 * N_EXPERTS) + it * 12 + 6 * i + j + 1)
                V.tensor_tensor(w_lo[:, j % SPLIT_SLOTS, :], ring[:, MOE_SLOT[j], :, :].rearrange("p a b -> p (a b)"),
                                w_hi[:, j % SPLIT_SLOTS, :].bitcast(F32), ALU.subtract)
                dve.drain().then_inc(w_lo_ready, 1)

            def hidden(it, i, f):
                b = UP_BANK
                n = 2 * i + f
                dve.wait_ge(filled[b], l * JOBS_LAYER[b] + it * 4 + JOBS_BEFORE[b] + n + 2)
                dve.wait_ge(silu_ready, l * 32 + it * 4 + n + 1)
                V.tensor_tensor(hid[:, f, :], psum[:, b, 0:TOK], sg[:, f, :], ALU.mult).then_inc(drained[b], 1)
                dve.drain()
                if f == 0:
                    dve.wait_ge(cb_ready[i], l * 128 + it * 16 + 16)
                V.tensor_tensor(hid[:, f, :], hid[:, f, :], cb[:, i, :], ALU.mult)
                dve.drain()
                V.tensor_copy(hid_hi[:, f, :], hid[:, f, :])
                dve.drain()
                V.tensor_tensor(hid_lo[:, f, :], hid[:, f, :], hid_hi[:, f, :].bitcast(F32), ALU.subtract)
                dve.drain().then_inc(hid_ready, 1)

            def second_expert(it):
                for j in range(4):
                    low_part(it, 1, j)
                hidden(it, 1, 0)
                low_part(it, 1, 4)
                low_part(it, 1, 5)
                hidden(it, 1, 1)

            for t in range(NT):
                variance(t, NT + t)
            l = layer.enter_context(dve.Fori(0, DEPTH))
            dve.wait_ge(prm_ready, nth(l, prm_ready, 16))
            def low_of_input(name, d):
                dve.wait_ge(x_hi_ready, nth(l, x_hi_ready, (0 if name == "hT" else DT) + d + 1))
                if name == "hT":
                    if d == 0:
                        dve.wait_ge(x_stored, nth(l, x_stored, 16))
                    V.tensor_tensor(x_lo[:, d, :], h32[:, d, :], x_hi[:, d, :].bitcast(F32), ALU.subtract)
                    dve.drain().then_inc(x_split, 1)
                else:
                    V.tensor_tensor(h_lo[:, d, :], h2[:, d, :], h_hi[:, d, :].bitcast(F32), ALU.subtract)
                    dve.drain().then_inc(h_split, 1)

            def low_of_unit(u):
                n = SPLIT_UNITS.index(u)
                dve.wait_ge(u_hi_ready, nth(l, u_hi_ready, n + 1))
                V.tensor_tensor(ring_lo[:, slot_of(u), :], ring[:, slot_of(u), :, :].rearrange("p a b -> p (a b)"),
                                u_hi[:, n % 2, :].bitcast(F32), ALU.subtract)
                dve.drain().then_inc(u_lo_ready, 1)

            for name, us, js in stages():
                if name != "hy":
                    for u in SPLIT_AT.get(name, []):
                        low_of_unit(u)
                if name[0] == "m":
                    n = int(name[1:])
                    at = ADA_UNITS * n
                    m = modT[:, at:at + ADA_UNITS, :]
                    bias = part("b_ada")[:, at:at + ADA_UNITS].rearrange("p (a b) -> p a b", b=1).to_broadcast(
                        [P, ADA_UNITS, 2])
                    o = psum[:, bank(name), 0:2 * ADA_UNITS].rearrange("p (a b) -> p a b", b=2)
                    dve.wait_ge(filled[bank(name)], filling(l, name))
                    if at // DT in (1, 4):
                        V.scalar_tensor_tensor(out=m, in0=o, scalar=1.0, in1=bias, op0=ALU.add,
                                               op1=ALU.add).then_inc(drained[bank(name)], 1)
                    else:
                        V.tensor_tensor(m, o, bias, ALU.add).then_inc(drained[bank(name)], 1)
                    dve.drain().then_inc(mod_ready, 1)
                elif name in ("hT", "h2T"):
                    s, sc = (0, 8) if name == "hT" else (24, 32)
                    for d in range(0, DT, 2):
                        dve.wait_ge(filled[bank(js[d])], filling(l, js[d]))
                        o = psum[:, bank(js[d]), :]
                        h = h32 if name == "hT" else h2
                        for c, (a, b) in enumerate(SEG):
                            i = V.tensor_scalar(h[:, d, a:b], o[:, a:b], modT[:, sc + d, c:c + 1],
                                                modT[:, s + d, c:c + 1], ALU.mult, ALU.add)
                        i.then_inc(drained[bank(js[d])], 1)
                        dve.drain().then_inc(hT_even, 1)
                        if d >= 2:
                            low_of_input(name, d - 2)
                            low_of_input(name, d - 1)
                    low_of_input(name, DT - 2)
                    low_of_input(name, DT - 1)
                elif name == "fil1":
                    sine_argument("fil1", part("hy_b1")[0:HY_FFN, :], fa[0:HY_FFN, :], fb[0:HY_FFN, :])
                elif name == "fil2":
                    dve.wait_ge(sin_ready, nth(l, sin_ready, 1))
                    sine_argument("fil2", part("hy_b2")[0:HY_FFN, :], fb[0:HY_FFN, :], fc[0:HY_FFN, :])
                elif name == "fil3":
                    dve.wait_ge(rows_ready, nth(l, rows_ready, 48))
                    for j in js:
                        t, o = int(j[4]), int(j[5])
                        dve.wait_ge(filled[bank(j)], filling(l, j))
                        V.tensor_tensor(ftmp, psum[:, bank(j), :], hydec[:, t, :], ALU.mult).then_inc(drained[bank(j)], 1)
                        dve.drain()
                        c = slice(o * HYC, (o + 1) * HYC)
                        V.tensor_tensor(hs[:, t, c], ftmp[:, 0:HYC], ftmp[:, HYC:512], ALU.add)
                        V.tensor_tensor(hd[:, t, c], ftmp[:, 0:HYC], ftmp[:, HYC:512], ALU.subtract)
                        dve.drain().then_inc(taps_ready, 1)
                elif name == "hy":
                    cw = part("conv_w").rearrange("p (a b) -> p a b", a=6)
                    for n in range(6):
                        if n < len(SPLIT_AT["hy"]):
                            low_of_unit(SPLIT_AT["hy"][n])
                        dve.wait_ge(filled[bank(js[n])], filling(l, js[n]))
                        o = psum[:, bank(js[n]), :]
                        z = zc[:, n, :]
                        V.tensor_scalar(z, o[:, 0:TOK], cw[:, n, 1:2], part("conv_b")[:, n:n + 1], ALU.mult, ALU.add)
                        dve.drain()
                        for a, b in SEG:
                            V.scalar_tensor_tensor(out=z[:, a + 1:b], in0=o[:, a:b - 1], scalar=cw[:, n, 0:1],
                                                   in1=z[:, a + 1:b], op0=ALU.mult, op1=ALU.add)
                        dve.drain()
                        for a, b in SEG:
                            i = V.scalar_tensor_tensor(out=z[:, a:b - 1], in0=o[:, a + 1:b], scalar=cw[:, n, 2:3],
                                                       in1=z[:, a:b - 1], op0=ALU.mult, op1=ALU.add)
                        i.then_inc(drained[bank(js[n])], 1)
                    dve.drain().then_inc(conv_ready, 1)
                elif name in ("vT", "uT"):
                    for t in range(NT):
                        dve.wait_ge(filled[bank(f"{name}{t}")], filling(l, f"{name}{t}"))
                        V.tensor_copy(vtok[:, t, :], psum[:, bank(f"{name}{t}"), 0:HYC]).then_inc(drained[bank(f"{name}{t}")], 1)
                        dve.drain().then_inc(vtok_ready, 1)
                elif name in ("rv1", "wq"):
                    if name == "rv1":
                        product_c(0)
                        dve.wait_ge(rq_ready, nth(l, rq_ready, 2))
                        dve.wait_ge(E_act, nth(l, E_act, 1))
                        for x in range(2):
                            V.tensor_tensor(rqd[:, x, :, :], rqd[:, x, :, :], rq[:, :, LP:TOK], ALU.mult)
                        dve.drain().then_inc(rqd_ready, 1)
                        dve.wait_ge(E_act, nth(l, E_act, 1))
                        for x in (1, 2):
                            V.tensor_tensor(E[:, :, x, :], E[:, :, x, :],
                                            dst[:, 3 + x:4 + x, :].to_broadcast([P, HEADS, P]), ALU.mult)
                        dve.drain()
                        V.tensor_tensor(E[:, :, 1, :], E[:, :, 1, :], E[:, :, 2, :], ALU.add)
                        dve.drain()
                        V.tensor_copy(E[:, :, 2, :], E[:, :, 1, :])
                        dve.drain().then_inc(E_ready, 1)
                elif name == "yv":
                    for c in range(2):
                        dve.wait_ge(filled[bank(f"yv{c}")], filling(l, f"yv{c}"))
                        V.scalar_tensor_tensor(out=zc[:, c, :], in0=zc[:, c, :], scalar=part("hy_bias")[:, c:c + 1],
                                               in1=psum[:, bank(f"yv{c}"), :][:, 0:TOK], op0=ALU.mult,
                                               op1=ALU.add).then_inc(drained[bank(f"yv{c}")], 1)
                    dve.drain()
                    V.tensor_tensor(zc[:, 0:2, :], zc[:, 0:2, :], zc[:, 2:4, :], ALU.mult)
                    dve.drain().then_inc(u_ready, 1)
                elif name == "U1":
                    product_c(1)
                elif name == "yu":
                    for c in range(2):
                        dve.wait_ge(filled[bank(f"yu{c}")], filling(l, f"yu{c}"))
                        V.scalar_tensor_tensor(out=zc[:, c, :], in0=zc[:, c, :], scalar=part("hy_bias")[:, 2 + c:3 + c],
                                               in1=psum[:, bank(f"yu{c}"), :][:, 0:TOK], op0=ALU.mult,
                                               op1=ALU.add).then_inc(drained[bank(f"yu{c}")], 1)
                    dve.drain()
                    V.tensor_tensor(yaT[:], zc[:, 0:2, :], zc[:, 4:6, :], ALU.mult)
                    dve.drain().then_inc(ya_ready, 1)
                elif name.startswith("ra"):
                    h = int(name[2])
                    A = AT[:, h % 2, :]
                    dve.wait_ge(filled[bank(f"ra{h}a")], filling(l, f"ra{h}a"))
                    o = psum[:, bank(f"ra{h}a"), :]
                    V.tensor_tensor(A[:, 0:LS], o[:, 0:LS], E[:, h, 2:4, :].rearrange("p a b -> p (a b)"), ALU.mult)
                    V.tensor_tensor(A[:, LS:TOK], o[:, LS:TOK], E[:, h, 2, :], ALU.mult).then_inc(drained[bank(f"ra{h}a")], 1)
                    dve.wait_ge(filled[bank(f"ra{h}b")], filling(l, f"ra{h}b"))
                    o = psum[:, bank(f"ra{h}b"), :]
                    V.tensor_tensor(A[:, TOK:640], o[:, 0:LS],
                                              E[:, h, 0:2, :].rearrange("p a b -> p (a b)"), ALU.mult).then_inc(drained[bank(f"ra{h}b")], 1)
                    dve.drain().then_inc(AT_ready, 1)
                elif name.startswith("ro"):
                    h = int(name[2])
                    dve.wait_ge(filled[bank(name)], filling(l, name))
                    o = psum[:, bank(name), :]
                    for t in range(NT):
                        V.bn_stats(stats[:, t, 0, :], o[:, t * P:(t + 1) * P])
                    dve.drain()
                    for t in range(NT):
                        V.bn_aggr(mv[:, t, :], stats[:, t, 0, :])
                    dve.drain()
                    V.tensor_scalar(mv[:, 0:NT, 1], mv[:, 0:NT, 1], LN_EPS, None, ALU.add)
                    dve.drain().then_inc(var_ready, 1)
                    dve.wait_ge(rg_ready, nth(l, rg_ready, 6))
                    for t in range(NT):
                        r = rg[:, t, h * DV:(h + 1) * DV]
                        i = V.scalar_tensor_tensor(out=r, in0=o[:, t * P:(t + 1) * P], scalar=mv[:, t, 0:1], in1=r,
                                                   op0=ALU.subtract, op1=ALU.mult)
                    i.then_inc(drained[bank(name)], 1)
                    rs_turn[0] += 1
                    dve.drain()
                    dve.wait_ge(rstd_ready, nth(l, rstd_ready, rs_turn[0]))
                    for t in range(NT):
                        r = rg[:, t, h * DV:(h + 1) * DV]
                        V.tensor_scalar(r, r, rstd[:, t:t + 1], None, ALU.mult)
                    dve.drain().then_inc(yc_ready, 1)
                elif name == "kr":
                    dve.wait_ge(filled[bank("kr")], filling(l, "kr"))
                    o = psum[:, bank("kr"), :][:, 0:256].rearrange("p (a b) -> p a b", a=HEADS)
                    for x in range(2):
                        i = V.tensor_tensor(kd[:, x, :, :], o,
                                            dkc[:, x, :].rearrange("p (a b) -> p a b", b=1).to_broadcast([P, HEADS, 64]),
                                            ALU.mult)
                    i.then_inc(drained[bank("kr")], 1)
                    dve.drain().then_inc(kd_ready, 1)
                elif name == "qkrot":
                    dve.wait_ge(filled[bank("pq")], filling(l, "pq"))
                    o = psum[:, bank("pq"), :]
                    sb_, cb_ = const("sin_b"), const("cos_b")
                    for j in range(2):
                        i = V.tensor_tensor(rt_tmp[:, j, :], o[:, j * LS:(j + 1) * LS], sb_, ALU.mult)
                        V.tensor_tensor(qB[:, j, LP:TOK], qB[:, j, LP:TOK], cb_, ALU.mult)
                    dve.drain()
                    dve.sem_inc(drained[bank("pq")], 1)
                    dve.wait_ge(filled[bank("pk")], filling(l, "pk"))
                    V.tensor_tensor(rt_tmp[:, 2, :], psum[:, bank("pk"), :][:, 0:LS], sb_, ALU.mult).then_inc(drained[bank("pk")], 1)
                    V.tensor_tensor(kB[:, LP:TOK], kB[:, LP:TOK], cb_, ALU.mult)
                    dve.drain()
                    V.tensor_tensor(qB[:, :, LP:TOK], qB[:, :, LP:TOK], rt_tmp[:, 0:2, :], ALU.add)
                    V.tensor_tensor(kB[:, LP:TOK], kB[:, LP:TOK], rt_tmp[:, 2, :], ALU.add)
                    dve.drain().then_inc(qkB_ready, 1)
                elif name == "kBo":
                    dve.wait_ge(filled[bank("kBo")], filling(l, "kBo"))
                    V.tensor_copy(kout, psum[:, bank("kBo"), 0:P]).then_inc(drained[bank("kBo")], 1)
                    dve.drain().then_inc(kout_ready, 1)
                elif name in ("cq", "ck"):
                    for t in range(NT):
                        dve.wait_ge(filled[bank(f"{name}{t}")], filling(l, f"{name}{t}"))
                        o = psum[:, bank(f"{name}{t}"), :]
                        if name == "cq":
                            V.tensor_copy(dtok[:, t, 0:256], o[:, 0:256]).then_inc(drained[bank(f"cq{t}")], 1)
                        else:
                            V.tensor_copy(vB[:, t, :], o[:, 0:P])
                            V.tensor_copy(dtok[:, t, 256:384], o[:, P:256]).then_inc(drained[bank(f"ck{t}")], 1)
                            dve.drain().then_inc(dtok_raw, 1)
                            dve.sem_inc(vB_ready, 1)
                elif name[:2] in ("sB", "sD"):
                    n, t = name[1], int(name[2])
                    nk = P if t == 0 else TOK
                    scale = (WIN_HD if n == "B" else QK) ** -0.5
                    for h in range(HEADS):
                        dve.wait_ge(filled[bank(js[h])], filling(l, js[h]))
                        o = psum[:, bank(js[h]), :]
                        if n == "B" and t:
                            c = slice(P, 2 * P) if t == 1 else slice(0, P)
                            V.tensor_tensor(o[:, c], o[:, c], const("mask")[:, (t - 1) * P:t * P], ALU.add)
                            dve.drain()
                        V.tensor_reduce(sm[:, 0, h:h + 1], o[:, 0:nk], AX.X, ALU.max)
                    dve.drain()
                    if n == "B":
                        V.tensor_scalar(sm[:, 0, :], sm[:, 0, :], scale, None, ALU.mult)
                        dve.drain()
                        V.tensor_tensor(sm[:, 0, :], sm[:, 0, :], part("sink"), ALU.max)
                        dve.drain()
                        V.tensor_tensor(sm[:, 2, :], part("sink"), sm[:, 0, :], ALU.subtract)
                        dve.drain()
                    V.tensor_scalar(sm[:, 0, :], sm[:, 0, :], -1.0 if n == "B" else -scale, None, ALU.mult)
                    dve.drain().then_inc(smax_ready, 1)
                    k = (0 if n == "B" else 3) + t
                    dve.wait_ge(exp_ready, nth(l, exp_ready, k + 1))
                    if n == "B":
                        V.tensor_tensor(sm[:, 1, :], sm[:, 1, :], sm[:, 2, :], ALU.add)
                        dve.drain()
                    V.reciprocal(sm[:, 3, :], sm[:, 1, :])
                    dve.drain()
                    for h in range(HEADS):
                        V.tensor_scalar(S[:, h, 0:nk], S[:, h, 0:nk], sm[:, 3, h:h + 1], None, ALU.mult)
                    dve.drain().then_inc(prob_ready, 1)
                    if name == "sB1":
                        rs_turn[0] += 1
                        dve.wait_ge(rstd_ready, nth(l, rstd_ready, rs_turn[0]))
                        for t in range(NT):
                            V.tensor_scalar(dtok[:, t, 0:256], dtok[:, t, 0:256], rstd[:, t:t + 1], None, ALU.mult)
                            V.scalar_tensor_tensor(out=dtok[:, t, 256:384], in0=dtok[:, t, 256:384],
                                                   scalar=rstd[:, 3 + t:4 + t], in1=part("kv_norm"),
                                                   op0=ALU.mult, op1=ALU.mult)
                        dve.drain().then_inc(dtok_ready, 1)
                elif name[:2] in ("pB", "pD"):
                    w = P if name[2] == "0" else TOK
                    for h in (0, 2):
                        dve.wait_ge(filled[bank(js[h])], filling(l, js[h]))
                        V.tensor_copy(PT[:, h, 0:w], psum[:, bank(js[h]), :][:, 0:w]).then_inc(drained[bank(js[h])], 1)
                        dve.drain().then_inc(PT_ready, 1)
                elif name[:2] in ("oB", "oD"):
                    t = int(name[2])
                    out, ready = (ybT, yb_ready) if name[1] == "B" else (ydT, yd_ready)
                    dve.wait_ge(filled[bank(name)], filling(l, name))
                    V.tensor_copy(out[:, :, t * P:(t + 1) * P], psum[:, bank(name), 0:256].rearrange("p (a b) -> p a b", a=2)).then_inc(drained[bank(name)], 1)
                    dve.drain().then_inc(ready, 1)
                elif name == "krp":
                    dve.wait_ge(filled[bank("krp")], filling(l, "krp"))
                    V.tensor_copy(krr, psum[:, bank("krp"), 0:TOK]).then_inc(drained[bank("krp")], 1)
                    dve.drain().then_inc(krr_ready, 1)
                elif name == "dT":
                    dve.wait_ge(filled[bank("krO")], filling(l, "krO"))
                    V.tensor_copy(dtok[:, 0, 384:416], psum[:, bank("krO"), NOPE:QK]).then_inc(drained[bank("krO")], 1)
                    dve.drain().then_inc(kro_ready, 1)
                elif name == "rK":
                    r = slice(NOPE, QK)
                    dve.wait_ge(filled[bank("rK")], filling(l, "rK"))
                    V.tensor_tensor(rt_tmp[r, 0, :], psum[:, bank("rK"), :][r, 0:LS], const("sin_d")[r, :],
                                              ALU.mult).then_inc(drained[bank("rK")], 1)
                    V.tensor_tensor(krr[r, LP:TOK], krr[r, LP:TOK], const("cos_d")[r, :], ALU.mult)
                    dve.drain()
                    V.tensor_tensor(krr[r, LP:TOK], krr[r, LP:TOK], rt_tmp[r, 0, :], ALU.add)
                    dve.drain()
                    for h in range(HEADS):
                        V.tensor_copy(kD[r, h, 0:TOK], krr[r, :])
                        V.tensor_copy(kD[r, h, TOK:512], part("ctx_kr")[r, :])
                    dve.drain().then_inc(kD_rope, 1)
                elif name == "rD":
                    r = slice(NOPE, QK)
                    for x in range(2):
                        dve.wait_ge(filled[bank(js[x])], filling(l, js[x]))
                        o = psum[:, bank(js[x]), :]
                        for y in range(2):
                            i = V.tensor_tensor(rt_tmp[r, y, :], o[r, y * LS:(y + 1) * LS], const("sin_d")[r, :], ALU.mult)
                        i.then_inc(drained[bank(js[x])], 1)
                        for y in range(2):
                            q = qD[r, 2 * x + y, LP:TOK]
                            V.tensor_tensor(q, q, const("cos_d")[r, :], ALU.mult)
                        dve.drain()
                        q = qD[r, 2 * x:2 * x + 2, LP:TOK]
                        V.tensor_tensor(q, q, rt_tmp[r, 0:2, :], ALU.add)
                        dve.drain().then_inc(qrot_ready, 1)
                elif name.startswith("br"):
                    d = int(name[2])
                    if d == 0:
                        dve.wait_ge(outs_stored, nth(l, outs_stored, 6 * 16))
                    dve.wait_ge(gate_ready, nth(l, gate_ready, 4 * d + 4))
                    for b in range(4):
                        g = gates[:, 4 * (d % 4) + b, :]
                        out = merged[:, d, :] if b == 0 else mt[:, b % 2, :]
                        dve.wait_ge(filled[bank(js[b])], filling(l, js[b]))
                        V.tensor_tensor(out, psum[:, bank(js[b]), :][:, 0:TOK], g, ALU.mult).then_inc(drained[bank(js[b])], 1)
                        dve.drain()
                        if b:
                            V.tensor_tensor(merged[:, d, :], merged[:, d, :], out, ALU.add)
                    dve.drain().then_inc(merged_ready, 1)
                elif name == "out":
                    dve.wait_ge(g1_ready, nth(l, g1_ready, 4))
                    dve.wait_ge(lnr_ready, nth(l, lnr_ready, 16))
                    dve.wait_ge(x_loaded, nth(l, x_loaded, 16))
                    update(js, g1bc, 0)
                    for j in range(3):
                        low_part(0, 0, j)
                elif name == "rl":
                    dve.wait_ge(scores_ready, nth(l, scores_ready, 1))
                    G = NT * N_GROUPS
                    b3 = rows[:, 0:48]
                    bg = b3.rearrange("p (g e) -> p g e", e=EPG)
                    sc = scores.rearrange("p g e -> p (g e)")
                    V.tensor_tensor(b3.rearrange("p (t e) -> p t e", t=NT), sc.rearrange("p (t e) -> p t e", t=NT),
                                    rb[:].rearrange("p (a e) -> p a e", a=1).to_broadcast([P, NT, N_EXPERTS]), ALU.add)
                    dve.drain()

                    def ranks(v, n, rank, big, ties):
                        shape = [P, n, EPG, EPG]
                        mine = v.rearrange("p g (e a) -> p g e a", a=1).to_broadcast(shape)
                        other = v.rearrange("p g (a e) -> p g a e", a=1).to_broadcast(shape)
                        B = big.rearrange("p (g e a) -> p g e a", e=EPG, a=EPG)
                        T = ties.rearrange("p (g e a) -> p g e a", e=EPG, a=EPG)
                        V.tensor_tensor(B, other, mine, ALU.is_gt)
                        V.tensor_tensor(T, other, mine, ALU.is_equal)
                        dve.drain()
                        V.tensor_tensor(T, T, const("tie").rearrange("p (g e a) -> p g e a", g=1, e=EPG)
                                        .to_broadcast(shape), ALU.mult)
                        dve.drain()
                        V.tensor_tensor(B, B, T, ALU.add)
                        dve.drain()
                        V.tensor_reduce(rank, B, AX.X, ALU.add)
                        dve.drain()

                    rank, sel = rows[:, 48:96].rearrange("p (g e) -> p g e", e=EPG), rows[:, 96:144]
                    selg = sel.rearrange("p (g e) -> p g e", e=EPG)
                    ranks(bg, G, rank, rows[:, 256:448], rows[:, 448:640])
                    V.tensor_scalar(selg, rank, 2.0, None, ALU.is_lt)
                    dve.drain()
                    low_part(0, 0, 3)
                    V.tensor_tensor(rank, selg, bg, ALU.mult)
                    dve.drain()
                    gsum, grank = rows[:, 144:156], rows[:, 156:168]
                    V.tensor_reduce(gsum, rank, AX.X, ALU.add)
                    dve.drain()
                    ranks(gsum.rearrange("p (t g) -> p t g", t=NT), NT, grank.rearrange("p (t g) -> p t g", t=NT),
                          rows[:, 256:304], rows[:, 448:496])
                    V.tensor_scalar(grank, grank, 0.0, None, ALU.is_equal)
                    dve.drain()
                    V.tensor_tensor(selg, selg, grank.rearrange("p (g a) -> p g a", a=1).to_broadcast([P, G, EPG]),
                                    ALU.mult)
                    dve.drain()
                    V.tensor_tensor(sel, sel, sc, ALU.mult)
                    dve.drain()
                    wsum = rows[:, 168:171]
                    V.tensor_reduce(wsum, sel.rearrange("p (t e) -> p t e", t=NT), AX.X, ALU.add)
                    dve.drain()
                    V.reciprocal(wsum, wsum)
                    V.tensor_scalar(sel, sel, ROUTE_SCALE, None, ALU.mult)
                    dve.drain()
                    V.tensor_tensor(comb, sel.rearrange("p (t e) -> p t e", t=NT),
                                    wsum.rearrange("p (t a) -> p t a", a=1).to_broadcast([P, NT, N_EXPERTS]), ALU.mult)
                    dve.drain().then_inc(comb_ready, 1)
                elif name == "cbT":
                    dve.wait_ge(filled[bank("cbT")], filling(l, "cbT"))
                    V.tensor_copy(combT[0:N_EXPERTS, :], psum[:, bank("cbT"), :][0:N_EXPERTS, 0:TOK]).then_inc(drained[bank("cbT")], 1)
                    dve.drain().then_inc(combT_ready, 1)
            hidden(0, 0, 0)
            low_part(0, 0, 4)
            low_part(0, 0, 5)
            hidden(0, 0, 1)
            second_expert(0)
            with dve.Fori(1, N_EXPERTS // 2) as it:
                for j in range(4):
                    low_part(it, 0, j)
                hidden(it, 0, 0)
                low_part(it, 0, 4)
                low_part(it, 0, 5)
                hidden(it, 0, 1)
                second_expert(it)
            dve.wait_ge(g2_ready, nth(l, g2_ready, 4))
            update(SUM_JOBS, g2bc, 2)
            dve.drain().then_inc(x2_ready, 1)
            dve.sem_inc(layer_free, 1)
            layer.close()


def kernel(**inputs):
    import concourse.bacc as bacc
    from concourse.bass_utils import run_bass_kernel_spmd

    a = {k: np.asarray(v) for k, v in inputs.items()}

    def k_tiles(w):
        n = w.shape[2] // P
        return np.ascontiguousarray(w.reshape(w.shape[0], DT, P, n, P).transpose(0, 3, 2, 1, 4)).reshape(
            w.shape[0], n, P, DT * P)

    def k_halves(w):
        n = w.shape[2] // 256
        return w.reshape(w.shape[0], 2, DT // 2, P, n, 256).transpose(0, 4, 1, 3, 2, 5).reshape(
            w.shape[0], 2 * n, P, DT * P)

    w_in = a["w_in"]
    at = np.cumsum([0, 768, 256, 128, 128, 256, 256, 512, 512, 256, 128, 32, 4096])
    hy, wq, wk, wv, rq, rk, rv, rg, cq, ck, kr, g = (w_in[:, :, at[i]:at[i + 1]] for i in range(12))
    wq = wq.reshape(DEPTH, D, 4, 64)[:, :, [0, 2, 1, 3]].reshape(DEPTH, D, 256)
    kr = np.concatenate([np.zeros((DEPTH, D, NOPE), np.float32), kr, np.zeros((DEPTH, D, P - QK), np.float32)], 2)
    g = g.reshape(DEPTH, D, 4, DT, P).transpose(0, 1, 3, 2, 4).reshape(DEPTH, D, 4 * D)
    arrays = {
        "units_ada": k_tiles(a["w_ada"]),
        "units_in": np.concatenate([k_tiles(np.concatenate([hy, rk, rq], 2)), k_halves(rv), k_halves(rg),
                                    k_tiles(np.concatenate([wq, wk], 2)), k_halves(cq),
                                    k_halves(np.concatenate([wv, ck], 2)), k_tiles(np.concatenate([kr, g], 2))], 1),
        "units_out": np.ascontiguousarray(a["w_out"].reshape(DEPTH, DT, P, D)),
        "hy_w3": np.ascontiguousarray(a["hy_w3"]),
        "router_w": np.concatenate([a["router_w"].reshape(DT, P, N_EXPERTS).transpose(1, 0, 2),
                                    np.zeros((P, DT, GROUP - N_EXPERTS), np.float32)], 2),
        "router_b": np.ascontiguousarray(np.broadcast_to(a["router_b"], (P, N_EXPERTS))),
    }
    br = np.concatenate([a["w_br_a"], a["w_br_b"], a["w_br_c"], a["w_br_d"]], 1)
    arrays["units_br"] = np.ascontiguousarray(
        br.reshape(DEPTH, 2, 5, P, DT, P).transpose(0, 4, 1, 3, 2, 5)).reshape(DEPTH, 2 * DT, P, 5 * P)
    up = [a[n].reshape(DEPTH, N_EXPERTS, DT, P, 2, P).transpose(0, 1, 4, 3, 2, 5).reshape(DEPTH, N_EXPERTS, 2, P, D)
          for n in ("moe_w_gate", "moe_w_up")]
    gu = np.stack(up, 3).reshape(DEPTH, N_EXPERTS, 4, P, D)
    down = a["moe_w_down"].reshape(DEPTH, N_EXPERTS, 2, P, D)
    arrays["units_moe"] = np.ascontiguousarray(np.concatenate([gu, down], 2))
    arrays["ln_rows"] = np.ascontiguousarray(np.broadcast_to(
        np.stack([a["ln1_g"], a["ln1_b"], a["ln2_g"], a["ln2_b"]], 1)[:, None], (DEPTH, P, 4, D)))
    arrays["x_in"] = np.ascontiguousarray(np.concatenate([a["x_prompt"][0], a["x_sample"][0]], 0)
                                          .reshape(NT, P, D).transpose(1, 0, 2))
    arrays["cond"] = np.zeros((P, DT, GROUP), np.float32)
    arrays["cond"][:, :, 0] = a["c_ctx"].reshape(DT, P).T
    arrays["cond"][:, :, 1] = a["c"][0].reshape(DT, P).T

    def rows(x, n=P, at=0):
        out = np.zeros((DEPTH, P, int(np.prod(x.shape[2:]))), np.float32)
        out[:, at:at + x.shape[1]] = x.reshape(x.shape[0], x.shape[1], -1)
        return out

    def wide(x):
        return np.broadcast_to(x[:, None], (DEPTH, P) + x.shape[1:])

    def pairs(x):
        return np.stack([np.repeat(x[:, [2 * j, 2 * j + 1]], 64, 1) for j in range(2)], 2)

    def state(x):
        return x[0].reshape(DEPTH, 2, 2, 64, DV).transpose(0, 2, 3, 1, 4).reshape(DEPTH, P, 2, DV)

    df, db = a["ret_decay_fwd"], a["ret_decay_bwd"]
    p = {
        "conv_w": a["hy_conv_w"].reshape(DEPTH, 3, 6, P).transpose(0, 3, 2, 1),
        "conv_b": a["hy_conv_b"].reshape(DEPTH, 6, P).transpose(0, 2, 1),
        "hy_bias": a["hy_bias"].reshape(DEPTH, 4, P).transpose(0, 2, 1),
        "hy_b1": a["hy_b1"][:, :, None], "hy_b2": a["hy_b2"][:, :, None],
        "hy_w1": a["hy_w1"], "hy_w2": a["hy_w2"],
        "decay": np.concatenate([wide(df), wide(db), pairs(df), pairs(db)], 2),
        "q_norm": a["mla_q_norm"].reshape(DEPTH, 2, P).transpose(0, 2, 1),
        "b_ada": a["b_ada"].reshape(DEPTH, 48, P).transpose(0, 2, 1),
        "sink": wide(a["win_sink"]), "kv_norm": wide(a["mla_kv_norm"]),
        "s0f": state(a["state_ret_fwd"]), "s0b": state(a["state_ret_bwd"]),
        "ctx_k": a["cache_win_k"][0].reshape(DEPTH, LP, P).transpose(0, 2, 1),
        "ctx_v": a["cache_win_v"][0].reshape(DEPTH, LP, P),
        "ctx_ckv": a["cache_mla_ckv"][0].transpose(0, 2, 1),
        "w_uq": a["mla_w_uq"].reshape(DEPTH, 2, P, HEADS * QK).transpose(0, 2, 1, 3),
        "w_ukv": a["mla_w_ukv"],
    }
    p["ctx_kr"] = None
    blocks = []
    for name, w in PARTS:
        if name == "ctx_kr":
            b = rows(a["cache_mla_krope"][0].transpose(0, 2, 1), at=NOPE)
        else:
            b = rows(np.asarray(p[name]))
        assert b.shape[2] == w, name
        blocks.append(b)
    arrays["params"] = np.ascontiguousarray(np.concatenate(blocks, 2))
    arrays["consts"], arrays["dist"], arrays["hy_decay"] = shape_constants()

    nc = bacc.Bacc("TRN2", target_bir_lowering=False, num_devices=1)
    args = {n: nc.dram_tensor(n, v.shape, mybir.dt.from_np(v.dtype), kind="ExternalInput").ap()
            for n, v in arrays.items()}
    outs = {"y_prompt": (P, D), "y_sample": (P, 2, D), "new_k": (DEPTH, P, P), "new_v": (DEPTH, P, P),
            "new_ckv": (DEPTH, P, P), "new_krope": (DEPTH, P, ROPE), "new_rf": (DEPTH, HEADS, 64, DV),
            "new_rb": (DEPTH, HEADS, 64, DV)}
    for n, shape in outs.items():
        args[n] = nc.dram_tensor(n, shape, F32, kind="ExternalOutput").ap()
    build(nc, **args)
    r = run_bass_kernel_spmd(nc, [arrays], core_ids=[0]).results[0]
    return (r["y_prompt"].reshape(1, LP, D), r["y_sample"].transpose(1, 0, 2).reshape(1, LS, D),
            r["new_k"].reshape(1, DEPTH, LP, 2, 64), r["new_v"].reshape(1, DEPTH, LP, 2, 64),
            r["new_ckv"].reshape(1, DEPTH, LP, P), r["new_krope"].reshape(1, DEPTH, LP, ROPE),
            r["new_rf"].reshape(1, DEPTH, HEADS, 64, DV), r["new_rb"].reshape(1, DEPTH, HEADS, 64, DV))
```
